# Optimizing a Trainium2 kernel written in Bass

```python
import math
import jax, jax.numpy as jnp
from jax import lax
import numpy as np

D_MODEL = 1024
BATCH = 1
SEQ = 256
DEPTH = 2
DEC_BATCH = 8
DEC_SEQ = 1
PAST_LEN = 1024
PAGE_SIZE = 128

N_A_LAYERS = DEPTH // 2
N_B_LAYERS = DEPTH - N_A_LAYERS
CHUNK = 128
D_A = D_MODEL
A_GROUPS = 8
A_GROUP_DIM = D_A // A_GROUPS
N_HEADS = 8
HEAD_DIM = D_MODEL // (2 * N_HEADS)
V_DIM = 2 * HEAD_DIM
ROT_DIM = HEAD_DIM // 4
ROPE_THETA = 500000.0
Q_BLOCK = 128
N_EXPERTS = 16
N_EXPERT_GROUPS = 4
EXPERTS_PER_GROUP = N_EXPERTS // N_EXPERT_GROUPS
TOP_K = 2
D_EXPERT = 512
DEEPNORM_ALPHA = (2 * DEPTH) ** 0.25
DEEPNORM_BETA = (8 * DEPTH) ** -0.25
LN_EPS = 1e-5

kernel_name = 'yoco_gmlp_diffattn_moe_step'

def layer_norm(x, g, b):
    xf = x.astype(jnp.float32)
    mu = xf.mean(-1, keepdims=True)
    var = jnp.square(xf - mu).mean(-1, keepdims=True)
    return ((xf - mu) * lax.rsqrt(var + LN_EPS) * g.astype(jnp.float32) + b.astype(jnp.float32)).astype(x.dtype)

def rms_norm(x, g):
    xf = x.astype(jnp.float32)
    ms = jnp.square(xf).mean(-1, keepdims=True)
    return (xf * lax.rsqrt(ms + LN_EPS) * g.astype(jnp.float32)).astype(x.dtype)

def rope(x, pos):
    inv = 1.0 / (ROPE_THETA ** (jnp.arange(0, ROT_DIM, 2, dtype=jnp.float32) / ROT_DIM))
    ang = pos.astype(jnp.float32)[:, None] * inv[None, :]
    cos = jnp.cos(ang)[None, :, None, None, :]
    sin = jnp.sin(ang)[None, :, None, None, :]
    xf = x.astype(jnp.float32)
    half = ROT_DIM // 2
    x1 = xf[..., :half]
    x2 = xf[..., half:ROT_DIM]
    out = jnp.concatenate([x1 * cos - x2 * sin, x2 * cos + x1 * sin, xf[..., ROT_DIM:]], axis=-1)
    return out.astype(x.dtype)

def ada_mod(c, w, b):
    m = jnp.einsum('bd,de->be', jax.nn.silu(c), w) + b
    return jnp.split(m[:, None, :], 6, axis=-1)

def chunk_gmlp(h, w_in, ln_g, ln_b, w_s, b_s, w_out):
    Bsz, T, _ = h.shape
    z = jax.nn.gelu(jnp.einsum('btd,de->bte', h, w_in))
    u, v = jnp.split(z, 2, axis=-1)
    v = layer_norm(v, ln_g, ln_b)
    L = min(T, CHUNK)
    mask = jnp.tril(jnp.ones((L, L), dtype=bool))
    ws = jnp.where(mask[None], w_s[:, :L, :L], 0).astype(v.dtype)
    vg = v.reshape(Bsz, T // L, L, A_GROUPS, A_GROUP_DIM)
    s = jnp.einsum('gij,bnjgc->bnigc', ws, vg) + b_s[:, :L].T[None, None, :, :, None]
    out = u * s.reshape(Bsz, T, D_A)
    return jnp.einsum('bte,ed->btd', out, w_out), v

def diff_lambda(lq1, lk1, lq2, lk2, lam_init):
    f32 = lambda a: a.astype(jnp.float32)
    return jnp.exp(jnp.sum(f32(lq1) * f32(lk1))) - jnp.exp(jnp.sum(f32(lq2) * f32(lk2))) + lam_init

def diff_combine(scores, lam):
    p = jax.nn.softmax(scores, axis=-1)
    return p[:, :, 0] - lam * p[:, :, 1]

def diff_attn_prompt(q, k, v, lam):
    Bsz, S = q.shape[:2]
    nb = S // Q_BLOCK
    qb = q.reshape(Bsz, nb, Q_BLOCK, N_HEADS, 2, HEAD_DIM).swapaxes(0, 1)
    k_pos = jnp.arange(S)
    scale = HEAD_DIM ** -0.5

    def block(args):
        q_i, i = args
        q_pos = i * Q_BLOCK + jnp.arange(Q_BLOCK)
        s = jnp.einsum('bqhcd,bshcd->bhcqs', q_i, k, preferred_element_type=jnp.float32) * scale
        s = jnp.where(q_pos[:, None] >= k_pos[None, :], s, -jnp.inf)
        w = diff_combine(s, lam).astype(v.dtype)
        return jnp.einsum('bhqs,bshe->bqhe', w, v)

    o = lax.map(block, (qb, jnp.arange(nb)))
    return o.swapaxes(0, 1).reshape(Bsz, S, N_HEADS, V_DIM)

def diff_attn_sample(q, k_new, v_new, k_past, v_past, lam):
    T = q.shape[1]
    P = k_past.shape[1]
    scale = HEAD_DIM ** -0.5
    s_past = jnp.einsum('bqhcd,bshcd->bhcqs', q, k_past, preferred_element_type=jnp.float32) * scale
    s_new = jnp.einsum('bqhcd,bshcd->bhcqs', q, k_new, preferred_element_type=jnp.float32) * scale
    s_new = jnp.where(jnp.tril(jnp.ones((T, T), dtype=bool)), s_new, -jnp.inf)
    w = diff_combine(jnp.concatenate([s_past, s_new], axis=-1), lam).astype(v_new.dtype)
    return (jnp.einsum('bhqs,bshe->bqhe', w[..., :P], v_past)
            + jnp.einsum('bhqs,bshe->bqhe', w[..., P:], v_new))

def diff_out(o, subln_g, lam_init, w_o):
    o = rms_norm(o, subln_g) * (1.0 - lam_init)
    Bsz, T = o.shape[:2]
    return jnp.einsum('bte,ed->btd', o.reshape(Bsz, T, N_HEADS * V_DIM), w_o)

def moe(h, router_w, router_bias, w_gate, w_up, w_down):
    Bsz, T, D = h.shape
    t = h.reshape(Bsz * T, D)
    logits = jnp.einsum('td,de->te', t, router_w, preferred_element_type=jnp.float32)
    scores = jax.nn.softmax(logits, axis=-1)
    sel = scores + router_bias.astype(jnp.float32)
    group_score = lax.top_k(sel.reshape(-1, N_EXPERT_GROUPS, EXPERTS_PER_GROUP), TOP_K)[0].sum(-1)
    best_group = jnp.argmax(group_score, axis=-1)
    in_group = (jnp.arange(N_EXPERTS) // EXPERTS_PER_GROUP)[None, :] == best_group[:, None]
    _, idx = lax.top_k(jnp.where(in_group, sel, -jnp.inf), TOP_K)
    wk = jnp.take_along_axis(scores, idx, axis=-1)
    wk = wk / wk.sum(-1, keepdims=True)
    gate = jnp.sum(jax.nn.one_hot(idx, N_EXPERTS, dtype=jnp.float32) * wk[..., None], axis=1)
    a = jax.nn.silu(jnp.einsum('td,edf->tef', t, w_gate)) * jnp.einsum('td,edf->tef', t, w_up)
    a = a * gate.astype(a.dtype)[..., None]
    return jnp.einsum('tef,efd->td', a, w_down).reshape(Bsz, T, D)

def run_trunk(x, c, pos, attend, p):
    Bsz, T, _ = x.shape
    v_rows = []
    k_sh = None
    v_sh = None
    for l in range(DEPTH):
        sh1, sc1, g1, sh2, sc2, g2 = ada_mod(c, p['ada_w'][l], p['ada_b'][l])
        h = x * (1 + sc1) + sh1
        if l < N_A_LAYERS:
            out, v_a = chunk_gmlp(h, p['a_w_in'][l], p['a_ln_g'][l], p['a_ln_b'][l],
                                  p['a_w_s'][l], p['a_b_s'][l], p['a_w_out'][l])
            v_rows.append(v_a)
        else:
            j = l - N_A_LAYERS
            q = jnp.einsum('btd,de->bte', h, p['b_w_q'][j]).reshape(Bsz, T, N_HEADS, 2, HEAD_DIM)
            q = rope(q, pos)
            lam_init = 0.8 - 0.6 * math.exp(-0.3 * l)
            lam = diff_lambda(p['b_lam_q1'][j], p['b_lam_k1'][j], p['b_lam_q2'][j], p['b_lam_k2'][j], lam_init)
            o = attend(q, k_sh, v_sh, lam)
            out = diff_out(o, p['b_subln_g'][j], lam_init, p['b_w_o'][j])
        x = layer_norm(DEEPNORM_ALPHA * x + (1 + g1) * out, p['ln_g'][l, 0], p['ln_b'][l, 0])
        h = x * (1 + sc2) + sh2
        f = moe(h, p['router_w'], p['router_bias'], p['moe_w_gate'][l], p['moe_w_up'][l], p['moe_w_down'][l])
        x = layer_norm(DEEPNORM_ALPHA * x + (1 + g2) * f, p['ln_g'][l, 1], p['ln_b'][l, 1])
        if l == N_A_LAYERS - 1:
            k_sh = rope(jnp.einsum('btd,de->bte', x, p['kv_w_k']).reshape(Bsz, T, N_HEADS, 2, HEAD_DIM), pos)
            v_sh = jnp.einsum('btd,de->bte', x, p['kv_w_v']).reshape(Bsz, T, N_HEADS, V_DIM)
    return x, k_sh, v_sh, v_rows

def setup_inputs(seed: int = 0) -> dict:
    key = jax.random.key(seed)
    keys = iter(jax.random.split(key, 64))

    def nrm(shape, scale):
        return jax.random.normal(next(keys), shape, jnp.float32) * scale

    n_pages = PAST_LEN // PAGE_SIZE
    n_used = DEC_BATCH * n_pages
    n_pool = n_used + max(1, n_used // 4)
    perm = jax.random.permutation(next(keys), n_pool)
    page_table = perm[:n_used].reshape(DEC_BATCH, n_pages).astype(jnp.int32)
    qk_w = N_HEADS * 2 * HEAD_DIM
    v_w = N_HEADS * V_DIM
    D = D_MODEL
    return {
        'x_prompt': nrm((BATCH, SEQ, D), 1.0),
        'x_sample': nrm((DEC_BATCH, DEC_SEQ, D), 1.0),
        'cache_k': nrm((n_pool, PAGE_SIZE, N_HEADS, 2, HEAD_DIM), 1.0),
        'cache_v': nrm((n_pool, PAGE_SIZE, N_HEADS, V_DIM), DEEPNORM_BETA),
        'page_table': page_table,
        'c_prompt': nrm((BATCH, D), 1.0),
        'c_sample': nrm((DEC_BATCH, D), 1.0),
        'ada_w': nrm((DEPTH, D, 6 * D), 0.5 * D ** -0.5),
        'ada_b': nrm((DEPTH, 6 * D), 0.01),
        'ln_g': 1.0 + nrm((DEPTH, 2, D), 0.02),
        'ln_b': nrm((DEPTH, 2, D), 0.01),
        'a_w_in': nrm((N_A_LAYERS, D, 2 * D_A), D ** -0.5),
        'a_ln_g': 1.0 + nrm((N_A_LAYERS, D_A), 0.02),
        'a_ln_b': nrm((N_A_LAYERS, D_A), 0.01),
        'a_w_s': nrm((N_A_LAYERS, A_GROUPS, CHUNK, CHUNK), CHUNK ** -0.5),
        'a_b_s': 1.0 + nrm((N_A_LAYERS, A_GROUPS, CHUNK), 0.01),
        'a_w_out': nrm((N_A_LAYERS, D_A, D), D_A ** -0.5 * DEEPNORM_BETA),
        'kv_w_k': nrm((D, qk_w), D ** -0.5),
        'kv_w_v': nrm((D, v_w), D ** -0.5 * DEEPNORM_BETA),
        'b_w_q': nrm((N_B_LAYERS, D, qk_w), D ** -0.5),
        'b_lam_q1': nrm((N_B_LAYERS, HEAD_DIM), 0.1),
        'b_lam_k1': nrm((N_B_LAYERS, HEAD_DIM), 0.1),
        'b_lam_q2': nrm((N_B_LAYERS, HEAD_DIM), 0.1),
        'b_lam_k2': nrm((N_B_LAYERS, HEAD_DIM), 0.1),
        'b_subln_g': 1.0 + nrm((N_B_LAYERS, V_DIM), 0.02),
        'b_w_o': nrm((N_B_LAYERS, v_w, D), v_w ** -0.5 * DEEPNORM_BETA),
        'router_w': nrm((D, N_EXPERTS), D ** -0.5),
        'router_bias': nrm((N_EXPERTS,), 0.01),
        'moe_w_gate': nrm((DEPTH, N_EXPERTS, D, D_EXPERT), D ** -0.5),
        'moe_w_up': nrm((DEPTH, N_EXPERTS, D, D_EXPERT), D ** -0.5),
        'moe_w_down': nrm((DEPTH, N_EXPERTS, D_EXPERT, D), D_EXPERT ** -0.5 * DEEPNORM_BETA),
    }

def reference(x_prompt, x_sample, cache_k, cache_v, page_table, c_prompt, c_sample,
              ada_w, ada_b, ln_g, ln_b, a_w_in, a_ln_g, a_ln_b, a_w_s, a_b_s, a_w_out,
              kv_w_k, kv_w_v, b_w_q, b_lam_q1, b_lam_k1, b_lam_q2, b_lam_k2, b_subln_g, b_w_o,
              router_w, router_bias, moe_w_gate, moe_w_up, moe_w_down):
    p = dict(ada_w=ada_w, ada_b=ada_b, ln_g=ln_g, ln_b=ln_b, a_w_in=a_w_in, a_ln_g=a_ln_g,
             a_ln_b=a_ln_b, a_w_s=a_w_s, a_b_s=a_b_s, a_w_out=a_w_out, kv_w_k=kv_w_k, kv_w_v=kv_w_v,
             b_w_q=b_w_q, b_lam_q1=b_lam_q1, b_lam_k1=b_lam_k1, b_lam_q2=b_lam_q2, b_lam_k2=b_lam_k2,
             b_subln_g=b_subln_g, b_w_o=b_w_o, router_w=router_w, router_bias=router_bias,
             moe_w_gate=moe_w_gate, moe_w_up=moe_w_up, moe_w_down=moe_w_down)

    pos_prompt = jnp.arange(x_prompt.shape[1], dtype=jnp.int32)
    y_prompt, k_prompt, v_prompt, _ = run_trunk(x_prompt, c_prompt, pos_prompt, diff_attn_prompt, p)

    n_seq, n_pages = page_table.shape
    past = n_pages * PAGE_SIZE
    k_past = cache_k[page_table].reshape(n_seq, past, N_HEADS, 2, HEAD_DIM)
    v_past = cache_v[page_table].reshape(n_seq, past, N_HEADS, V_DIM)
    pos_sample = past + jnp.arange(x_sample.shape[1], dtype=jnp.int32)

    def attend_sample(q, k_new, v_new, lam):
        return diff_attn_sample(q, k_new, v_new, k_past, v_past, lam)

    y_sample, k_sample, v_sample, v_rows_sample = run_trunk(x_sample, c_sample, pos_sample, attend_sample, p)
    chunk_v_sample = jnp.stack(v_rows_sample, axis=0)
    return (y_prompt, y_sample, k_prompt, v_prompt, k_sample, v_sample, chunk_v_sample)


_drawn_inputs = setup_inputs


def setup_inputs(seed=0):
    import zlib

    import numpy as np

    out = dict(_drawn_inputs(seed))
    spreads = {}
    factors = {'a_ln_g': 2.917, 'b_lam_q1': 4.675, 'b_lam_k1': 2.762, 'b_lam_k2': 8.0, 'b_subln_g': 4.778}
    for name, (base, spread) in spreads.items():
        noise = np.random.default_rng([zlib.crc32(name.encode()), seed]).standard_normal(out[name].shape)
        drawn = base * np.exp(spread * noise) if base else spread * noise
        out[name] = __import__('jax').numpy.asarray(drawn.astype(out[name].dtype))
    for name, factor in factors.items():
        out[name] = (out[name] * factor).astype(out[name].dtype)
    return out
```

```python
import math
from contextlib import ExitStack, contextmanager

import numpy as np

import concourse.bass as bass
from concourse import mybir

F32 = mybir.dt.float32
I32 = mybir.dt.int32
ALU = mybir.AluOpType
ACT = mybir.ActivationFunctionType
AX = mybir.AxisListType

P = 128
D = 1024
C = D // P
TP = 256
NB = 8
T = TP + NB
DEPTH = 2
NE = 16
EG = 4
FE = 512
FB = FE // P
H = 8
HD = 64
PAST = 1024
PAGE = 128
NPG = PAST // PAGE
POOLN = 80
ROT = HD // 4
ALPHA = (2 * DEPTH) ** 0.25
EPS = 1e-5
LAM_INIT = 0.8 - 0.6 * math.exp(-0.3 * 1)
NEG = -1e30
SLOTS = 6
TILE = 4096
NBANK = 4
NR = 1 + NB

K_ID, K_ROT, K_ONE, K_MEAN, K_MASK, K_COS, K_SIN = 0, 128, 256, 384, 512, 768, 768 + T
K_N = 768 + 2 * T
V_LNG, V_LNB, V_AG, V_AB, V_SUB, V_N = 0, 32, 64, 72, 80, 81


def constants():
    k = np.zeros((P, K_N), np.float32)
    k[:, K_ID:K_ID + P] = np.eye(P)
    half = ROT // 2
    for c in range(2):
        for i in range(half):
            a, b = c * HD + i, c * HD + half + i
            k[b, K_ROT + a] = -1.0
            k[a, K_ROT + b] = 1.0
    k[:, K_ONE:K_ONE + P] = 1.0
    k[:, K_MEAN:K_MEAN + P] = 1.0 / D
    k[:, K_MASK + P:K_MASK + 2 * P] = np.where(
        np.arange(P)[:, None] >= np.arange(P)[None, :], 0.0, NEG)
    inv = 1.0 / (np.float32(500000.0) ** (np.arange(0, ROT, 2, dtype=np.float32) / ROT))
    pos = np.concatenate([np.arange(TP), np.full(NB, PAST)]).astype(np.float32)
    ang = (pos[None, :] * inv.astype(np.float32)[:, None]).astype(np.float32)
    k[:, K_COS:K_COS + T] = 1.0
    for c in range(2):
        for r in range(2):
            a = c * HD + r * half
            k[a:a + half, K_COS:K_COS + T] = np.cos(ang)
            k[a:a + half, K_SIN:K_SIN + T] = np.sin(ang)
    return k


class Tally:

    def __init__(self, sem):
        self.sem, self.n, self.turn = sem, 0, None

    def add(self, k=1):
        self.n += k
        return self.value()

    def value(self, back=0):
        v = self.n - back
        return v if self.turn is None else self.turn + v


@contextmanager
def turns(eng, count, per):
    before = {t: t.n for t in per}
    with eng.Fori(0, count) as i:
        for t, k in per.items():
            t.turn = i * k
        yield i
    for t, k in per.items():
        assert t.n - before[t] == k, (t.sem, t.n - before[t], k)
        t.turn = None
        t.n = before[t] + k * count


def build(nc, a, o):
    with ExitStack() as ctx:
        def sb(name, shape, dt=F32):
            return ctx.enter_context(nc.sbuf_tensor(name, shape, dt))

        def sem(name):
            return ctx.enter_context(nc.semaphore(name))

        wring = sb("wring", [P, SLOTS, TILE])
        kst = sb("kst", [P, K_N])
        xT = sb("xT", [P, C, T])
        hT = sb("hT", [P, C, T])
        yT = sb("yT", [P, C, T])
        sqT = sb("sqT", [P, C, T])
        abT = sb("abT", [P, 2 * C, T])
        cqT = sb("cqT", [P, C, T])
        tokA = sb("tokA", [P, 3, D])
        tokB = sb("tokB", [P, 2, D])
        ws = sb("ws", [P, 8, P])
        wsT = sb("wsT", [P, 8, P])
        bsb = sb("bsb", [P, 8, P])
        ws00 = sb("ws00", [P, 8])
        rw = sb("rw", [P, C, NE])
        rbias = sb("rbias", [P, NE])
        vT = sb("vecT", [P, V_N])
        adabT = sb("adabT", [P, 96])
        crows = sb("crows", [P, D])
        cT = sb("cT", [P, C, NR])
        mrows = sb("mrows", [P, D])
        mT = sb("mT", [P, 48, NR])
        rs = sb("rs", [P, T])
        epsc = sb("epsc", [P, 1])
        lgT = sb("lgT", [NE, T])
        lg = sb("lg", [P, 3, NE])
        score = sb("score", [P, 3, NE])
        sel = sb("sel", [P, 3, NE])
        top = [sb(f"top{i}", [P, 3, NE]) for i in range(2)]
        key = sb("key", [P, 3, NE])
        pair = [sb(f"pair{i}", [P, 3, EG]) for i in range(4)]
        one = sb("one", [P, 3, 1])
        kidx = sb("kidx", [P, NE])
        kint = sb("kint", [P, NE], I32)
        ptab = sb("ptab", [1, NB * NPG], I32)
        lamx = sb("lamx", [P, 4, HD])
        lams = sb("lams", [1, 5])
        nlam = sb("nlam", [P, 1])
        subg = sb("subg", [P, 1])
        pst = sb("pst", [P, 2, 6])
        snew = sb("snew", [P, NB, 16])
        scol = sb("scol", [P, 1])

        vrow = tokA[0:V_N, 0, 0:P]
        arow = tokA[0:96, 0, P:2 * P]
        crow = crows[0:NR, :]
        mrow = mrows[0:NR, :].rearrange("p (b n) -> p b n", b=2)
        psc = mrows[:, :].rearrange("p (j c s) -> p j c s", j=2, c=2)
        pex = crows[:, :].rearrange("p (j c s) -> p j c s", j=2, c=2)
        sW = wsT[:, 0:4, :].rearrange("p a (x g h) -> p (a x) g h", g=NPG, h=H)
        pwT = wsT[:, 4:8, :].rearrange("p (j t) q -> p j t q", j=2)
        lamv = lamx[0:1, :, :]
        smx = lamx[:, 2:4, :].rearrange("p a d -> p (a d)")
        wnew = lamx[:, 2, :].rearrange("p (b h) -> p b h", b=NB)
        srow = lamv[0:1, 0:2, :].rearrange("o a d -> o (a d)")
        uT = abT[:, 0:C, :]
        zT = abT[:, C:2 * C, :]
        aT = cqT[:, :, :].rearrange("p (b f) t -> p b f t", b=2)
        upT = tokB[:, :, :].rearrange("p b n -> p (b n)")[:, 0:FB * T].rearrange("p (f t) -> p f t", f=FB)
        ident = kst[:, K_ID:K_ID + P]
        qbc = yT[:, :, :].rearrange("p c t -> p (c t)")[:, 0:2 * D].rearrange("p (b n) -> p b n", b=2)
        prod = sqT[:, :, :].rearrange("p c t -> p (c t)")[:, 0:2 * D]
        sS, sE = tokB[:, 0, :], tokB[:, 1, :]
        ksm = ws[:, :, :].rearrange("p g n -> p (g n)")
        osb = bsb[:, :, :].rearrange("p g n -> p (g n)")
        qtok = wsT[:, :, :].rearrange("p g n -> p (g n)")

        pj = [ctx.enter_context(nc.psum_tensor(f"pj{i}", [P, 512], F32)) for i in range(NBANK)]
        tb = [ctx.enter_context(nc.psum_tensor(f"tb{i}", [P, 512], F32)) for i in range(2)]
        st = [ctx.enter_context(nc.psum_tensor(f"st{i}", [P, T], F32)) for i in range(2)]

        consts_in, rows_in, x_in, small_in, table_in = (
            sem(n) for n in ("consts_in", "rows_in", "x_in", "small_in", "table_in"))
        slot_in = [sem(f"slot{i}_in") for i in range(SLOTS)]
        stored = {n: sem(f"{n}_stored") for n in ("cv", "kp", "ks", "vp", "vs", "yp", "ys")}
        pool_own = sem("pool_own")
        ws_masked = sem("ws_masked")
        c_silu = sem("c_silu")
        pj_done, pj_evac = sem("pj_done"), sem("pj_evac")
        tb_done, tb_evac = sem("tb_done"), sem("tb_evac")
        st_done = sem("st_done")
        dve_own = sem("dve_own")
        op_ready = sem("op_ready")
        act_in = sem("act_in")
        act_out = sem("act_out")
        sq_ready = sem("sq_ready")
        a_ready = sem("a_ready")
        acc_done = sem("acc_done")
        keys_used = sem("keys_used")

        at = {}
        block = ctx.enter_context(nc.Block())

        @block.tensor
        def _(pe):
            g, b, sd = Tally(pj_done), Tally(tb_done), Tally(st_done)
            op, an, sqn = Tally(op_ready), Tally(a_ready), Tally(sq_ready)
            loads = [0] * SLOTS
            banks = [0]

            def loaded(s, k=1, turn=0):
                loads[s] += 16 * k
                pe.wait_ge(slot_in[s], turn + loads[s])

            def operand():
                pe.wait_ge(op_ready, op.add())

            def squares():
                pe.wait_ge(sq_ready, sqn.add())

            def group(rows, n, pairs):
                k = banks[0]
                banks[0] += 1
                if k >= NBANK:
                    pe.wait_ge(pj_evac, g.value(NBANK - 1))
                out = pj[k % NBANK][0:rows, 0:n]
                for j, (lhsT, rhs) in enumerate(pairs):
                    m = pe.matmul(out, lhsT, rhs, start=(j == 0), stop=(j == len(pairs) - 1))
                m.then_inc(pj_done, 1)
                g.add()

            def small(parts):
                if b.n >= 2:
                    pe.wait_ge(tb_evac, b.value(1))
                bank = tb[b.n % 2]
                for (rows, c0, n), fn in parts:
                    m = fn(bank[0:rows, c0:c0 + n])
                m.then_inc(tb_done, 1)
                b.add()

            def emptied():
                pe.wait_ge(tb_evac, b.value())

            def tr(src, rows=P):
                return lambda dst: pe.transpose(dst, src, ident[0:rows, 0:rows])

            def mm(lhsT, rhs, start=True, stop=True):
                return lambda dst: pe.matmul(dst, lhsT, rhs, start=start, stop=stop)

            def project(s, src, turn=0):
                loaded(s, turn=turn)
                w = wring[:, s, :].rearrange("p (k n) -> p k n", n=512)
                for f in range(4):
                    group(P, T, [(w[:, k, f * P:(f + 1) * P], src[:, k, :]) for k in range(C)])

            def stat(src, which):
                for k in range(C):
                    m = pe.matmul(st[which][:, :], kst[:, K_MEAN:K_MEAN + P], src[:, k, :],
                                  start=(k == 0), stop=(k == C - 1))
                m.then_inc(st_done, 1)
                sd.add()

            def norm(src):
                stat(src, 0)
                squares()
                stat(sqT, 1)

            def to_tokens(src):
                for q in range(2):
                    small([((NB, c * P, P), tr(src[:, 4 * q + c, TP:T])) for c in range(4)])
                for j in range(2):
                    for q in range(2):
                        small([((P, c * P, P), tr(src[:, 4 * q + c, j * P:(j + 1) * P])) for c in range(4)])

            row_group = {}

            def ada_tile(l, n, s):
                loaded(s)
                w = wring[:, s, :].rearrange("p (k n) -> p k n", n=512)
                group(NR, 512, [(cT[:, k, :], w[:, k, :]) for k in range(C)])
                row_group[n] = g.n

            def ada_turn(l, n):
                pe.wait_ge(pj_evac, row_group[n])
                small([((P, 16 * c, NR), tr(mrow[:, n % 2, c * P:(c + 1) * P], NR)) for c in range(4)])
                at[f"turn{l}_{n}"] = b.n

            pe.wait_ge(consts_in, 16)
            pe.wait_ge(rows_in, 16 * 8)
            small([((P, 0, V_N), tr(vrow, V_N)), ((P, P, 96), tr(arow, 96))])
            pe.wait_ge(c_silu, 1)
            small([((P, 16 * c, NR), tr(crow[:, c * P:(c + 1) * P], NR)) for c in range(C)])
            pe.wait_ge(x_in, 32)
            for j in range(2):
                for q in range(2):
                    small([((P, c * P, P), tr(tokB[:, j, (4 * q + c) * P:(4 * q + c + 1) * P])) for c in range(4)])
            small([((P, 16 * c, NB), tr(tokA[0:NB, 2, c * P:(c + 1) * P], NB)) for c in range(C)])
            for n in range(12):
                ada_tile(0, n, n % SLOTS)
                if n:
                    ada_turn(0, n - 1)
            ada_turn(0, 11)
            pe.wait_ge(ws_masked, 1)
            for q in range(2):
                small([((P, c * P, P), tr(ws[:, 4 * q + c, :])) for c in range(4)])

            operand()
            for n in range(4):
                project(n, hT)
            at["uv"] = g.n
            pe.wait_ge(pj_evac, g.n)
            norm(zT)
            operand()
            to_tokens(zT)
            at["v_tok"] = b.n
            emptied()
            for q in range(4):
                small([((P, P * (2 * i + j), P), mm(tokA[:, j, (2 * q + i) * P:(2 * q + i + 1) * P], wsT[:, 2 * q + i, :]))
                       for i in range(2) for j in range(2)])
            operand()
            for n in range(2):
                project(4 + n, uT)
            at["a_out"] = g.n
            operand()
            norm(yT)

            def moe(l):
                operand()
                small([((NE, 0, T), mm(rw[:, k, :], hT[:, k, :], k == 0, k == C - 1)) for k in range(C)])
                emptied()
                small([((n, NE * j, NE), tr(lgT[:, j * P:j * P + n], NE)) for j, n in enumerate((P, P, NB))])
                operand()
                small([((NE, P * j, n), tr(lg[0:n, j, :], n)) for j, n in enumerate((P, P, NB))])
                emptied()
                for e in range(NE):
                    small([((P, 0, T), mm(ident[0:NE, e:e + 1].to_broadcast([NE, P]), lgT[:]))])
                at[f"moe{l}"] = g.n

                def step(s3, up, par, turn=0):
                    if up:
                        project(s3, hT, turn)
                        project(s3 + 1, hT, turn)
                    if par is not None:
                        loaded(s3 + 2, turn=turn)
                        pe.wait_ge(a_ready, an.add())
                        w = wring[:, s3 + 2, :].rearrange("p (k n) -> p k n", n=D)
                        for d in range(C):
                            group(P, T, [(w[:, k, d * P:(d + 1) * P], aT[:, par, k, :]) for k in range(FB)])

                step(0, True, None)
                step(3, True, 0)
                step(0, True, 1)
                with turns(pe, 6, {g: 32, an: 2}) as i:
                    step(3, True, 0, i * 16)
                    step(0, True, 1, i * 16)
                for s in range(SLOTS):
                    loads[s] += 16 * 5
                step(3, True, 0)
                step(0, False, 1)
                at[f"moe{l}_end"] = g.n

            moe(0)
            operand()
            norm(yT)

            operand()
            for s in (0, 1, 3, 4):
                project(s, xT)
            at["kv"] = g.n
            for n, s in enumerate((5, 2, 0, 1)):
                ada_tile(1, n, s)
                if n:
                    ada_turn(1, n - 1)
            ada_turn(1, 3)
            operand()
            for s in (3, 4):
                project(s, hT)
            at["q"] = g.n
            for src, ready in ((uT, at["kv"]), (cqT, at["q"])):
                pe.wait_ge(pj_evac, ready)
                for h in range(H):
                    small([((P, 0, T), mm(kst[:, K_ROT:K_ROT + P], src[:, h, :]))])
            operand()
            for q in range(2):
                small([((NB, c * P, P), tr(cqT[:, 4 * q + c, TP:T])) for c in range(4)])
            operand()
            for c in range(2):
                small([((P, 0, 64), mm(kst[HD * c:HD * (c + 1), K_ONE:K_ONE + P], rs[HD * c:HD * (c + 1), 0:64]))])
            operand()
            small([((P, 0, 1), mm(kst[0:1, K_ONE:K_ONE + P], lams[0:1, 4:5]))])
            to_tokens(uT)
            at["k_tok"] = b.n
            to_tokens(zT)
            at["v2_tok"] = b.n

            at["spread"] = g.n
            at["key_loads"] = list(loads)
            for s in range(NB):
                for n in range(2):
                    group(P, 512, [(ident[0:NB, s:s + 1].to_broadcast([NB, P]), qtok[0:NB, n * 512:(n + 1) * 512])])
                ada_tile(1, 4 + s, 4 + s % 2)
                if s:
                    ada_turn(1, 3 + s)
            ada_turn(1, 11)

            operand()
            small([((P, 0, P), tr(smx))])
            emptied()
            small([((1, 0, P), tr(scol[:]))])
            emptied()
            small([((P, 0, P), mm(kst[0:1, K_ONE:K_ONE + P], srow))])
            operand()
            small([((P, 0, P), mm(kst[:, K_ONE:K_ONE + P], smx))])

            for s in range(4):
                loads[s] += 64 * 4
            operand()
            at["values"] = g.n
            for h in range(H):
                seq = h
                for c in range(2):
                    small([((P, P * j, (j + 1) * P), mm(cqT[HD * c:HD * (c + 1), h, j * P:(j + 1) * P],
                                                        uT[HD * c:HD * (c + 1), h, 0:(j + 1) * P])) for j in range(2)])
                par = 2 * (seq % 2)
                for k in range(2):
                    loaded(par + k, 4)

                def values(n):
                    group(H, 512, [(sW[:, seq, p, :], wring[:, par + p // 4, (p % 4) * D + n * 512:(p % 4) * D + (n + 1) * 512])
                                   for p in range(NPG)])

                values(0)
                for j in range(2):
                    operand()
                    small([((P, P * t, P), tr(pex[:, j, 0, t * P:(t + 1) * P])) for t in range(j + 1)])
                values(1)
                for j in range(2):
                    pe.wait_ge(tb_evac, b.value(1))
                    small([((P, 0, P), mm(tokA[:, t, h * P:(h + 1) * P], pwT[:, j, t, :], t == 0, t == j))
                           for t in range(j + 1)])
                pe.wait_ge(pj_evac, g.n)
                small([((P, H * c, H), tr(osb[0:H, c * P:(c + 1) * P], H)) for c in range(C)])
                at[f"rows{h}"] = b.n

            squares()
            for h in range(H):
                small([((P, 0, T), mm(kst[:, K_ONE:K_ONE + P], sqT[:, h, :]))])
            at["rms"] = b.n
            operand()
            for n in range(2):
                project(4 + n, hT)
            at["b_out"] = g.n
            operand()
            norm(yT)
            moe(1)
            operand()
            norm(yT)
            operand()
            to_tokens(xT)
            at["y_tok"] = b.n
            at["end"] = g.n

        @block.sync
        def _(sp):
            free = [None] * SLOTS
            done = [0]

            def slot(s, n=512):
                return wring[:, s, :].rearrange("p (k n) -> p k n", n=n)

            def load(s, src, groups, n=512):
                if free[s]:
                    sp.wait_ge(*free[s])
                sp.dma_start(slot(s, n), src).then_inc(slot_in[s], 16)
                done[0] += groups
                free[s] = (pj_done, done[0])

            def columns(name, n, l=None):
                w = a[name] if l is None else a[name][l]
                return w.rearrange("(k p) n -> p k n", p=P)[:, :, n * 512:(n + 1) * 512]

            sp.dma_start(kst[:], a["consts"]).then_inc(consts_in, 16)
            sp.dma_start(crow[0:1, :], a["c_prompt"]).then_inc(rows_in, 16)
            sp.dma_start(crow[1:NR, :], a["c_sample"]).then_inc(rows_in, 16)
            sp.dma_start(vrow[V_LNG:V_LNG + 32, :], a["ln_g"].rearrange("l j (c p) -> (l j c) p", p=P)).then_inc(rows_in, 16)
            sp.dma_start(vrow[V_LNB:V_LNB + 32, :], a["ln_b"].rearrange("l j (c p) -> (l j c) p", p=P)).then_inc(rows_in, 16)
            sp.dma_start(vrow[V_AG:V_AG + 8, :], a["a_ln_g"].rearrange("l (c p) -> (l c) p", p=P)).then_inc(rows_in, 16)
            sp.dma_start(vrow[V_AB:V_AB + 8, :], a["a_ln_b"].rearrange("l (c p) -> (l c) p", p=P)).then_inc(rows_in, 16)
            sp.dma_start(vrow[V_SUB:V_SUB + 1, :], a["b_subln_g"]).then_inc(rows_in, 16)
            sp.dma_start(arow, a["ada_b"].rearrange("l (c p) -> (l c) p", p=P)).then_inc(rows_in, 16)
            sp.dma_start(tokB[:], a["x_prompt"][0].rearrange("(j p) d -> p j d", p=P)).then_inc(x_in, 16)
            sp.dma_start(tokA[0:NB, 2, :], a["x_sample"].rearrange("b t d -> (b t) d")).then_inc(x_in, 16)
            for n in range(12):
                load(n % SLOTS, columns("ada_w", n, 0), 1)
            for n in range(4):
                load(n, columns("a_w_in", n, 0), 4)
            for n in range(2):
                load(4 + n, columns("a_w_out", n, 0), 4)

            def moe_loads(l):
                gate = a["moe_w_gate"][l].rearrange("e (k p) n -> e p k n", p=P)
                up = a["moe_w_up"][l].rearrange("e (k p) n -> e p k n", p=P)
                down = a["moe_w_down"][l].rearrange("e (k p) n -> e p k n", p=P)

                def step(s, e):
                    if e < NE:
                        load(s, gate[e], 4)
                        load(s + 1, up[e], 4)
                    if e > 0:
                        load(s + 2, down[e - 1], 8, D)

                step(0, 0)
                step(3, 1)
                step(0, 2)
                first = at[f"moe{l}"] + 8
                with sp.Fori(0, 6) as i:
                    for k in range(2):
                        s = 3 - 3 * k
                        e = i * 2 + (3 + k)
                        for slot_, src, n, used in ((s, gate[bass.ds(e, 1)], 512, 4), (s + 1, up[bass.ds(e, 1)], 512, 8),
                                                    (s + 2, down[bass.ds(e - 1, 1)], D, 16)):
                            sp.wait_ge(pj_done, i * 32 + (first + 16 * k + used))
                            sp.dma_start(slot(slot_, n), src.rearrange("a p k n -> p (a k) n")).then_inc(slot_in[slot_], 16)
                last = first + 16 * 13
                done[0] = last + 16
                for k, s in ((-1, 3), (0, 0)):
                    for j, used in enumerate((4, 8, 16)):
                        free[s + j] = (pj_done, last + 16 * k + used)
                step(3, 15)
                step(0, 16)
                assert done[0] == at[f"moe{l}_end"]

            moe_loads(0)
            for s, n in ((0, 0), (1, 1)):
                load(s, columns("kv_w_k", n), 4)
            for s, n in ((3, 0), (4, 1)):
                load(s, columns("kv_w_v", n), 4)
            for n, s in enumerate((5, 2, 0, 1)):
                load(s, columns("ada_w", n, 1), 1)
            for s, n in ((3, 0), (4, 1)):
                load(s, columns("b_w_q", n, 0), 4)
            assert done[0] == at["spread"]

            keys = a["cache_k"].rearrange("g p h c d -> g p (h c d)")
            vals = a["cache_v"].rearrange("g p h e -> g p (h e)")

            def pages(cache, seq, k, s, sem_, value):
                with sp.Fori(0, 4) as i:
                    page = sp.value_load(ptab[0:1, bass.ds(seq * NPG + 4 * k + i, 1)], min_val=0, max_val=POOLN - 1)
                    sp.wait_ge(sem_, value)
                    sp.dma_start(wring[:, s, bass.ds(i * D, D)],
                                 cache[bass.ds(page, 1)].rearrange("a p n -> p (a n)")).then_inc(slot_in[s], 16)

            sp.wait_ge(table_in, 16)
            spread = at["spread"]
            for seq in range(2):
                for k in range(2):
                    pages(keys, seq, k, 2 * seq + k, *free[2 * seq + k])
                sp.wait_ge(*free[4 + seq])
                sp.dma_start(slot(4 + seq), columns("ada_w", 4 + seq, 1)).then_inc(slot_in[4 + seq], 16)
            ada1 = a["ada_w"][1].rearrange("(k p) n -> p k n", p=P)
            with sp.Fori(0, 3) as t:
                for seq in range(2):
                    for k in range(2):
                        pages(keys, t * 2 + (2 + seq), k, 2 * seq + k, keys_used, t * 4 + (2 * seq + k + 1))
                    sp.wait_ge(pj_done, t * 6 + (spread + 3 * (seq + 1)))
                    sp.dma_start(slot(4 + seq), ada1[:, :, bass.ds(t * 1024 + (6 + seq) * 512, 512)]).then_inc(slot_in[4 + seq], 16)
            for seq in range(2):
                for k in range(2):
                    pages(vals, seq, k, 2 * seq + k, keys_used, 12 + 2 * seq + k + 1)
            for n in range(2):
                sp.wait_ge(pj_done, spread + 3 * (7 + n))
                sp.dma_start(slot(4 + n), columns("b_w_o", n, 0)).then_inc(slot_in[4 + n], 16)
            values = at["values"]
            with sp.Fori(0, 3) as t:
                for seq in range(2):
                    for k in range(2):
                        pages(vals, t * 2 + (2 + seq), k, 2 * seq + k, pj_done, t * 4 + (values + 2 * (seq + 1)))
            free[0] = free[1] = (pj_done, values + 14)
            free[2] = free[3] = (pj_done, values + 16)
            free[4] = (pj_done, values + 20)
            free[5] = (pj_done, values + 24)
            done[0] = values + 24
            moe_loads(1)

            sp.wait_ge(tb_evac, at["y_tok"])
            sp.dma_start(o["y_prompt"][0].rearrange("(j p) d -> p j d", p=P), tokA[:, 0:2, :]).then_inc(stored["yp"], 16)
            sp.dma_start(o["y_sample"].rearrange("b t d -> (b t) d"), tokA[0:NB, 2, :]).then_inc(stored["ys"], 16)
            for n in stored:
                sp.wait_ge(stored[n], 16)

        @block.gpsimd
        def _(pool):
            pool.dma_start(ptab[:], a["page_table"].rearrange("(o b) n -> o (b n)", o=1)).then_inc(table_in, 16)
            pool.dma_start(ws[:], a["a_w_s"][0].rearrange("g i j -> i g j")).then_inc(small_in, 16)
            pool.dma_start(bsb[:], a["a_b_s"].to_broadcast([P, 8, P])).then_inc(small_in, 16)
            pool.dma_start(ws00[:], a["a_w_s"][0:1, :, 0, 0].to_broadcast([P, 8]),
                           allow_slow_non_contiguous=True).then_inc(small_in, 16)
            pool.dma_start(rw[:], a["router_w"].rearrange("(k p) e -> p k e", p=P)).then_inc(small_in, 16)
            pool.dma_start(rbias[:], a["router_bias"].rearrange("(o e) -> o e", o=1).to_broadcast([P, NE])).then_inc(small_in, 16)
            for n, name in enumerate(("b_lam_q1", "b_lam_k1", "b_lam_q2", "b_lam_k2")):
                pool.dma_start(lamv[:, n, :], a[name]).then_inc(small_in, 16)
            pool.memset(epsc[:], EPS).then_inc(pool_own, 1)
            pool.iota(kint[:], pattern=[[-1, NE]], base=NE, channel_multiplier=0).then_inc(pool_own, 1)
            pool.wait_ge(pool_own, 2)
            pool.tensor_copy(kidx[:], kint[:]).then_inc(pool_own, 1)
            pool.wait_ge(small_in, 16 * 9)
            pool.affine_select(out=ws[:], in_=ws[:], compare_op=ALU.is_ge, fill=0.0, base=0,
                               pattern=[[0, 8], [-1, P]], channel_multiplier=1).then_inc(ws_masked, 1)
            pool.wait_ge(tb_evac, at["v_tok"])
            pool.dma_start(o["chunk_v_sample"].rearrange("l b t d -> (l b t) d"), tokA[0:NB, 2, :]).then_inc(stored["cv"], 16)
            pool.wait_ge(tb_evac, at["k_tok"])
            pool.dma_start(o["k_prompt"][0].rearrange("(j p) h c d -> p j (h c d)", p=P), tokB[:]).then_inc(stored["kp"], 16)
            pool.dma_start(o["k_sample"].rearrange("b t h c d -> (b t) (h c d)"), ksm[0:NB, :]).then_inc(stored["ks"], 16)
            pool.wait_ge(tb_evac, at["v2_tok"])
            pool.dma_start(o["v_prompt"][0].rearrange("(j p) h e -> p j (h e)", p=P), tokA[:, 0:2, :]).then_inc(stored["vp"], 16)
            pool.dma_start(o["v_sample"].rearrange("b t h e -> (b t) (h e)"), tokA[0:NB, 2, :]).then_inc(stored["vs"], 16)

        @block.scalar
        def _(act):
            g, inp, an, acc = Tally(pj_evac), Tally(act_in), Tally(a_ready), Tally(acc_done)
            banks = [0]

            def evac(dst, func=ACT.Copy, rows=P, n=T):
                bank = pj[banks[0] % NBANK]
                banks[0] += 1
                act.wait_ge(pj_done, g.add())
                act.activation(dst, bank[0:rows, 0:n], func).then_inc(pj_evac, 1)

            def answer(dst, src, func, **kw):
                act.wait_ge(act_in, inp.add())
                act.activation(dst, src, func, **kw).then_inc(act_out, 1)

            sd = Tally(st_done)

            def square(src):
                act.wait_ge(act_in, inp.add())
                act.activation(sqT[:], src, ACT.Square).then_inc(sq_ready, 1)

            def norm(src):
                square(src)
                act.wait_ge(st_done, sd.add(2))
                act.activation(rs[:], st[1][:, :], ACT.Sqrt, bias=epsc[:, 0:1]).then_inc(act_out, 1)

            def rows(l, n):
                if n >= 2:
                    act.wait_ge(tb_done, at[f"turn{l}_{n - 2}"])
                evac(mrow[:, n % 2, :], rows=NR, n=512)

            act.wait_ge(rows_in, 16 * 8)
            act.activation(crow, crow, ACT.Silu).then_inc(c_silu, 1)
            for n in range(12):
                rows(0, n)
            for f in range(2 * C):
                evac(abT[:, f, :], ACT.Gelu_apprx_tanh)
            act.wait_ge(pool_own, 1)
            norm(zT)
            for f in range(C):
                evac(yT[:, f, :])
            norm(yT[:])

            def moe(l):
                answer(score[:], lg[:], ACT.Exp)

                def up(par, wait):
                    for f in range(FB):
                        evac(aT[:, par, f, :], ACT.Silu)
                    if wait:
                        act.wait_ge(a_ready, an.add())
                    for f in range(FB):
                        evac(upT[:, f, :])

                def down(wait):
                    if wait:
                        act.wait_ge(acc_done, acc.add())
                    for d in range(C):
                        evac(sqT[:, d, :])

                up(0, False)
                up(1, True)
                down(False)
                up(0, True)
                down(True)
                with turns(act, 6, {g: 32, an: 2, acc: 2}):
                    up(1, True)
                    down(True)
                    up(0, True)
                    down(True)
                up(1, True)
                down(True)
                down(True)
                an.add()
                acc.add()

            moe(0)
            norm(yT[:])
            for f in range(2 * C):
                evac(abT[:, f, :])
            for n in range(4):
                rows(1, n)
            for f in range(C):
                evac(cqT[:, f, :])
            answer(lams[0:1, 2:4], lams[0:1, 0:2], ACT.Exp)
            for s in range(NB):
                if s >= 2:
                    act.wait_ge(keys_used, 2 * (s - 1))
                for n in range(2):
                    evac(qbc[:, s % 2, n * 512:(n + 1) * 512], n=512)
                rows(1, 4 + s)
            answer(sE, sE, ACT.Exp)
            answer(snew[:], snew[:], ACT.Exp)
            for h in range(H):
                for j in range(2):
                    n = (j + 1) * P
                    act.wait_ge(act_in, inp.add())
                    act.activation(pex[:, j, 0, 0:n], psc[:, j, 0, 0:n], ACT.Exp, bias=pst[:, j, 0:1],
                                   accum_out=pst[:, j, 2:3]).then_inc(act_out, 1)
                    act.activation(pex[:, j, 1, 0:n], psc[:, j, 1, 0:n], ACT.Exp, bias=pst[:, j, 1:2],
                                   accum_out=pst[:, j, 3:4]).then_inc(act_out, 1)
                if h:
                    act.wait_ge(tb_done, at[f"rows{h - 1}"])
                for n in range(2):
                    evac(osb[0:H, n * 512:(n + 1) * 512], rows=H, n=512)
            square(hT[:])
            act.wait_ge(tb_evac, at["rms"])
            act.activation(yT[:], yT[:], ACT.Sqrt).then_inc(act_out, 1)
            for f in range(C):
                evac(yT[:, f, :])
            norm(yT[:])
            moe(1)
            norm(yT[:])
            assert g.n == at["end"]

        @block.vector
        def _(dve):
            own, tbe, op, inp, out = Tally(dve_own), Tally(tb_evac), Tally(op_ready), Tally(act_in), Tally(act_out)
            an, acc, gp = Tally(a_ready), Tally(acc_done), Tally(pj_evac)
            sd = Tally(st_done)

            def link(ins):
                ins.then_inc(dve_own, 1)
                dve.wait_ge(dve_own, own.add())

            def last_empty():
                dve.wait_ge(tb_evac, tbe.value())

            def batch():
                dve.wait_ge(tb_done, tbe.value() + 1)
                return tb[tbe.n % 2]

            def empty(ins):
                ins.then_inc(tb_evac, 1)
                tbe.add()

            def ready(ins):
                ins.then_inc(op_ready, 1)
                dve.wait_ge(op_ready, op.add())

            def ask(ins):
                ins.then_inc(act_in, 1)
                inp.add()

            def answered(n=1):
                dve.wait_ge(act_out, out.add(n))

            def mod_rows(l, n):
                bank = batch()[:, 0:64].rearrange("p (c r) -> p c r", r=16)[:, :, 0:NR]
                plus = 1.0 if (n // 2) % 3 else 0.0
                bias = adabT[:, 48 * l + 4 * n:48 * l + 4 * n + 4].unsqueeze(2).to_broadcast([P, 4, NR])
                empty(dve.scalar_tensor_tensor(mT[:, 4 * n:4 * n + 4, :], bank, plus, bias, ALU.add, ALU.add))

            def modulate(sh, sc):
                for c in range(C):
                    dve.tensor_scalar(hT[:, c, 0:TP], xT[:, c, 0:TP], mT[:, sc + c, 0:1], mT[:, sh + c, 0:1],
                                      ALU.mult, ALU.add)
                link(dve.tensor_tensor(hT[:, :, TP:T], xT[:, :, TP:T], mT[:, sc:sc + C, 1:NR], ALU.mult))
                ready(dve.tensor_tensor(hT[:, :, TP:T], hT[:, :, TP:T], mT[:, sh:sh + C, 1:NR], ALU.add))

            def residual(gate, groups):
                link(dve.tensor_scalar(xT[:], xT[:], ALPHA, None, ALU.mult))
                if groups:
                    dve.wait_ge(pj_evac, groups)
                for c in range(C):
                    dve.scalar_tensor_tensor(yT[:, c, 0:TP], yT[:, c, 0:TP], mT[:, gate + c, 0:1], xT[:, c, 0:TP],
                                             ALU.mult, ALU.add)
                link(dve.tensor_tensor(yT[:, :, TP:T], yT[:, :, TP:T], mT[:, gate:gate + C, 1:NR], ALU.mult))
                ready(dve.tensor_tensor(yT[:, :, TP:T], yT[:, :, TP:T], xT[:, :, TP:T], ALU.add))

            def across(x):
                return x.unsqueeze(1).to_broadcast([P, C, T])

            def norm(src, dst, g0, b0):
                dve.wait_ge(st_done, sd.add())
                ask(dve.tensor_tensor(src, src, across(st[0][:, :]), ALU.subtract))
                sd.add()
                answered()
                link(dve.reciprocal(rs[:], rs[:]))
                link(dve.tensor_tensor(src, src, across(rs[:]), ALU.mult))
                for c in range(C):
                    i = dve.tensor_scalar(dst[:, c, :], src[:, c, :], vT[:, g0 + c:g0 + c + 1], vT[:, b0 + c:b0 + c + 1],
                                          ALU.mult, ALU.add)
                return i

            def tokens(sample, prompt):
                for q in range(2):
                    empty(dve.tensor_copy(sample[0:NB, q * 512:(q + 1) * 512], batch()[0:NB, :]))
                for j in range(2):
                    for q in range(2):
                        empty(dve.tensor_copy(prompt[:, j, q * 512:(q + 1) * 512], batch()[:, :]))

            link(dve.memset(lg[:], 0.0))
            bank = batch()
            link(dve.tensor_copy(vT[:], bank[:, 0:V_N]))
            empty(dve.tensor_copy(adabT[:], bank[:, P:P + 96]))
            empty(dve.tensor_copy(cT[:], batch()[:, 0:128].rearrange("p (c r) -> p c r", r=16)[:, :, 0:NR]))
            for j in range(2):
                for q in range(2):
                    empty(dve.tensor_copy(xT[:, 4 * q:4 * q + 4, j * P:(j + 1) * P],
                                          batch()[:, :].rearrange("p (c t) -> p c t", c=4)))
            empty(dve.tensor_copy(xT[:, :, TP:T], batch()[:, 0:128].rearrange("p (c r) -> p c r", r=16)[:, :, 0:NB]))
            for n in range(12):
                mod_rows(0, n)
            for q in range(2):
                empty(dve.tensor_copy(wsT[:, 4 * q:4 * q + 4, :], batch()[:, :].rearrange("p (c t) -> p c t", c=4)))
            last_empty()
            modulate(0, 8)

            ready(norm(zT, zT, V_AG, V_AB))
            tokens(tokA[:, 2, :], tokA)
            dve.wait_ge(small_in, 16 * 9)
            for q in range(4):
                mix = psc[:, q % 2, :, :].rearrange("p g (j i) -> p g j i", j=2)
                empty(dve.tensor_tensor(mix, batch()[:, :].rearrange("p (g j i) -> p g j i", g=2, j=2),
                                        bsb[:, 2 * q:2 * q + 2, :].unsqueeze(2).to_broadcast([P, 2, 2, P]), ALU.add))
                last_empty()
                dve.tensor_tensor(uT[:, 2 * q:2 * q + 2, 0:TP], uT[:, 2 * q:2 * q + 2, 0:TP], psc[:, q % 2, :, :], ALU.mult)
            mix = rs[:, 0:64].rearrange("p (c b) -> p c b", b=NB)
            link(dve.tensor_tensor(mix, zT[:, :, TP:T], ws00[:].unsqueeze(2).to_broadcast([P, C, NB]), ALU.mult))
            link(dve.tensor_tensor(mix, mix, bsb[:, :, 0:1].to_broadcast([P, C, NB]), ALU.add))
            ready(dve.tensor_tensor(uT[:, :, TP:T], uT[:, :, TP:T], mix, ALU.mult))
            residual(16, at["a_out"])
            link(norm(yT[:], xT, V_LNG, V_LNB))

            def reduce(dst, src, op):
                link(dve.tensor_reduce(dst, src, AX.X, op))

            def first_max(dst, src, keys, shape):
                reduce(one[:], src, ALU.max)
                link(dve.tensor_tensor(dst, src, one[:].to_broadcast(shape), ALU.is_equal))
                link(dve.tensor_tensor(dst, dst, keys, ALU.mult))
                reduce(one[:], dst, ALU.max)
                link(dve.tensor_tensor(dst, dst, one[:].to_broadcast(shape), ALU.is_equal))

            dve.wait_ge(pool_own, 3)

            def moe(l):
                modulate(24, 32)
                empty(dve.tensor_copy(lgT[:], batch()[0:NE, 0:T]))
                bank = batch()[:, 0:3 * NE].rearrange("p (j e) -> p j e", e=NE)
                dve.tensor_copy(lg[:, 0:2, :], bank[:, 0:2, :])
                empty(dve.tensor_copy(lg[0:NB, 2, :], bank[0:NB, 2, :]))
                last_empty()
                full = [P, 3, NE]
                reduce(one[:], lg[:], ALU.max)
                ask(dve.tensor_tensor(lg[:], lg[:], one[:].to_broadcast(full), ALU.subtract))
                answered()
                reduce(one[:], score[:], ALU.add)
                link(dve.reciprocal(one[:], one[:]))
                link(dve.tensor_tensor(score[:], score[:], one[:].to_broadcast(full), ALU.mult))
                link(dve.tensor_tensor(sel[:], score[:], rbias[:].unsqueeze(1).to_broadcast(full), ALU.add))
                s4 = sel[:].rearrange("p j (g e) -> p j g e", e=EG)
                dve.tensor_tensor(pair[0][:], s4[:, :, :, 0], s4[:, :, :, 1], ALU.max)
                dve.tensor_tensor(pair[1][:], s4[:, :, :, 0], s4[:, :, :, 1], ALU.min)
                dve.tensor_tensor(pair[2][:], s4[:, :, :, 2], s4[:, :, :, 3], ALU.max)
                link(dve.tensor_tensor(pair[3][:], s4[:, :, :, 2], s4[:, :, :, 3], ALU.min))
                link(dve.tensor_tensor(pair[1][:], pair[1][:], pair[3][:], ALU.max))
                dve.tensor_tensor(pair[3][:], pair[0][:], pair[2][:], ALU.min)
                link(dve.tensor_tensor(pair[0][:], pair[0][:], pair[2][:], ALU.max))
                link(dve.tensor_tensor(pair[1][:], pair[1][:], pair[3][:], ALU.max))
                link(dve.tensor_tensor(pair[0][:], pair[0][:], pair[1][:], ALU.add))
                first_max(pair[2][:], pair[0][:], kidx[:, 12:16].unsqueeze(1).to_broadcast([P, 3, EG]), [P, 3, EG])
                link(dve.tensor_scalar(pair[2][:], pair[2][:], -NEG, NEG, ALU.mult, ALU.add))
                link(dve.tensor_tensor(s4, s4, pair[2][:].unsqueeze(3).to_broadcast([P, 3, EG, EG]), ALU.add))
                keys = kidx[:].unsqueeze(1).to_broadcast(full)
                first_max(top[0][:], sel[:], keys, full)
                link(dve.scalar_tensor_tensor(sel[:], top[0][:], 2 * NEG, sel[:], ALU.mult, ALU.add))
                first_max(top[1][:], sel[:], keys, full)
                link(dve.tensor_tensor(top[0][:], top[0][:], top[1][:], ALU.add))
                link(dve.tensor_tensor(score[:], score[:], top[0][:], ALU.mult))
                reduce(one[:], score[:], ALU.add)
                link(dve.reciprocal(one[:], one[:]))
                ready(dve.tensor_tensor(lg[:], score[:], one[:].to_broadcast(full), ALU.mult))
                empty(dve.tensor_copy(lgT[:], batch()[0:NE, 0:T]))
                for e in range(NE):
                    empty(dve.tensor_copy(abT[:, e, :], batch()[:, 0:T]))
                last_empty()
                link(dve.memset(yT[:], 0.0))
                gp.n = at[f"moe{l}"]

                def gated(par, e):
                    dve.wait_ge(pj_evac, gp.add(8))
                    link(dve.tensor_tensor(aT[:, par, :, :], aT[:, par, :, :], upT, ALU.mult))
                    dve.tensor_tensor(aT[:, par, :, :], aT[:, par, :, :], abT[:, bass.ds(e, 1), :].to_broadcast([P, FB, T]),
                                      ALU.mult).then_inc(a_ready, 1)
                    an.add()

                def added():
                    dve.wait_ge(pj_evac, gp.add(8))
                    dve.tensor_tensor(yT[:], yT[:], sqT[:], ALU.add).then_inc(acc_done, 1)
                    dve.wait_ge(acc_done, acc.add())

                gated(0, 0)
                gated(1, 1)
                added()
                gated(0, 2)
                added()
                with turns(dve, 6, {gp: 32, own: 2, an: 2, acc: 2}) as i:
                    gated(1, i * 2 + 3)
                    added()
                    gated(0, i * 2 + 4)
                    added()
                gated(1, 15)
                added()
                added()
                residual(40, None)

            moe(0)
            ready(norm(yT[:], xT, V_LNG + 8, V_LNB + 8))

            for n in range(4):
                mod_rows(1, n)
            last_empty()
            modulate(0, 8)
            cos = kst[:, K_COS:K_COS + T]
            sin = kst[:, K_SIN:K_SIN + T]
            for x in (uT, cqT[:]):
                for h in range(H):
                    turned = sqT[:, h, :]
                    empty(dve.tensor_tensor(turned, batch()[:, 0:T], sin, ALU.mult))
                last_empty()
                link(dve.tensor_tensor(x, x, across(cos), ALU.mult))
                i = dve.tensor_tensor(x, x, sqT[:], ALU.add)
                if x is uT:
                    link(i)
            ready(i)
            for q in range(2):
                empty(dve.tensor_scalar(qtok[0:NB, q * 512:(q + 1) * 512], batch()[0:NB, :], HD ** -0.5, None, ALU.mult))
            ready(dve.tensor_tensor(rs[:, 0:64].rearrange("p (h b) -> p h b", b=NB), cqT[:, :, TP:T], uT[:, :, TP:T], ALU.mult))
            for c in range(2):
                empty(dve.tensor_scalar(snew[:].rearrange("p b (h c) -> p c h b", c=2)[:, c],
                                        batch()[:, 0:64].rearrange("p (h b) -> p h b", b=NB), HD ** -0.5, None, ALU.mult))
            lv = lamv.rearrange("o (a b) d -> o a b d", b=2)
            link(dve.tensor_tensor(lv[:, :, 0, :], lv[:, :, 0, :], lv[:, :, 1, :], ALU.mult))
            ask(dve.tensor_reduce(lams[0:1, 0:2].unsqueeze(2), lv[:, :, 0, :], AX.X, ALU.add))
            answered()
            link(dve.tensor_tensor(lams[0:1, 4:5], lams[0:1, 3:4], lams[0:1, 2:3], ALU.subtract))
            ready(dve.tensor_scalar(lams[0:1, 4:5], lams[0:1, 4:5], -LAM_INIT, None, ALU.add))
            empty(dve.tensor_copy(nlam[:], batch()[:, 0:1]))
            link(dve.tensor_scalar(subg[:], vT[:, V_SUB:V_SUB + 1], 1.0 - LAM_INIT, None, ALU.mult))
            tokens(ksm, tokB)
            dve.wait_ge(stored["cv"], 16)
            tokens(tokA[:, 2, :], tokA)
            dve.wait_ge(stored["kp"], 16)

            for s in range(NB):
                dve.wait_ge(pj_evac, at["spread"] + 3 * s + 2)
                for k in range(2):
                    slot = 2 * (s % 2) + k
                    dve.wait_ge(slot_in[slot], at["key_loads"][slot] + 64 * (s // 2 + 1))
                    for q in range(2):
                        two = [P, 2, D]
                        link(dve.tensor_tensor(prod.rearrange("p (g n) -> p g n", g=2),
                                               wring[:, slot, q * 2 * D:(q + 1) * 2 * D].rearrange("p (g n) -> p g n", g=2),
                                               qbc[:, s % 2:s % 2 + 1, :].to_broadcast(two), ALU.mult))
                        c0 = s * 128 + (4 * k + 2 * q) * 16
                        i = dve.tensor_reduce(sS[:, c0:c0 + 32], prod.rearrange("p (x d) -> p x d", d=HD), AX.X, ALU.add)
                        if q == 0:
                            link(i)
                    i.then_inc(keys_used, 1)
                    dve.wait_ge(keys_used, 2 * s + k + 1)
                mod_rows(1, 4 + s)
            last_empty()

            by_page = sS.rearrange("p (b g x) -> p b x g", b=NB, g=NPG)
            m3 = smx.rearrange("p (b x) -> p b x", b=NB)
            ready(dve.tensor_reduce(m3, by_page, AX.X, ALU.max))
            empty(dve.tensor_reduce(scol[:], batch()[:, 0:P], AX.X, ALU.max))
            empty(dve.tensor_copy(srow, batch()[0:1, 0:P]))
            empty(dve.tensor_tensor(m3, batch()[:, 0:P].rearrange("p (b x) -> p b x", b=NB), snew[:], ALU.max))
            last_empty()
            e4 = sE.rearrange("p (b g x) -> p b g x", b=NB, g=NPG)
            wide = [P, NB, NPG, 16]
            ask(dve.tensor_tensor(e4, sS.rearrange("p (b g x) -> p b g x", b=NB, g=NPG),
                                  m3.unsqueeze(2).to_broadcast(wide), ALU.subtract))
            ask(dve.tensor_tensor(snew[:], snew[:], m3, ALU.subtract))
            dve.wait_ge(act_in, inp.value())
            answered()
            ready(dve.tensor_reduce(m3, sE.rearrange("p (b g x) -> p b x g", b=NB, g=NPG), AX.X, ALU.add))
            answered()
            empty(dve.tensor_tensor(m3, batch()[:, 0:P].rearrange("p (b x) -> p b x", b=NB), snew[:], ALU.add))
            last_empty()
            link(dve.reciprocal(smx, smx))
            odd = smx.rearrange("p (x c) -> p x c", c=2)[:, :, 1:2]
            link(dve.tensor_scalar(odd, odd, nlam[:, 0:1], None, ALU.mult))
            dve.tensor_tensor(e4, e4, m3.unsqueeze(2).to_broadcast(wide), ALU.mult)
            link(dve.tensor_tensor(snew[:], snew[:], m3, ALU.mult))
            e5 = sE.rearrange("p (b x c) -> p b x c", b=NB, c=2)
            dve.tensor_tensor(sW.rearrange("p b g h -> p b (g h)"), e5[:, :, :, 0], e5[:, :, :, 1], ALU.add)
            n4 = snew[:].rearrange("p b (h c) -> p b h c", c=2)
            ready(dve.tensor_tensor(wnew, n4[:, :, :, 0], n4[:, :, :, 1], ALU.add))

            for h in range(H):
                for c in range(2):
                    bank = batch()
                    for j in range(2):
                        n = (j + 1) * P
                        i = dve.scalar_tensor_tensor(psc[:, j, c, 0:n], bank[:, P * j:P * j + n], HD ** -0.5,
                                                     kst[:, K_MASK + (1 - j) * P:K_MASK + 2 * P], ALU.mult, ALU.add)
                    empty(i)
                last_empty()
                for j in range(2):
                    n = (j + 1) * P
                    ask(dve.tensor_reduce(pst[:, j, 0:2].unsqueeze(2), psc[:, j, :, 0:n], AX.X, ALU.max, negate=True))
                for j in range(2):
                    n = (j + 1) * P
                    answered(2)
                    link(dve.reciprocal(pst[:, j, 4:6], pst[:, j, 2:4]))
                    dve.tensor_scalar(psc[:, j, 0, 0:n], pex[:, j, 0, 0:n], pst[:, j, 4:5], None, ALU.mult)
                    link(dve.tensor_scalar(pst[:, j, 5:6], pst[:, j, 5:6], nlam[:, 0:1], None, ALU.mult))
                    ready(dve.scalar_tensor_tensor(pex[:, j, 0, 0:n], pex[:, j, 1, 0:n], pst[:, j, 5:6], psc[:, j, 0, 0:n],
                                                   ALU.mult, ALU.add))
                for j in range(2):
                    empty(dve.tensor_copy(pwT[:, j, 0:j + 1, :], batch()[:, 0:(j + 1) * P].rearrange("p (t q) -> p t q", q=P)))
                for j in range(2):
                    empty(dve.tensor_copy(hT[:, h, j * P:(j + 1) * P], batch()[:, 0:P]))
                empty(dve.tensor_copy(hT[:, :, TP + h:TP + h + 1], batch()[:, 0:(H + 1) * (H - 1) + 1:H + 1].unsqueeze(2)))
            mix = rs[:, 0:64].rearrange("p (h b) -> p h b", b=NB)
            link(dve.tensor_tensor(mix, zT[:, :, TP:T], wnew.rearrange("p b h -> p h b"), ALU.mult))
            ask(dve.tensor_tensor(hT[:, :, TP:T], hT[:, :, TP:T], mix, ALU.add))
            for h in range(H):
                empty(dve.tensor_scalar(yT[:, h, :], batch()[:, 0:T], 1.0 / P, EPS, ALU.mult, ALU.add))
            answered()
            link(dve.reciprocal(yT[:], yT[:]))
            link(dve.tensor_tensor(hT[:], hT[:], yT[:], ALU.mult))
            ready(dve.tensor_scalar(hT[:], hT[:], subg[:, 0:1], None, ALU.mult))
            residual(16, at["b_out"])
            link(norm(yT[:], xT, V_LNG + 16, V_LNB + 16))
            moe(1)
            ready(norm(yT[:], xT, V_LNG + 24, V_LNB + 24))
            dve.wait_ge(stored["vp"], 16)
            dve.wait_ge(stored["vs"], 16)
            tokens(tokA[:, 2, :], tokA)


_OUTS = [("y_prompt", (1, TP, D)), ("y_sample", (NB, 1, D)), ("k_prompt", (1, TP, H, 2, HD)),
         ("v_prompt", (1, TP, H, P)), ("k_sample", (NB, 1, H, 2, HD)), ("v_sample", (NB, 1, H, P)),
         ("chunk_v_sample", (1, NB, 1, D))]


def kernel(**inputs):
    import concourse.bacc as bacc
    from concourse.bass_utils import run_bass_kernel_spmd

    nc = bacc.Bacc("TRN2", target_bir_lowering=False, num_devices=1)
    arrays = {f"in_{n}": np.ascontiguousarray(v) for n, v in inputs.items()}
    arrays["in_consts"] = constants()
    ins = {n[3:]: nc.dram_tensor(n, v.shape, mybir.dt.from_np(v.dtype), kind="ExternalInput").ap()
           for n, v in arrays.items()}
    outs = {n: nc.dram_tensor(f"out_{n}", s, F32, kind="ExternalOutput").ap() for n, s in _OUTS}
    build(nc, ins, outs)
    r = run_bass_kernel_spmd(nc, [arrays], core_ids=[0])
    return tuple(r.results[0][f"out_{n}"] for n, _ in _OUTS)
```

```python
import math
from contextlib import ExitStack, contextmanager

import numpy as np

import concourse.bass as bass
from concourse import mybir

F32 = mybir.dt.float32
I32 = mybir.dt.int32
ALU = mybir.AluOpType
ACT = mybir.ActivationFunctionType
AX = mybir.AxisListType

P = 128
D = 1024
C = D // P
TP = 256
NB = 8
T = TP + NB
DEPTH = 2
NE = 16
EG = 4
FE = 512
FB = FE // P
H = 8
HD = 64
PAST = 1024
PAGE = 128
NPG = PAST // PAGE
POOLN = 80
ROT = HD // 4
ALPHA = (2 * DEPTH) ** 0.25
EPS = 1e-5
LAM_INIT = 0.8 - 0.6 * math.exp(-0.3 * 1)
NEG = -1e30
SLOTS = 6
TILE = 4096
NBANK = 4
TOP = 2
SLOT_N = TOP * T
SPAN = P
PACK = SLOT_N + SPAN
NK = -(-SLOT_N // P)
LAST = SLOT_N - (NK - 1) * P
NR = 1 + NB
PAIRS = ((2, 0), (1, 3), (4, 5))
LOADS = [("k", 0), ("k", 1)] + [x for m in range(NB - 2) for x in (("k", m + 2), ("v", m))] + [("v", NB - 2), ("v", NB - 1)]

K_ID, K_ROT, K_ONE, K_TRI, K_MASK, K_IOTA, K_PART = 0, 128, 256, 384, 512, 768, 768 + T
K_N = 768 + T + 5
V_LNG, V_LNB, V_AG, V_AB, V_SUB, V_N = 0, 32, 64, 72, 80, 81


def constants():
    k = np.zeros((P, K_N), np.float32)
    k[:, K_ID:K_ID + P] = np.eye(P)
    half = ROT // 2
    for c in range(2):
        for i in range(half):
            a, b = c * HD + i, c * HD + half + i
            k[b, K_ROT + a] = -1.0
            k[a, K_ROT + b] = 1.0
    k[:, K_ONE:K_ONE + P] = 1.0
    k[:, K_TRI:K_TRI + P] = np.arange(P)[:, None] < np.arange(P)[None, :]
    k[:, K_IOTA:K_IOTA + T] = np.arange(T)
    k[:, K_MASK + P:K_MASK + 2 * P] = np.where(
        np.arange(P)[:, None] >= np.arange(P)[None, :], 0.0, NEG)
    k[:, K_PART:K_PART + 5] = np.arange(P)[:, None] + P * np.arange(5)[None, :]
    return k


def rotary():
    k = np.zeros((P, 2, T), np.float32)
    half = ROT // 2
    inv = 1.0 / (np.float32(500000.0) ** (np.arange(0, ROT, 2, dtype=np.float32) / ROT))
    pos = np.concatenate([np.arange(TP), np.full(NB, PAST)]).astype(np.float32)
    ang = (pos[None, :] * inv.astype(np.float32)[:, None]).astype(np.float32)
    k[:, 0] = 1.0
    for c in range(2):
        for r in range(2):
            a = c * HD + r * half
            k[a:a + half, 0] = np.cos(ang)
            k[a:a + half, 1] = np.sin(ang)
    return k


def cache_slot(kind, seq, k):
    j = LOADS.index((kind, seq))
    return PAIRS[j % 3][k], 4 * (j // 3 + 1)


class Tally:

    def __init__(self, sem):
        self.sem, self.n, self.turn = sem, 0, None

    def add(self, k=1):
        self.n += k
        return self.value()

    def value(self, back=0):
        v = self.n - back
        return v if self.turn is None else self.turn + v


@contextmanager
def turns(eng, count, per):
    before = {t: t.n for t in per}
    with eng.Fori(0, count) as i:
        for t, k in per.items():
            t.turn = i * k
        yield i
    for t, k in per.items():
        assert t.n - before[t] == k, (t.sem, t.n - before[t], k)
        t.turn = None
        t.n = before[t] + k * count


def build(nc, a, o):
    with ExitStack() as ctx:
        def sb(name, shape, dt=F32):
            return ctx.enter_context(nc.sbuf_tensor(name, shape, dt))

        def sem(name):
            return ctx.enter_context(nc.semaphore(name))

        wring = sb("wring", [P, SLOTS, TILE])
        kst = sb("kst", [P, K_N])
        xT = sb("xT", [P, C, T])
        hT = sb("hT", [P, C, T])
        yT = sb("yT", [P, C, T])
        reg1 = sb("reg1", [P, C * PACK])
        reg2 = sb("reg2", [P, C * PACK])
        tokA = sb("tokA", [P, 3, D])
        tokB = sb("tokB", [P, 2, D])
        ws = sb("ws", [P, 8, P])
        wsT = sb("wsT", [P, 8, P])
        bsb = sb("bsb", [P, 8, P])
        ws00 = sb("ws00", [P, 8])
        rw = sb("rw", [P, C, NE])
        rbias = sb("rbias", [P, NE])
        vT = sb("vecT", [P, V_N])
        adabT = sb("adabT", [P, 96])
        cT = sb("cT", [P, C, NR])
        mT = sb("mT", [P, 48, NR])
        rs = sb("rs", [P, T])
        epsc = sb("epsc", [P, 1])
        lgT = sb("lgT", [NE, T])
        lg = sb("lg", [P, 3, NE])
        score = sb("score", [P, 3, NE])
        sel = sb("sel", [P, 3, NE])
        top = [sb(f"top{i}", [P, 3, NE]) for i in range(2)]
        key = sb("key", [P, 3, NE])
        pair = [sb(f"pair{i}", [P, 3, EG]) for i in range(4)]
        one = sb("one", [P, 3, 1])
        stack = sb("stack", [P, 3, 4, NE])
        sg = sb("sg", [P, 3, 6])
        ncol = sb("ncol", [NE, 1])
        pos = sb("pos", [P, 3, NE])
        nrow = sb("nrow", [P, 2 * NE])
        lim = sb("lim", [P, 2, NE])
        starts = sb("starts", [1, 3 * NE + 1], I32)
        startf = sb("startf", [1, 3 * NE + 1])
        kidx = sb("kidx", [P, NE])
        ptab = sb("ptab", [1, NB * NPG], I32)
        lamx = sb("lamx", [P, 4, HD])
        lams = sb("lams", [1, 5])
        nlam = sb("nlam", [P, 1])
        subg = sb("subg", [P, 1])
        pst = sb("pst", [P, 2, 6])
        scol = sb("scol", [P, 1])

        abT = reg1[:, 0:2 * C * T].rearrange("p (c t) -> p c t", t=T)
        crows = reg1[:, 2 * C * T:C * PACK]
        cqT = reg2[:, 0:C * T].rearrange("p (c t) -> p c t", t=T)
        sqT = reg2[:, C * T:2 * C * T].rearrange("p (c t) -> p c t", t=T)
        mrows = reg2[:, 2 * C * T:C * PACK]
        xg = reg1[:, :].rearrange("p (c n) -> p c n", n=PACK)
        yg = reg2[:, :].rearrange("p (c n) -> p c n", n=PACK)
        yr = reg1[:, 0:NK * D].rearrange("p (k n) -> p k n", n=D)
        pick = yT[:, :, :].rearrange("p c t -> p (c t)")[:, 0:3 * SLOT_N].rearrange("p (j n) -> p j n", n=SLOT_N)
        put = hT[:, :, :].rearrange("p c t -> p (c t)")[:, 0:NK * T].rearrange("p (k t) -> p k t", t=T)
        piece = hT[:, :, :].rearrange("p c t -> p (c t)")[:, 0:2048].rearrange("p (b k n) -> p b k n", b=2, n=P)
        flatB = tokB[:, :, :].rearrange("p b n -> p (b n)")
        aT = flatB[:, 0:1024].rearrange("p (b f n) -> p b f n", b=2, n=P)
        upT = flatB[:, 1024:1536].rearrange("p (f n) -> p f n", n=P)
        sgB = flatB[:, 0:4 * T].rearrange("p (i t) -> p i t", t=T)
        xe = tokA[:, 0:2, :].rearrange("p b (c n) -> p b c n", n=P)
        cos, sin = flatB[:, 0:T], flatB[:, T:2 * T]
        snew = stack[:, :, :, :].rearrange("p j i e -> p (j i) e")[:, 0:NB, :]
        sS = flatB[:, 0:NB * (NPG + 1) * 16].rearrange("p (b g x) -> p b g x", b=NB, g=NPG + 1)
        vrow = tokA[0:V_N, 0, 0:P]
        arow = tokA[0:96, 0, P:2 * P]
        crow = crows[0:NR, :]
        psc = mrows[:, :].rearrange("p (j c s) -> p j c s", j=2, c=2)
        pex = crows[:, :].rearrange("p (j c s) -> p j c s", j=2, c=2)
        sW = wsT[:, 0:4, :].rearrange("p a (x g h) -> p (a x) g h", g=NPG, h=H)
        pwT = wsT[:, 4:8, :].rearrange("p (j t) q -> p j t q", j=2)
        lamv = lamx[0:1, :, :]
        smx = lamx[:, 2:4, :].rearrange("p a d -> p (a d)")
        wnew = lamx[:, 0, :].rearrange("p (b h) -> p b h", b=NB)
        uT = abT[:, 0:C, :]
        zT = abT[:, C:2 * C, :]
        ident = kst[:, K_ID:K_ID + P]
        qbc = yT[:, :, :].rearrange("p c t -> p (c t)")[:, 0:2 * D].rearrange("p (b n) -> p b n", b=2)
        prod = sqT[:, :, :].rearrange("p c t -> p (c t)")[:, 0:2 * D]
        ksm = ws[:, :, :].rearrange("p g n -> p (g n)")
        osb = ksm
        qtok = bsb[:, :, :].rearrange("p g n -> p (g n)")

        def mrow(l, n):
            rows = mrows if l == 0 and n < 10 else qtok
            return rows[0:NR, (n % 2) * 512:(n % 2 + 1) * 512]

        def before(l, n):
            return (l, n - 2) if n >= 2 else (l - 1, n + 10)

        pj = [ctx.enter_context(nc.psum_tensor(f"pj{i}", [P, 512], F32)) for i in range(NBANK)]
        tb = [ctx.enter_context(nc.psum_tensor(f"tb{i}", [P, 512], F32)) for i in range(2)]
        st = [ctx.enter_context(nc.psum_tensor(f"st{i}", [P, T], F32)) for i in range(2)]

        consts_in, rows_in, x_in, small_in, table_in = (
            sem(n) for n in ("consts_in", "rows_in", "x_in", "small_in", "table_in"))
        slot_in = [sem(f"slot{i}_in") for i in range(SLOTS)]
        stored = {n: sem(f"{n}_stored") for n in ("cv", "kp", "ks", "vp", "vs", "yp", "ys")}
        pool_own = sem("pool_own")
        ws_masked = sem("ws_masked")
        c_silu = sem("c_silu")
        pj_done, pj_evac = sem("pj_done"), sem("pj_evac")
        tb_done, tb_evac = sem("tb_done"), sem("tb_evac")
        st_done = sem("st_done")
        dve_own = sem("dve_own")
        op_ready = sem("op_ready")
        act_in = sem("act_in")
        act_out = sem("act_out")
        sq_ready = sem("sq_ready")
        a_ready = sem("a_ready")
        xe_ready = sem("xe_ready")
        yg_clear = sem("yg_clear")
        rotary_in = sem("rotary_in")
        routed = sem("routed")
        more = [{n: sem(f"more{l}_{n}") for n in ("x", "piece", "done", "silu", "evac", "mask")} for l in range(DEPTH)]
        keys_used = sem("keys_used")
        values_used = sem("values_used")

        at = {}
        block = ctx.enter_context(nc.Block())

        @block.tensor
        def _(pe):
            g, b, sd = Tally(pj_done), Tally(tb_done), Tally(st_done)
            op, an, sqn = Tally(op_ready), Tally(a_ready), Tally(sq_ready)
            loads = [0] * SLOTS
            banks = [0]
            uses = at["uses"] = []

            def loaded(s, k=1, turn=0):
                loads[s] += 16 * k
                pe.wait_ge(slot_in[s], turn + loads[s])

            def operand():
                pe.wait_ge(op_ready, op.add())

            def squares():
                pe.wait_ge(sq_ready, sqn.add())

            def group(rows, n, pairs):
                k = banks[0]
                banks[0] += 1
                if k >= NBANK:
                    pe.wait_ge(pj_evac, g.value(NBANK - 1))
                out = pj[k % NBANK][0:rows, 0:n]
                for j, (lhsT, rhs) in enumerate(pairs):
                    m = pe.matmul(out, lhsT, rhs, start=(j == 0), stop=(j == len(pairs) - 1))
                m.then_inc(pj_done, 1)
                g.add()

            def small(parts):
                if b.n >= 2:
                    pe.wait_ge(tb_evac, b.value(1))
                bank = tb[b.n % 2]
                for (rows, c0, n), fn in parts:
                    m = fn(bank[0:rows, c0:c0 + n])
                m.then_inc(tb_done, 1)
                b.add()

            def emptied():
                pe.wait_ge(tb_evac, b.value())

            def tr(src, rows=P):
                return lambda dst: pe.transpose(dst, src, ident[0:rows, 0:rows])

            def mm(lhsT, rhs, start=True, stop=True):
                return lambda dst: pe.matmul(dst, lhsT, rhs, start=start, stop=stop)

            def project(s, src, turn=0):
                loaded(s, turn=turn)
                w = wring[:, s, :].rearrange("p (k n) -> p k n", n=512)
                for f in range(4):
                    group(P, T, [(w[:, k, f * P:(f + 1) * P], src[:, k, :]) for k in range(C)])
                uses.append((s, g.n))

            def stat(src, which):
                for k in range(C):
                    m = pe.matmul(st[which][:, :], kst[:, K_ONE:K_ONE + P], src[:, k, :],
                                  start=(k == 0), stop=(k == C - 1))
                m.then_inc(st_done, 1)
                sd.add()

            def norm(src, beside=lambda: None):
                stat(src, 0)
                beside()
                squares()
                stat(sqT, 1)

            def to_tokens(src):
                for q in range(2):
                    small([((NB, c * P, P), tr(src[:, 4 * q + c, TP:T])) for c in range(4)])
                for j in range(2):
                    for q in range(2):
                        small([((P, c * P, P), tr(src[:, 4 * q + c, j * P:(j + 1) * P])) for c in range(4)])

            row_group = {}

            def ada_tile(l, n, s):
                loaded(s)
                w = wring[:, s, :].rearrange("p (k n) -> p k n", n=512)
                group(NR, 512, [(cT[:, k, :], w[:, k, :]) for k in range(C)])
                row_group[l, n] = g.n
                uses.append((s, g.n))

            def ada_turn(l, n):
                pe.wait_ge(pj_evac, row_group[l, n])
                small([((P, 16 * c, NR), tr(mrow(l, n)[:, c * P:(c + 1) * P], NR)) for c in range(4)])
                at[f"turn{l}_{n}"] = b.n

            pe.wait_ge(consts_in, 16)
            pe.wait_ge(rows_in, 16 * 8)
            small([((P, 0, V_N), tr(vrow, V_N)), ((P, P, 96), tr(arow, 96))])
            pe.wait_ge(c_silu, 1)
            small([((P, 16 * c, NR), tr(crow[:, c * P:(c + 1) * P], NR)) for c in range(C)])
            pe.wait_ge(x_in, 32)
            for j in range(2):
                for q in range(2):
                    small([((P, c * P, P), tr(tokB[:, j, (4 * q + c) * P:(4 * q + c + 1) * P])) for c in range(4)])
            small([((P, 16 * c, NB), tr(tokA[0:NB, 2, c * P:(c + 1) * P], NB)) for c in range(C)])
            for n in range(4):
                ada_tile(0, n, n)
                if n:
                    ada_turn(0, n - 1)
            ada_turn(0, 3)
            pe.wait_ge(ws_masked, 1)
            for q in range(2):
                small([((P, c * P, P), tr(ws[:, 4 * q + c, :])) for c in range(4)])
            ada_tile(0, 4, 4)

            operand()
            for s in (5, 0, 1, 2):
                project(s, hT)
            at["uv"] = g.n
            ada_turn(0, 4)
            pe.wait_ge(pj_evac, g.n)
            norm(zT, lambda: ada_tile(0, 5, 3))
            ada_turn(0, 5)
            ada_tile(0, 6, 4)
            operand()
            to_tokens(zT)
            at["v_tok"] = b.n
            emptied()
            for q in range(4):
                small([((P, P * (2 * i + j), P), mm(tokA[:, j, (2 * q + i) * P:(2 * q + i + 1) * P], wsT[:, 2 * q + i, :]))
                       for i in range(2) for j in range(2)])
            ada_turn(0, 6)
            ada_tile(0, 7, 5)
            operand()
            for s in (0, 1):
                project(s, uT)
            at["a_out"] = g.n
            ada_turn(0, 7)
            ada_tile(0, 8, 2)
            operand()

            def beside():
                ada_turn(0, 8)
                ada_tile(0, 9, 3)

            norm(yT, beside)
            ada_turn(0, 9)
            ada_tile(0, 10, 4)

            def moe(l):
                operand()
                small([((NE, 0, T), mm(rw[:, k, :], hT[:, k, :], k == 0, k == C - 1)) for k in range(C)])
                emptied()
                small([((n, NE * j, NE), tr(lgT[:, j * P:j * P + n], NE)) for j, n in enumerate((P, P, NB))])
                at[f"router{l}"] = b.n
                ada_tile(l, 11, (5, 2)[l])
                to_tokens(hT)
                operand()
                tiles = (P, P, NB)
                small([((NE, 0, 1), mm(key[0:n, j, :], kst[0:n, K_ONE:K_ONE + 1], j == 0, j == 2))
                       for j, n in enumerate(tiles)])
                emptied()
                count = ncol[:, 0:1].to_broadcast([NE, P])
                below = kst[0:NE, K_TRI:K_TRI + NE]
                parts = []
                for j, n in enumerate(tiles):
                    at_j = (n, NE * j, NE)
                    parts.append((at_j, mm(ncol[:, 0:1].to_broadcast([NE, n]), below, True, False)))
                    for i in range(j):
                        parts.append((at_j, mm(kst[:, K_ONE:K_ONE + n], key[:, i, :], False, False)))
                    parts.append((at_j, mm(kst[0:n, K_TRI:K_TRI + n], key[0:n, j, :], False, True)))
                parts.append(((P, 3 * NE, NE), mm(count, ident[0:NE, 0:NE])))
                parts.append(((P, 4 * NE, NE), mm(count, below)))
                small(parts)
                ada_turn(l, 10)
                if l == 0:
                    ada_tile(1, 0, 2)
                ada_turn(l, 11)
                operand()
                for c in range(C):
                    for half in range(2):
                        group(P, T, [(tokA[0:n, j, c * P:(c + 1) * P], pick[0:n, j, half * T:(half + 1) * T])
                                     for j, n in enumerate(tiles)])
                at[f"moe{l}"] = g.n
                if l == 0:
                    ada_turn(1, 0)
                xn = Tally(xe_ready)
                xn.n = NE * l

                def block4(s, n, blocks, src):
                    w = wring[:, s, :].rearrange("p (k n) -> p k n", n=n)
                    bank = pj[banks[0] % NBANK]
                    banks[0] += 1
                    pe.wait_ge(pj_evac, g.value(NBANK - 1))
                    for i, f in enumerate(blocks):
                        for k in range(4096 // n):
                            m = pe.matmul(bank[:, i * P:(i + 1) * P], w[:, k, f * P:(f + 1) * P], src[:, k, :],
                                          start=(k == 0), stop=(k == 4096 // n - 1))
                    m.then_inc(pj_done, 1)
                    g.add()

                def step(s3, up, par, turn=0):
                    if up:
                        pe.wait_ge(xe_ready, xn.add())
                        for s in (s3, s3 + 1):
                            loaded(s, turn=turn)
                            block4(s, 512, range(FB), xe[:, int(s3 > 0), :, :])
                    if par is not None:
                        loaded(s3 + 2, turn=turn)
                        pe.wait_ge(a_ready, an.add())
                        for d in range(2):
                            block4(s3 + 2, D, range(4 * d, 4 * d + 4), aT[:, par, :, :])

                step(0, True, None)
                step(3, True, 0)
                step(0, True, 1)
                with turns(pe, 6, {g: 8, an: 2, xn: 2}) as i:
                    step(3, True, 0, i * 16)
                    step(0, True, 1, i * 16)
                for s in range(SLOTS):
                    loads[s] += 16 * 5
                step(3, True, 0)
                step(0, False, 1)
                pe.wait_ge(pj_evac, g.n)
                at[f"moe{l}_main"] = g.n
                more_pe(l)
                small([((6, P * j, n), tr(sg[0:n, j, :], n)) for j, n in enumerate(tiles)])
                emptied()
                for i in range(4):
                    small([((P, 0, T), mm(ident[0:4, i:i + 1].to_broadcast([4, P]), lgT[0:4, :]))])
                for k in range(NK):
                    n = P if k < NK - 1 else LAST
                    for q in range(2):
                        small([((n, c * P, P), tr(yg[:, 4 * q + c, k * P:k * P + n])) for c in range(4)])
                if l == 0:
                    ada_tile(1, 1, 0)
                operand()
                for c in range(C):
                    group(P, T, [(yr[0:(P if k < NK - 1 else LAST), k, c * P:(c + 1) * P], put[0:(P if k < NK - 1 else LAST), k, :])
                                 for k in range(NK)])
                at[f"moe{l}_end"] = g.n

            def more_pe(l):
                m = more[l]
                pe.wait_ge(routed, l + 1)
                many = pe.value_load(starts[0:1, 3 * NE:3 * NE + 1], min_val=0, max_val=1)
                with pe.If(many):
                    x, p_, ev = Tally(m["x"]), Tally(m["piece"]), Tally(m["evac"])
                    with turns(pe, NE, {x: 2, p_: 32 * 24, ev: 24}):
                        for half in range(2):
                            pe.wait_ge(m["x"], x.add())
                            for rnd in range(12):
                                pe.wait_ge(m["piece"], p_.add(32))
                                if rnd < 4:
                                    for b_ in range(2):
                                        for k in range(C):
                                            i = pe.matmul(pj[b_][:, 0:P], piece[:, b_, k, :], xe[:, 0, k, :],
                                                          start=(k == 0), stop=(k == C - 1))
                                else:
                                    for k in range(FB):
                                        i = pe.matmul(pj[0][:, 0:P], piece[:, k // 2, k % 2, :], aT[:, 0, k, :],
                                                      start=(k == 0), stop=(k == FB - 1))
                                i.then_inc(m["done"], 1)
                                pe.wait_ge(m["evac"], ev.add())
                with pe.Else():
                    pe.nop()

            moe(0)
            ada_turn(1, 1)
            ada_tile(1, 2, 1)
            operand()

            def beside():
                ada_turn(1, 2)
                ada_tile(1, 3, 3)

            norm(yT, beside)
            ada_turn(1, 3)
            ada_tile(1, 4, 4)

            operand()
            for s in (5, 2, 0, 1):
                project(s, xT)
            at["kv"] = g.n
            ada_turn(1, 4)
            operand()
            for s in (3, 4):
                project(s, hT)
            at["q"] = g.n
            for src, ready in ((uT, at["kv"]), (cqT, at["q"])):
                pe.wait_ge(pj_evac, ready)
                for h in range(H):
                    small([((P, 0, T), mm(kst[:, K_ROT:K_ROT + P], src[:, h, :]))])
            ada_tile(1, 5, 5)
            ada_turn(1, 5)
            operand()
            for q in range(2):
                small([((NB, c * P, P), tr(cqT[:, 4 * q + c, TP:T])) for c in range(4)])
            operand()
            for c in range(2):
                small([((P, 0, 64), mm(kst[HD * c:HD * (c + 1), K_ONE:K_ONE + P], rs[HD * c:HD * (c + 1), 0:64]))])
            operand()
            small([((P, 0, 1), mm(kst[0:1, K_ONE:K_ONE + P], lams[0:1, 4:5]))])
            to_tokens(uT)
            at["k_tok"] = b.n
            to_tokens(zT)
            at["v2_tok"] = b.n

            at["spread"] = g.n
            at["cache_loads"] = list(loads)
            for s in range(SLOTS):
                loads[s] += 16 * sum(4 for j in range(len(LOADS)) if s in PAIRS[j % 3])

            def spread(s):
                for n in range(2):
                    group(P, 512, [(ident[0:NB, s:s + 1].to_broadcast([NB, P]), qtok[0:NB, n * 512:(n + 1) * 512])])
                at[f"spread{s}"] = g.n

            def values(s, k):
                slot, count = cache_slot("v", s, k)
                pe.wait_ge(slot_in[slot], at["cache_loads"][slot] + 16 * count)
                for n in range(2):
                    if k == 0:
                        pe.wait_ge(pj_evac, g.n + n + 1 - NBANK)
                    out = pj[(banks[0] + n) % NBANK][0:H, :]
                    for p in range(4):
                        m = pe.matmul(out, sW[:, s, 4 * k + p, :], wring[:, slot, p * D + n * 512:p * D + (n + 1) * 512],
                                      start=(k == 0 and p == 0), stop=(k == 1 and p == 3))
                    if k:
                        m.then_inc(pj_done, 1)
                if k:
                    g.add(2)
                    banks[0] += 2
                    at[f"values{s}"] = g.n
                else:
                    m.then_inc(values_used, 1)

            spread(0)
            for s in range(NB + 2):
                if s + 1 < NB:
                    spread(s + 1)
                if s >= 2:
                    operand()
                if 1 <= s <= NB:
                    operand()
                    small([((16, 0, P), tr(smx[:, 16 * (s - 1):16 * s]))])
                if s < NB:
                    for c in range(2):
                        small([((P, P * j, (j + 1) * P), mm(cqT[HD * c:HD * (c + 1), s, j * P:(j + 1) * P],
                                                            uT[HD * c:HD * (c + 1), s, 0:(j + 1) * P])) for j in range(2)])
                if s >= 2:
                    values(s - 2, 0)
                if 1 <= s <= NB:
                    if s < NB:
                        pe.wait_ge(tb_evac, b.value(2))
                    else:
                        emptied()
                    small([((P, 0, 16), mm(scol[0:16, 0:1].to_broadcast([16, P]), ident[0:16, 0:16]))])
                if s >= 2:
                    values(s - 2, 1)
                if s < NB:
                    for j in range(2):
                        operand()
                        small([((P, P * t, P), tr(pex[:, j, 0, t * P:(t + 1) * P])) for t in range(j + 1)])
                    turned = b.n
                if s == NB:
                    ada_tile(1, 6, 1)
                if s == NB + 1:
                    ada_tile(1, 7, 3)
                if s >= 2:
                    pe.wait_ge(pj_evac, at[f"values{s - 2}"])
                    small([((P, H * c, H), tr(osb[0:H, c * P:(c + 1) * P], H)) for c in range(C)])
                    at[f"rows{s - 2}"] = b.n
                if 1 <= s <= NB:
                    operand()
                    small([((P, 0, 16), mm(kst[:, K_ONE:K_ONE + P], smx[:, 16 * (s - 1):16 * s]))])
                if s < NB:
                    pe.wait_ge(tb_evac, turned)
                    for j in range(2):
                        small([((P, 0, P), mm(tokA[:, t, s * P:(s + 1) * P], pwT[:, j, t, :], t == 0, t == j))
                               for t in range(j + 1)])
            ada_turn(1, 6)
            ada_turn(1, 7)
            ada_tile(1, 8, 4)

            squares()
            for h in range(H):
                small([((P, 0, T), mm(kst[:, K_ONE:K_ONE + P], sqT[:, h, :]))])
            at["rms"] = b.n
            ada_turn(1, 8)
            operand()
            for s in (5, 1):
                project(s, hT)
            at["b_out"] = g.n
            ada_tile(1, 9, 3)
            operand()
            norm(yT, lambda: ada_turn(1, 9))
            ada_tile(1, 10, 4)
            moe(1)
            operand()
            norm(yT)
            operand()
            to_tokens(xT)
            at["y_tok"] = b.n
            at["end"] = g.n

        @block.sync
        def _(sp):
            free = [None] * SLOTS
            done = [0]

            def slot(s, n=512):
                return wring[:, s, :].rearrange("p (k n) -> p k n", n=n)

            def load(s, src, groups=None, n=512):
                if free[s]:
                    sp.wait_ge(*free[s])
                sp.dma_start(slot(s, n), src).then_inc(slot_in[s], 16)
                if groups is None:
                    user, done[0] = at["uses"].pop(0)
                    assert user == s
                else:
                    done[0] += groups
                free[s] = (pj_done, done[0])

            def ada(l, n, s):
                load(s, columns("ada_w", n, l))

            def columns(name, n, l=None):
                w = a[name] if l is None else a[name][l]
                return w.rearrange("(k p) n -> p k n", p=P)[:, :, n * 512:(n + 1) * 512]

            sp.dma_start(kst[:], a["consts"]).then_inc(consts_in, 16)
            sp.dma_start(crow[0:1, :], a["c_prompt"]).then_inc(rows_in, 16)
            sp.dma_start(crow[1:NR, :], a["c_sample"]).then_inc(rows_in, 16)
            sp.dma_start(vrow[V_LNG:V_LNG + 32, :], a["ln_g"].rearrange("l j (c p) -> (l j c) p", p=P)).then_inc(rows_in, 16)
            sp.dma_start(vrow[V_LNB:V_LNB + 32, :], a["ln_b"].rearrange("l j (c p) -> (l j c) p", p=P)).then_inc(rows_in, 16)
            sp.dma_start(vrow[V_AG:V_AG + 8, :], a["a_ln_g"].rearrange("l (c p) -> (l c) p", p=P)).then_inc(rows_in, 16)
            sp.dma_start(vrow[V_AB:V_AB + 8, :], a["a_ln_b"].rearrange("l (c p) -> (l c) p", p=P)).then_inc(rows_in, 16)
            sp.dma_start(vrow[V_SUB:V_SUB + 1, :], a["b_subln_g"]).then_inc(rows_in, 16)
            sp.dma_start(arow, a["ada_b"].rearrange("l (c p) -> (l c) p", p=P)).then_inc(rows_in, 16)
            sp.dma_start(tokB[:], a["x_prompt"][0].rearrange("(j p) d -> p j d", p=P)).then_inc(x_in, 16)
            sp.dma_start(tokA[0:NB, 2, :], a["x_sample"].rearrange("b t d -> (b t) d")).then_inc(x_in, 16)
            for n in range(5):
                ada(0, n, n)
            for n, s in enumerate((5, 0, 1, 2)):
                load(s, columns("a_w_in", n, 0))
            for n, s in ((5, 3), (6, 4), (7, 5)):
                ada(0, n, s)
            for n, s in enumerate((0, 1)):
                load(s, columns("a_w_out", n, 0))
            for n, s in ((8, 2), (9, 3), (10, 4), (11, 5)):
                ada(0, n, s)
            ada(1, 0, 2)

            def more_sp(l):
                m = more[l]
                sp.wait_ge(routed, l + 1)
                many = sp.value_load(starts[0:1, 3 * NE:3 * NE + 1], min_val=0, max_val=1)
                with sp.If(many):
                    sp.wait_ge(pj_evac, at[f"moe{l}_main"])
                    done = Tally(m["evac"])
                    w = [a[n][l].rearrange("e (k p) n -> e p k n", p=P) for n in ("moe_w_gate", "moe_w_up", "moe_w_down")]
                    with turns(sp, NE, {done: 24}) as e:
                        for rnd in [*range(12)] * 2:
                                for b_ in range(2):
                                    if rnd < 4:
                                        src = w[b_][bass.ds(e, 1), :, :, rnd * P:(rnd + 1) * P]
                                        dst = piece[:, b_, :, :]
                                    else:
                                        src = w[2][bass.ds(e, 1), :, 2 * b_:2 * b_ + 2, (rnd - 4) * P:(rnd - 3) * P]
                                        dst = piece[:, b_, 0:2, :]
                                    sp.wait_ge(m["evac"], done.value())
                                    sp.dma_start(dst, src.rearrange("a p k n -> p (a k) n")).then_inc(m["piece"], 16)
                                done.add()
                with sp.Else():
                    sp.nop()

            def moe_loads(l):
                gate = a["moe_w_gate"][l].rearrange("e (k p) n -> e p k n", p=P)
                up = a["moe_w_up"][l].rearrange("e (k p) n -> e p k n", p=P)
                down = a["moe_w_down"][l].rearrange("e (k p) n -> e p k n", p=P)

                def step(s, e):
                    if e < NE:
                        load(s, gate[e], 1)
                        load(s + 1, up[e], 1)
                    if e > 0:
                        load(s + 2, down[e - 1], 2, D)

                done[0] = at[f"moe{l}"]
                step(0, 0)
                step(3, 1)
                step(0, 2)
                first = at[f"moe{l}"] + 2
                with sp.Fori(0, 6) as i:
                    for k in range(2):
                        s = 3 - 3 * k
                        e = i * 2 + (3 + k)
                        for slot_, src, n, used in ((s, gate[bass.ds(e, 1)], 512, 1), (s + 1, up[bass.ds(e, 1)], 512, 2),
                                                    (s + 2, down[bass.ds(e - 1, 1)], D, 4)):
                            sp.wait_ge(pj_done, i * 8 + (first + 4 * k + used))
                            sp.dma_start(slot(slot_, n), src.rearrange("a p k n -> p (a k) n")).then_inc(slot_in[slot_], 16)
                last = first + 4 * 13
                done[0] = last + 4
                for k, s in ((-1, 3), (0, 0)):
                    for j, used in enumerate((1, 2, 4)):
                        free[s + j] = (pj_done, last + 4 * k + used)
                step(3, 15)
                step(0, 16)
                assert done[0] == at[f"moe{l}_main"]
                more_sp(l)
                done[0] = at[f"moe{l}_end"]

            moe_loads(0)
            for n, s in ((1, 0), (2, 1), (3, 3), (4, 4)):
                ada(1, n, s)
            for name, slots in (("kv_w_k", (5, 2)), ("kv_w_v", (0, 1))):
                for n, s in enumerate(slots):
                    load(s, columns(name, n))
            for n, s in enumerate((3, 4)):
                load(s, columns("b_w_q", n, 0))
            ada(1, 5, 5)

            keys = a["cache_k"].rearrange("g p h c d -> g p (h c d)")
            vals = a["cache_v"].rearrange("g p h e -> g p (h e)")

            def pages(cache, seq, k, s, sem_, value):
                with sp.Fori(0, 4) as i:
                    page = sp.value_load(ptab[0:1, bass.ds(seq * NPG + 4 * k + i, 1)], min_val=0, max_val=POOLN - 1)
                    sp.wait_ge(sem_, value)
                    sp.dma_start(wring[:, s, bass.ds(i * D, D)],
                                 cache[bass.ds(page, 1)].rearrange("a p n -> p (a n)")).then_inc(slot_in[s], 16)

            def used(kind, seq, k):
                if kind == "k":
                    return keys_used, 2 * seq + k + 1
                return (pj_done, at[f"values{seq}"]) if k else (values_used, seq + 1)

            sp.wait_ge(table_in, 16)
            for kind, seq in LOADS:
                for k in range(2):
                    s, _ = cache_slot(kind, seq, k)
                    pages(keys if kind == "k" else vals, seq, k, s, *free[s])
                    free[s] = used(kind, seq, k)
            for n, s in ((6, 1), (7, 3), (8, 4)):
                ada(1, n, s)
            for n, s in enumerate((5, 1)):
                load(s, columns("b_w_o", n, 0))
            for n, s in ((9, 3), (10, 4), (11, 2)):
                ada(1, n, s)
            assert not at["uses"]
            moe_loads(1)

            sp.wait_ge(tb_evac, at["y_tok"])
            sp.dma_start(o["y_prompt"][0].rearrange("(j p) d -> p j d", p=P), tokA[:, 0:2, :]).then_inc(stored["yp"], 16)
            sp.dma_start(o["y_sample"].rearrange("b t d -> (b t) d"), tokA[0:NB, 2, :]).then_inc(stored["ys"], 16)
            for n in stored:
                sp.wait_ge(stored[n], 16)

        @block.gpsimd
        def _(pool):
            pool.dma_start(ptab[:], a["page_table"].rearrange("(o b) n -> o (b n)", o=1)).then_inc(table_in, 16)
            pool.dma_start(ws[:], a["a_w_s"][0].rearrange("g i j -> i g j")).then_inc(small_in, 16)
            pool.dma_start(bsb[:], a["a_b_s"].to_broadcast([P, 8, P])).then_inc(small_in, 16)
            pool.dma_start(ws00[:], a["a_w_s"][0:1, :, 0, 0].to_broadcast([P, 8]),
                           allow_slow_non_contiguous=True).then_inc(small_in, 16)
            pool.dma_start(rw[:], a["router_w"].rearrange("(k p) e -> p k e", p=P)).then_inc(small_in, 16)
            pool.dma_start(rbias[:], a["router_bias"].rearrange("(o e) -> o e", o=1).to_broadcast([P, NE])).then_inc(small_in, 16)
            for n, name in enumerate(("b_lam_q1", "b_lam_k1", "b_lam_q2", "b_lam_k2")):
                pool.dma_start(lamv[:, n, :], a[name]).then_inc(small_in, 16)
            pool.memset(epsc[:], EPS).then_inc(pool_own, 1)
            kint = stack[:, 0, 0, :].bitcast(I32)
            pool.iota(kint, pattern=[[-1, NE]], base=NE, channel_multiplier=0).then_inc(pool_own, 1)
            pool.wait_ge(pool_own, 2)
            pool.tensor_copy(kidx[:], kint).then_inc(pool_own, 1)
            pool.wait_ge(small_in, 16 * 9)
            pool.affine_select(out=ws[:], in_=ws[:], compare_op=ALU.is_ge, fill=0.0, base=0,
                               pattern=[[0, 8], [-1, P]], channel_multiplier=1).then_inc(ws_masked, 1)
            pool.wait_ge(tb_evac, at["v_tok"])
            pool.dma_start(o["chunk_v_sample"].rearrange("l b t d -> (l b t) d"), tokA[0:NB, 2, :]).then_inc(stored["cv"], 16)

            def clear(l):
                pool.wait_ge(tb_evac, at[f"router{l}"])
                pool.memset(reg2[:], 0.0).then_inc(yg_clear, 1)

            clear(0)
            pool.wait_ge(tb_evac, at["turn1_1"])
            pool.dma_start(flatB[:, 0:2 * T], a["rotary"].rearrange("p a t -> p (a t)")).then_inc(rotary_in, 16)
            pool.wait_ge(tb_evac, at["k_tok"])
            pool.dma_start(o["k_prompt"][0].rearrange("(j p) h c d -> p j (h c d)", p=P), tokB[:]).then_inc(stored["kp"], 16)
            pool.dma_start(o["k_sample"].rearrange("b t h c d -> (b t) (h c d)"), ksm[0:NB, :]).then_inc(stored["ks"], 16)
            pool.wait_ge(tb_evac, at["v2_tok"])
            pool.dma_start(o["v_prompt"][0].rearrange("(j p) h e -> p j (h e)", p=P), tokA[:, 0:2, :]).then_inc(stored["vp"], 16)
            pool.dma_start(o["v_sample"].rearrange("b t h e -> (b t) (h e)"), tokA[0:NB, 2, :]).then_inc(stored["vs"], 16)
            clear(1)

        @block.scalar
        def _(act):
            g, inp, an = Tally(pj_evac), Tally(act_in), Tally(a_ready)
            banks = [0]

            def evac(dst, func=ACT.Copy, rows=P, n=T):
                bank = pj[banks[0] % NBANK]
                banks[0] += 1
                act.wait_ge(pj_done, g.add())
                act.activation(dst, bank[0:rows, 0:n] if n < 512 or rows < P else bank[:, :].rearrange("p (f n) -> p f n", n=P), func).then_inc(pj_evac, 1)

            def answer(dst, src, func, **kw):
                act.wait_ge(act_in, inp.add())
                act.activation(dst, src, func, **kw).then_inc(act_out, 1)

            sd = Tally(st_done)

            def square(src):
                act.wait_ge(act_in, inp.add())
                act.activation(sqT[:], src, ACT.Square).then_inc(sq_ready, 1)

            def norm(src, beside=lambda: None):
                square(src)
                beside()
                act.wait_ge(st_done, sd.add(2))
                act.activation(rs[:], st[1][:, :], ACT.Sqrt, bias=epsc[:, 0:1], scale=1.0 / D).then_inc(act_out, 1)

            def rows(l, n):
                if l or n >= 2:
                    act.wait_ge(tb_done, at["turn%d_%d" % before(l, n)])
                evac(mrow(l, n), rows=NR, n=512)

            act.wait_ge(rows_in, 16 * 8)
            act.activation(crow, crow, ACT.Silu).then_inc(c_silu, 1)
            for n in range(5):
                rows(0, n)
            for f in range(2 * C):
                evac(abT[:, f, :], ACT.Gelu_apprx_tanh)
            act.wait_ge(pool_own, 1)
            norm(zT, lambda: rows(0, 5))
            rows(0, 6)
            rows(0, 7)
            for f in range(C):
                evac(yT[:, f, :])
            rows(0, 8)
            norm(yT[:], lambda: rows(0, 9))
            rows(0, 10)

            def moe(l):
                answer(score[:], lg[:], ACT.Exp)
                rows(l, 11)
                if l == 0:
                    rows(1, 0)
                for c in range(C):
                    for half in range(2):
                        evac(xg[:, c, half * T:(half + 1) * T])
                act.wait_ge(routed, l + 1)
                act.wait_ge(yg_clear, l + 1)

                def up(par, wait):
                    evac(aT[:, par, :, :], ACT.Silu, n=512)
                    if wait:
                        act.wait_ge(a_ready, an.add())
                    evac(upT, n=512)

                def down(e):
                    first = act.value_load(starts[0:1, bass.ds(e, 1)], min_val=0, max_val=SLOT_N)
                    for d in range(2):
                        evac(yg[:, 4 * d:4 * d + 4, bass.ds(first, P)], n=512)

                up(0, False)
                up(1, True)
                down(0)
                up(0, True)
                down(1)
                with turns(act, 6, {g: 8, an: 2}) as i:
                    up(1, True)
                    down(i * 2 + 2)
                    up(0, True)
                    down(i * 2 + 3)
                up(1, True)
                down(14)
                act.wait_ge(pj_evac, g.value())
                down(15)
                an.add()
                m = more[l]
                many = act.value_load(starts[0:1, 3 * NE:3 * NE + 1], min_val=0, max_val=1)
                with act.If(many):
                    done = Tally(m["done"])
                    with turns(act, NE, {done: 24}):
                        for half in range(2):
                            for rnd in range(4):
                                act.wait_ge(m["done"], done.add())
                                act.activation(aT[:, 0, rnd, :], pj[0][:, 0:P], ACT.Silu).then_inc(m["silu"], 1)
                            done.add(8)
                with act.Else():
                    act.nop()
                if l == 0:
                    rows(1, 1)
                for c in range(C):
                    evac(yT[:, c, :])

            moe(0)
            rows(1, 2)
            norm(yT[:], lambda: rows(1, 3))
            rows(1, 4)
            for f in range(2 * C):
                evac(abT[:, f, :])
            for f in range(C):
                evac(cqT[:, f, :])
            rows(1, 5)
            answer(lams[0:1, 2:4], lams[0:1, 0:2], ACT.Exp)

            def spread(s):
                if s >= 2:
                    act.wait_ge(keys_used, 2 * (s - 1))
                for n in range(2):
                    evac(qbc[:, s % 2, n * 512:(n + 1) * 512].rearrange("p (f n) -> p f n", n=P), n=512)

            act.wait_ge(stored["ks"], 16)
            spread(0)
            for s in range(NB + 2):
                if s + 1 < NB:
                    spread(s + 1)
                if s < NB:
                    for j in range(2):
                        n = (j + 1) * P
                        act.wait_ge(act_in, inp.add())
                        for c in range(2):
                            act.activation(pex[:, j, c, 0:n], psc[:, j, c, 0:n], ACT.Exp, bias=pst[:, j, c:c + 1],
                                           accum_out=pst[:, j, 2 + c:3 + c]).then_inc(act_out, 1)
                if 1 <= s <= NB:
                    answer(sS[:, s - 1], sS[:, s - 1], ACT.Exp)
                if s >= 2:
                    if s >= 3:
                        act.wait_ge(tb_done, at[f"rows{s - 3}"])
                    for n in range(2):
                        evac(osb[0:H, n * 512:(n + 1) * 512], rows=H, n=512)
                if s >= NB:
                    rows(1, 6 + s - NB)
            rows(1, 8)
            square(hT[:])
            act.wait_ge(tb_evac, at["rms"])
            act.activation(yT[:], yT[:], ACT.Sqrt).then_inc(act_out, 1)
            for f in range(C):
                evac(yT[:, f, :])
            rows(1, 9)
            norm(yT[:])
            rows(1, 10)
            moe(1)
            norm(yT[:])
            assert g.n == at["end"]

        @block.vector
        def _(dve):
            own, tbe, op, inp, out = Tally(dve_own), Tally(tb_evac), Tally(op_ready), Tally(act_in), Tally(act_out)
            an, gp = Tally(a_ready), Tally(pj_evac)
            sd = Tally(st_done)

            def link(ins):
                ins.then_inc(dve_own, 1)
                dve.wait_ge(dve_own, own.add())

            def last_empty():
                dve.wait_ge(tb_evac, tbe.value())

            def batch():
                dve.wait_ge(tb_done, tbe.value() + 1)
                return tb[tbe.n % 2]

            def empty(ins):
                ins.then_inc(tb_evac, 1)
                tbe.add()

            def ready(ins):
                ins.then_inc(op_ready, 1)
                dve.wait_ge(op_ready, op.add())

            def ask(ins):
                ins.then_inc(act_in, 1)
                inp.add()

            def answered(n=1):
                dve.wait_ge(act_out, out.add(n))

            def mod_rows(l, n):
                bank = batch()[:, 0:64].rearrange("p (c r) -> p c r", r=16)[:, :, 0:NR]
                plus = 1.0 if (n // 2) % 3 else 0.0
                bias = adabT[:, 48 * l + 4 * n:48 * l + 4 * n + 4].unsqueeze(2).to_broadcast([P, 4, NR])
                empty(dve.scalar_tensor_tensor(mT[:, 4 * n:4 * n + 4, :], bank, plus, bias, ALU.add, ALU.add))

            def modulate(sh, sc):
                for c in range(C):
                    dve.tensor_scalar(hT[:, c, 0:TP], xT[:, c, 0:TP], mT[:, sc + c, 0:1], mT[:, sh + c, 0:1],
                                      ALU.mult, ALU.add)
                link(dve.tensor_tensor(hT[:, :, TP:T], xT[:, :, TP:T], mT[:, sc:sc + C, 1:NR], ALU.mult))
                ready(dve.tensor_tensor(hT[:, :, TP:T], hT[:, :, TP:T], mT[:, sh:sh + C, 1:NR], ALU.add))

            def residual(gate, groups):
                link(dve.tensor_scalar(xT[:], xT[:], ALPHA, None, ALU.mult))
                if groups:
                    dve.wait_ge(pj_evac, groups)
                for c in range(C):
                    dve.scalar_tensor_tensor(yT[:, c, 0:TP], yT[:, c, 0:TP], mT[:, gate + c, 0:1], xT[:, c, 0:TP],
                                             ALU.mult, ALU.add)
                link(dve.tensor_tensor(yT[:, :, TP:T], yT[:, :, TP:T], mT[:, gate:gate + C, 1:NR], ALU.mult))
                ready(dve.tensor_tensor(yT[:, :, TP:T], yT[:, :, TP:T], xT[:, :, TP:T], ALU.add))

            def across(x):
                return x.unsqueeze(1).to_broadcast([P, C, T])

            def norm(src, dst, g0, b0, beside=lambda: None):
                dve.wait_ge(st_done, sd.add())
                ask(dve.scalar_tensor_tensor(src, across(st[0][:, :]), -1.0 / D, src, ALU.mult, ALU.add))
                sd.add()
                beside()
                answered()
                link(dve.reciprocal(rs[:], rs[:]))
                link(dve.tensor_tensor(src, src, across(rs[:]), ALU.mult))
                for c in range(C):
                    i = dve.tensor_scalar(dst[:, c, :], src[:, c, :], vT[:, g0 + c:g0 + c + 1], vT[:, b0 + c:b0 + c + 1],
                                          ALU.mult, ALU.add)
                return i

            def tokens(sample, prompt):
                for q in range(2):
                    empty(dve.tensor_copy(sample[0:NB, q * 512:(q + 1) * 512], batch()[0:NB, :]))
                for j in range(2):
                    for q in range(2):
                        empty(dve.tensor_copy(prompt[:, j, q * 512:(q + 1) * 512], batch()[:, :]))

            dve.memset(pos[:], 0.0)
            link(dve.memset(lg[:], 0.0))
            bank = batch()
            link(dve.tensor_copy(vT[:], bank[:, 0:V_N]))
            empty(dve.tensor_copy(adabT[:], bank[:, P:P + 96]))
            empty(dve.tensor_copy(cT[:], batch()[:, 0:128].rearrange("p (c r) -> p c r", r=16)[:, :, 0:NR]))
            for j in range(2):
                for q in range(2):
                    empty(dve.tensor_copy(xT[:, 4 * q:4 * q + 4, j * P:(j + 1) * P],
                                          batch()[:, :].rearrange("p (c t) -> p c t", c=4)))
            empty(dve.tensor_copy(xT[:, :, TP:T], batch()[:, 0:128].rearrange("p (c r) -> p c r", r=16)[:, :, 0:NB]))
            for n in range(4):
                mod_rows(0, n)
            for q in range(2):
                empty(dve.tensor_copy(wsT[:, 4 * q:4 * q + 4, :], batch()[:, :].rearrange("p (c t) -> p c t", c=4)))
            last_empty()
            modulate(0, 8)

            mod_rows(0, 4)
            ready(norm(zT, zT, V_AG, V_AB))
            mod_rows(0, 5)
            tokens(tokA[:, 2, :], tokA)
            dve.wait_ge(small_in, 16 * 9)
            for q in range(4):
                both = sqT[:, 2 * (q % 2):2 * (q % 2) + 2, 0:TP]
                mix = both.rearrange("p g (j i) -> p g j i", j=2)
                empty(dve.tensor_tensor(mix, batch()[:, :].rearrange("p (g j i) -> p g j i", g=2, j=2),
                                        bsb[:, 2 * q:2 * q + 2, :].unsqueeze(2).to_broadcast([P, 2, 2, P]), ALU.add))
                last_empty()
                dve.tensor_tensor(uT[:, 2 * q:2 * q + 2, 0:TP], uT[:, 2 * q:2 * q + 2, 0:TP], both, ALU.mult)
            mix = rs[:, 0:64].rearrange("p (c b) -> p c b", b=NB)
            link(dve.tensor_tensor(mix, zT[:, :, TP:T], ws00[:].unsqueeze(2).to_broadcast([P, C, NB]), ALU.mult))
            link(dve.tensor_tensor(mix, mix, bsb[:, :, 0:1].to_broadcast([P, C, NB]), ALU.add))
            ready(dve.tensor_tensor(uT[:, :, TP:T], uT[:, :, TP:T], mix, ALU.mult))
            mod_rows(0, 6)
            mod_rows(0, 7)
            residual(16, at["a_out"])
            link(norm(yT[:], xT, V_LNG, V_LNB, lambda: mod_rows(0, 8)))
            mod_rows(0, 9)
            last_empty()

            def reduce(dst, src, op):
                link(dve.tensor_reduce(dst, src, AX.X, op))

            def first_max(dst, src, keys, shape):
                reduce(one[:], src, ALU.max)
                link(dve.tensor_tensor(dst, src, one[:].to_broadcast(shape), ALU.is_equal))
                link(dve.tensor_tensor(dst, dst, keys, ALU.mult))
                reduce(one[:], dst, ALU.max)
                link(dve.tensor_tensor(dst, dst, one[:].to_broadcast(shape), ALU.is_equal))

            dve.wait_ge(pool_own, 3)

            def more_dve(l):
                m = more[l]
                many = dve.value_load(starts[0:1, 3 * NE:3 * NE + 1], min_val=0, max_val=1)
                with dve.If(many):
                    done, silu, ev, x, ms = (Tally(m[n]) for n in ("done", "silu", "evac", "x", "mask"))
                    with turns(dve, NE, {done: 24, silu: 8, ev: 24, x: 2, ms: 18}) as e:
                        for half in range(2):
                            first = dve.value_load(starts[0:1, bass.ds(e + NE * (half + 1), 1)], min_val=0, max_val=SLOT_N)
                            dve.tensor_scalar(upT[:, 0, :], kst[:, K_IOTA:K_IOTA + P], lim[:, half, bass.ds(e, 1)], None,
                                              ALU.is_lt).then_inc(m["mask"], 1)
                            dve.wait_ge(m["mask"], ms.add())
                            dve.tensor_copy(xe[:, 0, :, :], xg[:, :, bass.ds(first, P)]).then_inc(m["x"], 1)
                            x.add()
                            for rnd in range(12):
                                dve.wait_ge(m["done"], done.add())
                                if rnd < 4:
                                    dve.wait_ge(m["silu"], silu.add())
                                    i = dve.tensor_tensor(aT[:, 0, rnd, :], aT[:, 0, rnd, :], pj[1][:, 0:P], ALU.mult)
                                else:
                                    dve.tensor_tensor(upT[:, 1, :], pj[0][:, 0:P], upT[:, 0, :], ALU.mult).then_inc(m["mask"], 1)
                                    dve.wait_ge(m["mask"], ms.add())
                                    row = yg[:, rnd - 4:rnd - 3, bass.ds(first, P)]
                                    i = dve.tensor_tensor(row, row, upT[:, 1:2, :], ALU.add)
                                i.then_inc(m["evac"], 1)
                                dve.wait_ge(m["evac"], ev.add())
                with dve.Else():
                    dve.nop()

            def moe(l):
                modulate(24, 32)
                empty(dve.tensor_copy(lgT[:], batch()[0:NE, 0:T]))
                bank = batch()[:, 0:3 * NE].rearrange("p (j e) -> p j e", e=NE)
                dve.tensor_copy(lg[:, 0:2, :], bank[:, 0:2, :])
                empty(dve.tensor_copy(lg[0:NB, 2, :], bank[0:NB, 2, :]))
                last_empty()
                full = [P, 3, NE]
                reduce(one[:], lg[:], ALU.max)
                ask(dve.tensor_tensor(lg[:], lg[:], one[:].to_broadcast(full), ALU.subtract))
                answered()
                reduce(one[:], score[:], ALU.add)
                link(dve.reciprocal(one[:], one[:]))
                link(dve.tensor_tensor(score[:], score[:], one[:].to_broadcast(full), ALU.mult))
                link(dve.tensor_tensor(sel[:], score[:], rbias[:].unsqueeze(1).to_broadcast(full), ALU.add))
                s4 = sel[:].rearrange("p j (g e) -> p j g e", e=EG)
                dve.tensor_tensor(pair[0][:], s4[:, :, :, 0], s4[:, :, :, 1], ALU.max)
                dve.tensor_tensor(pair[1][:], s4[:, :, :, 0], s4[:, :, :, 1], ALU.min)
                dve.tensor_tensor(pair[2][:], s4[:, :, :, 2], s4[:, :, :, 3], ALU.max)
                link(dve.tensor_tensor(pair[3][:], s4[:, :, :, 2], s4[:, :, :, 3], ALU.min))
                link(dve.tensor_tensor(pair[1][:], pair[1][:], pair[3][:], ALU.max))
                dve.tensor_tensor(pair[3][:], pair[0][:], pair[2][:], ALU.min)
                link(dve.tensor_tensor(pair[0][:], pair[0][:], pair[2][:], ALU.max))
                link(dve.tensor_tensor(pair[1][:], pair[1][:], pair[3][:], ALU.max))
                link(dve.tensor_tensor(pair[0][:], pair[0][:], pair[1][:], ALU.add))
                first_max(pair[2][:], pair[0][:], kidx[:, 12:16].unsqueeze(1).to_broadcast([P, 3, EG]), [P, 3, EG])
                link(dve.tensor_scalar(pair[2][:], pair[2][:], -NEG, NEG, ALU.mult, ALU.add))
                link(dve.tensor_tensor(s4, s4, pair[2][:].unsqueeze(3).to_broadcast([P, 3, EG, EG]), ALU.add))
                keys = kidx[:].unsqueeze(1).to_broadcast(full)
                first_max(top[0][:], sel[:], keys, full)
                link(dve.scalar_tensor_tensor(sel[:], top[0][:], 2 * NEG, sel[:], ALU.mult, ALU.add))
                first_max(top[1][:], sel[:], keys, full)
                ready(dve.tensor_tensor(key[:], top[0][:], top[1][:], ALU.add))
                for n in (("cv",), ("vp", "vs"))[l]:
                    dve.wait_ge(stored[n], 16)
                tokens(tokA[:, 2, :], tokA)
                empty(dve.tensor_copy(ncol[:], batch()[0:NE, 0:1]))
                link(dve.tensor_tensor(score[:], score[:], key[:], ALU.mult))
                reduce(one[:], score[:], ALU.add)
                link(dve.reciprocal(one[:], one[:]))
                link(dve.tensor_tensor(score[:], score[:], one[:].to_broadcast(full), ALU.mult))
                bank = batch()
                dve.tensor_copy(pos[:, 0:2, :], bank[:, 0:2 * NE].rearrange("p (j e) -> p j e", e=NE))
                dve.tensor_copy(pos[0:NB, 2, :], bank[0:NB, 2 * NE:3 * NE])
                empty(dve.tensor_copy(nrow[:], bank[:, 3 * NE:5 * NE]))
                last_empty()
                for i in range(2):
                    dve.tensor_tensor(stack[:, :, i, :], top[i][:], pos[:], ALU.mult)
                    link(dve.tensor_tensor(stack[:, :, 2 + i, :], top[i][:], score[:], ALU.mult))
                reduce(sg[:, :, 0:4].unsqueeze(3), stack[:], ALU.add)
                link(dve.tensor_scalar(sg[:, :, 4:6], sg[:, :, 0:2], -float(T), None, ALU.add))
                for j in range(3):
                    for half in range(2):
                        at_h = pick[:, j, half * T:(half + 1) * T]
                        s0 = 4 * half
                        iota = kst[:, K_IOTA:K_IOTA + T]
                        link(dve.tensor_scalar(at_h, iota, sg[:, j, s0:s0 + 1], None, ALU.is_equal))
                        i = dve.scalar_tensor_tensor(at_h, iota, sg[:, j, s0 + 1:s0 + 2], at_h, ALU.is_equal, ALU.add)
                ready(i)
                mod_rows(l, 10)
                mod_rows(l, 11)
                dve.tensor_copy(startf[:, 0:NE], nrow[0:1, NE:2 * NE])
                for k in range(2):
                    dve.tensor_scalar(startf[:, NE * (k + 1):NE * (k + 2)], nrow[0:1, NE:2 * NE], float(SPAN * (k + 1)),
                                      float(SLOT_N), ALU.add, ALU.min)
                    dve.tensor_scalar(lim[:, k, :], nrow[:, 0:NE], -float(SPAN * (k + 1)), None, ALU.add)
                reduce(startf[:, 3 * NE:3 * NE + 1], nrow[0:1, 0:NE], ALU.max)
                link(dve.tensor_scalar(startf[:, 3 * NE:3 * NE + 1], startf[:, 3 * NE:3 * NE + 1], float(SPAN), None, ALU.is_gt))
                dve.tensor_copy(starts[:], startf[:]).then_inc(routed, 1)
                dve.wait_ge(routed, l + 1)
                link(dve.memset(xg[:, :, SLOT_N:PACK], 0.0))
                dve.wait_ge(pj_evac, at[f"moe{l}"])
                gp.n = at[f"moe{l}"]
                xn = Tally(xe_ready)
                xn.n = NE * l

                def gather(par, e):
                    first = dve.value_load(starts[0:1, bass.ds(e, 1)], min_val=0, max_val=SLOT_N)
                    dve.tensor_copy(xe[:, par, :, :], xg[:, :, bass.ds(first, P)]).then_inc(xe_ready, 1)
                    xn.add()

                def gated(par, groups):
                    dve.wait_ge(pj_evac, gp.add(groups))
                    dve.tensor_tensor(aT[:, par, :, :], aT[:, par, :, :], upT, ALU.mult).then_inc(a_ready, 1)
                    an.add()

                gather(0, 0)
                gather(1, 1)
                if l == 0:
                    mod_rows(1, 0)
                gated(0, 2)
                gather(0, 2)
                gated(1, 2)
                with turns(dve, 6, {gp: 8, an: 2, xn: 2}) as i:
                    gather(1, i * 2 + 3)
                    gated(0, 4)
                    gather(0, i * 2 + 4)
                    gated(1, 4)
                gather(1, 15)
                gated(0, 4)
                gated(1, 4)
                dve.wait_ge(pj_evac, gp.add(4))
                assert gp.n == at[f"moe{l}_main"]
                more_dve(l)
                empty(dve.tensor_copy(lgT[0:6, :], batch()[0:6, 0:T]))
                for i in range(4):
                    empty(dve.tensor_copy(sgB[:, i, :], batch()[:, 0:T]))
                for k in range(NK):
                    n = P if k < NK - 1 else LAST
                    for q in range(2):
                        empty(dve.tensor_copy(yr[0:n, k, q * 512:(q + 1) * 512], batch()[0:n, :]))
                last_empty()
                for k in range(NK):
                    mine = kst[:, K_PART + k:K_PART + k + 1]
                    dve.scalar_tensor_tensor(put[:, k, :], sgB[:, 0, :], mine, sgB[:, 2, :], ALU.is_equal, ALU.mult)
                    link(dve.scalar_tensor_tensor(rs[:], sgB[:, 1, :], mine, sgB[:, 3, :], ALU.is_equal, ALU.mult))
                    i = dve.tensor_tensor(put[:, k, :], put[:, k, :], rs[:], ALU.add)
                    if k < NK - 1:
                        link(i)
                ready(i)
                if l == 0:
                    mod_rows(1, 1)
                residual(40, at[f"moe{l}_end"])

            moe(0)
            ready(norm(yT[:], xT, V_LNG + 8, V_LNB + 8, lambda: mod_rows(1, 2)))

            mod_rows(1, 3)
            last_empty()
            modulate(0, 8)
            mod_rows(1, 4)
            dve.wait_ge(rotary_in, 16)
            for x in (uT, cqT):
                for h in range(H):
                    turned = sqT[:, h, :]
                    empty(dve.tensor_tensor(turned, batch()[:, 0:T], sin, ALU.mult))
                last_empty()
                link(dve.tensor_tensor(x, x, across(cos), ALU.mult))
                i = dve.tensor_tensor(x, x, sqT[:], ALU.add)
                if x is uT:
                    link(i)
            ready(i)
            mod_rows(1, 5)
            for q in range(2):
                empty(dve.tensor_scalar(qtok[0:NB, q * 512:(q + 1) * 512], batch()[0:NB, :], HD ** -0.5, None, ALU.mult))
            ready(dve.tensor_tensor(rs[:, 0:64].rearrange("p (h b) -> p h b", b=NB), cqT[:, :, TP:T], uT[:, :, TP:T], ALU.mult))
            for c in range(2):
                empty(dve.tensor_scalar(snew.rearrange("p b (h c) -> p c h b", c=2)[:, c],
                                        batch()[:, 0:64].rearrange("p (h b) -> p h b", b=NB), HD ** -0.5, None, ALU.mult))
            lv = lamv.rearrange("o (a b) d -> o a b d", b=2)
            link(dve.tensor_tensor(lv[:, :, 0, :], lv[:, :, 0, :], lv[:, :, 1, :], ALU.mult))
            ask(dve.tensor_reduce(lams[0:1, 0:2].unsqueeze(2), lv[:, :, 0, :], AX.X, ALU.add))
            answered()
            link(dve.tensor_tensor(lams[0:1, 4:5], lams[0:1, 3:4], lams[0:1, 2:3], ALU.subtract))
            ready(dve.tensor_scalar(lams[0:1, 4:5], lams[0:1, 4:5], -LAM_INIT, None, ALU.add))
            empty(dve.tensor_copy(nlam[:], batch()[:, 0:1]))
            link(dve.tensor_scalar(subg[:], vT[:, V_SUB:V_SUB + 1], 1.0 - LAM_INIT, None, ALU.mult))
            tokens(ksm, tokB)
            dve.wait_ge(stored["cv"], 16)
            tokens(tokA[:, 2, :], tokA)
            dve.wait_ge(stored["kp"], 16)

            dve.tensor_copy(sS[:, :, NPG, :], snew)

            def scores(s, k, q):
                slot, count = cache_slot("k", s, k)
                if q == 0:
                    if k == 0:
                        dve.wait_ge(pj_evac, at[f"spread{s}"])
                    dve.wait_ge(slot_in[slot], at["cache_loads"][slot] + 16 * count)
                link(dve.tensor_tensor(prod.rearrange("p (g n) -> p g n", g=2),
                                       wring[:, slot, q * 2 * D:(q + 1) * 2 * D].rearrange("p (g n) -> p g n", g=2),
                                       qbc[:, s % 2:s % 2 + 1, :].to_broadcast([P, 2, D]), ALU.mult))
                g0 = 4 * k + 2 * q
                i = dve.tensor_reduce(sS[:, s, g0:g0 + 2, :].rearrange("p g x -> p (g x)").unsqueeze(2),
                                      prod.rearrange("p (x d) -> p x d", d=HD), AX.X, ALU.add)
                if q == 0:
                    link(i)
                else:
                    i.then_inc(keys_used, 1)
                    dve.wait_ge(keys_used, 2 * s + k + 1)

            for s in range(NB + 2):
                m = s - 1
                soft = 0 <= m < NB
                if soft:
                    mine = smx[:, 16 * m:16 * m + 16]
                    wide = mine.unsqueeze(1).to_broadcast([P, NPG + 1, 16])
                if s < NB:
                    scores(s, 0, 0)
                if soft:
                    empty(dve.tensor_reduce(scol[0:16, :], batch()[0:16, 0:P], AX.X, ALU.max))
                if s < NB:
                    for c in range(2):
                        bank = batch()
                        for j in range(2):
                            n = (j + 1) * P
                            i = dve.scalar_tensor_tensor(psc[:, j, c, 0:n], bank[:, P * j:P * j + n], HD ** -0.5,
                                                         kst[:, K_MASK + (1 - j) * P:K_MASK + 2 * P], ALU.mult, ALU.add)
                        empty(i)
                    last_empty()
                    for j in range(2):
                        n = (j + 1) * P
                        ask(dve.tensor_reduce(pst[:, j, 0:2].unsqueeze(2), psc[:, j, :, 0:n], AX.X, ALU.max, negate=True))
                    scores(s, 0, 1)
                if soft:
                    empty(dve.tensor_copy(mine, batch()[:, 0:16]))
                    last_empty()
                    ask(dve.tensor_tensor(sS[:, m], sS[:, m], wide, ALU.subtract))
                if s < NB:
                    for j in range(2):
                        n = (j + 1) * P
                        answered(2)
                        link(dve.reciprocal(pst[:, j, 4:6], pst[:, j, 2:4]))
                        dve.tensor_scalar(psc[:, j, 0, 0:n], pex[:, j, 0, 0:n], pst[:, j, 4:5], None, ALU.mult)
                        link(dve.tensor_scalar(pst[:, j, 5:6], pst[:, j, 5:6], nlam[:, 0:1], None, ALU.mult))
                        ready(dve.scalar_tensor_tensor(pex[:, j, 0, 0:n], pex[:, j, 1, 0:n], pst[:, j, 5:6],
                                                       psc[:, j, 0, 0:n], ALU.mult, ALU.add))
                    scores(s, 1, 0)
                if soft:
                    answered()
                if s < NB:
                    for j in range(2):
                        empty(dve.tensor_copy(pwT[:, j, 0:j + 1, :],
                                              batch()[:, 0:(j + 1) * P].rearrange("p (t q) -> p t q", q=P)))
                if s >= 2:
                    empty(dve.tensor_copy(hT[:, :, TP + s - 2:TP + s - 1],
                                          batch()[:, 0:(H + 1) * (H - 1) + 1:H + 1].unsqueeze(2)))
                if soft:
                    ready(dve.tensor_reduce(mine.unsqueeze(2), sS[:, m, 0:NPG, :].rearrange("p g x -> p x g"), AX.X, ALU.add))
                if s < NB:
                    scores(s, 1, 1)
                if soft:
                    empty(dve.tensor_tensor(mine, batch()[:, 0:16], sS[:, m, NPG, :], ALU.add))
                    last_empty()
                    link(dve.reciprocal(mine, mine))
                    odd = mine.rearrange("p (x c) -> p x c", c=2)[:, :, 1:2]
                    link(dve.tensor_scalar(odd, odd, nlam[:, 0:1], None, ALU.mult))
                    link(dve.tensor_tensor(sS[:, m], sS[:, m], wide, ALU.mult))
                    e4 = sS[:, m].rearrange("p g (h c) -> p g h c", c=2)
                    dve.tensor_tensor(sW[:, m], e4[:, 0:NPG, :, 0], e4[:, 0:NPG, :, 1], ALU.add)
                    ready(dve.tensor_tensor(wnew[:, m, :], e4[:, NPG, :, 0], e4[:, NPG, :, 1], ALU.add))
                if s < NB:
                    for j in range(2):
                        empty(dve.tensor_copy(hT[:, s, j * P:(j + 1) * P], batch()[:, 0:P]))
                    ready(dve.tensor_reduce(smx[:, 16 * s:16 * s + 16].unsqueeze(2),
                                            sS[:, s].rearrange("p g x -> p x g"), AX.X, ALU.max))
            mod_rows(1, 6)
            mod_rows(1, 7)
            mix = rs[:, 0:64].rearrange("p (h b) -> p h b", b=NB)
            link(dve.tensor_tensor(mix, zT[:, :, TP:T], wnew.rearrange("p b h -> p h b"), ALU.mult))
            ask(dve.tensor_tensor(hT[:, :, TP:T], hT[:, :, TP:T], mix, ALU.add))
            for h in range(H):
                empty(dve.tensor_scalar(yT[:, h, :], batch()[:, 0:T], 1.0 / P, EPS, ALU.mult, ALU.add))
            mod_rows(1, 8)
            answered()
            link(dve.reciprocal(yT[:], yT[:]))
            link(dve.tensor_tensor(hT[:], hT[:], yT[:], ALU.mult))
            ready(dve.tensor_scalar(hT[:], hT[:], subg[:, 0:1], None, ALU.mult))
            residual(16, at["b_out"])
            link(norm(yT[:], xT, V_LNG + 16, V_LNB + 16, lambda: mod_rows(1, 9)))
            last_empty()
            moe(1)
            ready(norm(yT[:], xT, V_LNG + 24, V_LNB + 24))
            dve.wait_ge(stored["vp"], 16)
            dve.wait_ge(stored["vs"], 16)
            tokens(tokA[:, 2, :], tokA)


_OUTS = [("y_prompt", (1, TP, D)), ("y_sample", (NB, 1, D)), ("k_prompt", (1, TP, H, 2, HD)),
         ("v_prompt", (1, TP, H, P)), ("k_sample", (NB, 1, H, 2, HD)), ("v_sample", (NB, 1, H, P)),
         ("chunk_v_sample", (1, NB, 1, D))]


def kernel(**inputs):
    import concourse.bacc as bacc
    from concourse.bass_utils import run_bass_kernel_spmd

    nc = bacc.Bacc("TRN2", target_bir_lowering=False, num_devices=1)
    arrays = {f"in_{n}": np.ascontiguousarray(v) for n, v in inputs.items()}
    arrays["in_consts"] = constants()
    arrays["in_rotary"] = rotary()
    ins = {n[3:]: nc.dram_tensor(n, v.shape, mybir.dt.from_np(v.dtype), kind="ExternalInput").ap()
           for n, v in arrays.items()}
    outs = {n: nc.dram_tensor(f"out_{n}", s, F32, kind="ExternalOutput").ap() for n, s in _OUTS}
    build(nc, ins, outs)
    r = run_bass_kernel_spmd(nc, [arrays], core_ids=[0])
    return tuple(r.results[0][f"out_{n}"] for n, _ in _OUTS)
```

```python
import math
from contextlib import ExitStack, contextmanager

import numpy as np

import concourse.bass as bass
from concourse import mybir

F32 = mybir.dt.float32
F32R = mybir.dt.float32r
I32 = mybir.dt.int32
ALU = mybir.AluOpType
ACT = mybir.ActivationFunctionType
AX = mybir.AxisListType

P = 128
D = 1024
C = D // P
TP = 256
NB = 8
T = TP + NB
DEPTH = 2
NE = 16
EG = 4
FE = 512
FB = FE // P
H = 8
HD = 64
PAST = 1024
PAGE = 128
NPG = PAST // PAGE
POOLN = 80
ROT = HD // 4
ALPHA = (2 * DEPTH) ** 0.25
EPS = 1e-5
LAM_INIT = 0.8 - 0.6 * math.exp(-0.3 * 1)
NEG = -1e30
SLOTS = 6
TILE = 4096
NBANK = 4
TOP = 2
SLOT_N = TOP * T
SPAN = P
PACK = SLOT_N + SPAN
NK = -(-SLOT_N // P)
LAST = SLOT_N - (NK - 1) * P
NR = 1 + NB
PAIRS = ((2, 0), (1, 3), (4, 5))
LOADS = [("k", 0), ("k", 1)] + [x for m in range(NB - 2) for x in (("k", m + 2), ("v", m))] + [("v", NB - 2), ("v", NB - 1)]

K_ID, K_ROT, K_ONE, K_TRI, K_MASK, K_IOTA, K_PART = 0, 128, 256, 384, 512, 768, 768 + T
K_N = 768 + T + 5
V_LNG, V_LNB, V_AG, V_AB, V_SUB, V_N = 0, 32, 64, 72, 80, 81


def constants():
    k = np.zeros((P, K_N), np.float32)
    k[:, K_ID:K_ID + P] = np.eye(P)
    half = ROT // 2
    for c in range(2):
        for i in range(half):
            a, b = c * HD + i, c * HD + half + i
            k[b, K_ROT + a] = -1.0
            k[a, K_ROT + b] = 1.0
    k[:, K_ONE:K_ONE + P] = 1.0
    k[:, K_TRI:K_TRI + P] = np.arange(P)[:, None] < np.arange(P)[None, :]
    k[:, K_IOTA:K_IOTA + T] = np.arange(T)
    k[:, K_MASK + P:K_MASK + 2 * P] = np.where(
        np.arange(P)[:, None] >= np.arange(P)[None, :], 0.0, NEG)
    k[:, K_PART:K_PART + 5] = np.arange(P)[:, None] + P * np.arange(5)[None, :]
    return k


def rotary():
    k = np.zeros((P, 2, T), np.float32)
    half = ROT // 2
    inv = 1.0 / (np.float32(500000.0) ** (np.arange(0, ROT, 2, dtype=np.float32) / ROT))
    pos = np.concatenate([np.arange(TP), np.full(NB, PAST)]).astype(np.float32)
    ang = (pos[None, :] * inv.astype(np.float32)[:, None]).astype(np.float32)
    k[:, 0] = 1.0
    for c in range(2):
        for r in range(2):
            a = c * HD + r * half
            k[a:a + half, 0] = np.cos(ang)
            k[a:a + half, 1] = np.sin(ang)
    return k


def cache_slot(kind, seq, k):
    j = LOADS.index((kind, seq))
    return PAIRS[j % 3][k], 4 * (j // 3 + 1)


class Tally:

    def __init__(self, sem):
        self.sem, self.n, self.turn = sem, 0, None

    def add(self, k=1):
        self.n += k
        return self.value()

    def value(self, back=0):
        v = self.n - back
        return v if self.turn is None else self.turn + v


@contextmanager
def turns(eng, count, per):
    before = {t: t.n for t in per}
    with eng.Fori(0, count) as i:
        for t, k in per.items():
            t.turn = i * k
        yield i
    for t, k in per.items():
        assert t.n - before[t] == k, (t.sem, t.n - before[t], k)
        t.turn = None
        t.n = before[t] + k * count


def build(nc, a, o):
    with ExitStack() as ctx:
        place = {}

        def sb(name, shape, dt=F32):
            place[name] = -(-nc.sbuf_base // 32) * 32
            return ctx.enter_context(nc.sbuf_tensor(name, shape, dt))

        def rounded(name, of, first, n):
            return nc.alloc_sbuf_tensor_at(name, [P, n], F32R, offset=place[of] + 4 * first)[:, :]

        def sem(name):
            return ctx.enter_context(nc.semaphore(name))

        wring = sb("wring", [P, SLOTS, TILE])
        kst = sb("kst", [P, K_N])
        xT = sb("xT", [P, C, T])
        hT = sb("hT", [P, C, T])
        yT = sb("yT", [P, C, T])
        reg1 = sb("reg1", [P, C * PACK])
        reg2 = sb("reg2", [P, C * PACK])
        tok4 = sb("tok4", [P, 4, D])
        tokA = tok4[:, 0:3, :]
        bsb = tok4[:, 3, :].rearrange("p (g n) -> p g n", n=P)
        tokB = sb("tokB", [P, 2, D])
        ws2 = sb("ws2", [P, 16, P])
        ws = ws2[:, 0:8, :]
        wsT = ws2[:, 8:16, :]
        ws00 = sb("ws00", [P, 8])
        rw = sb("rw", [P, C, NE])
        rbias = sb("rbias", [P, NE])
        vT = sb("vecT", [P, V_N])
        adabT = sb("adabT", [P, 96])
        cT = sb("cT", [P, C, NR])
        mT = sb("mT", [P, 48, NR])
        rs = sb("rs", [P, T])
        epsc = sb("epsc", [P, 1])
        lgT = sb("lgT", [NE, T])
        lg = sb("lg", [P, 3, NE])
        score = sb("score", [P, 3, NE])
        sel = sb("sel", [P, 3, NE])
        top = [sb(f"top{i}", [P, 3, NE]) for i in range(2)]
        key = sb("key", [P, 3, NE])
        pair = [sb(f"pair{i}", [P, 3, EG]) for i in range(4)]
        one = sb("one", [P, 3, 1])
        stack = sb("stack", [P, 3, 4, NE])
        sg = sb("sg", [P, 3, 6])
        ncol = sb("ncol", [NE, 1])
        pos = sb("pos", [P, 3, NE])
        nrow = sb("nrow", [P, 2 * NE])
        lim = sb("lim", [P, 2, NE])
        starts = sb("starts", [1, 3 * NE + 1], I32)
        startf = sb("startf", [1, 3 * NE + 1])
        kidx = sb("kidx", [P, NE])
        ptab = sb("ptab", [1, NB * NPG], I32)
        lamx = sb("lamx", [P, 4, HD])
        lams = sb("lams", [1, 5])
        nlam = sb("nlam", [P, 1])
        subg = sb("subg", [P, 1])
        pst = sb("pst", [P, 2, 6])
        scol = sb("scol", [P, 1])

        abT = reg1[:, 0:2 * C * T].rearrange("p (c t) -> p c t", t=T)
        crows = reg1[:, 2 * C * T:C * PACK]
        cqT = reg2[:, 0:C * T].rearrange("p (c t) -> p c t", t=T)
        sqT = reg2[:, C * T:2 * C * T].rearrange("p (c t) -> p c t", t=T)
        mrows = reg2[:, 2 * C * T:C * PACK]
        xg = reg1[:, :].rearrange("p (c n) -> p c n", n=PACK)
        yg = reg2[:, :].rearrange("p (c n) -> p c n", n=PACK)
        yr = reg1[:, 0:NK * D].rearrange("p (k n) -> p k n", n=D)
        pick = yT[:, :, :].rearrange("p c t -> p (c t)")[:, 0:3 * SLOT_N].rearrange("p (j n) -> p j n", n=SLOT_N)
        put = hT[:, :, :].rearrange("p c t -> p (c t)")[:, 0:NK * T].rearrange("p (k t) -> p k t", t=T)
        piece = hT[:, :, :].rearrange("p c t -> p (c t)")[:, 0:2048].rearrange("p (b k n) -> p b k n", b=2, n=P)
        flatB = tokB[:, :, :].rearrange("p b n -> p (b n)")
        aT = flatB[:, 0:512].rearrange("p (f n) -> p f n", n=P)
        atok = flatB[:, 512:1024]
        upT = flatB[:, 1024:1536].rearrange("p (f n) -> p f n", n=P)
        sgB = flatB[:, 0:4 * T].rearrange("p (i t) -> p i t", t=T)
        xe = tokA[:, 0, :].rearrange("p (c n) -> p c n", n=P)
        xhi = rounded("xhi", "tok4", 0, D).rearrange("p (c n) -> p c n", n=P)
        xlo = rounded("xlo", "tok4", D, D).rearrange("p (c n) -> p c n", n=P)
        whi = [rounded(f"whi{q}", of, first, 2048).rearrange("p (k n) -> p k n", n=512)
               for q, (of, first) in enumerate((("ws2", 0), ("hT", 0), ("tok4", 2 * D), ("yT", 0)))]
        yR, hR = (rounded(f"{n}_rounded", n, 0, C * T).rearrange("p (c t) -> p c t", t=T) for n in ("yT", "hT"))
        uR = rounded("u_rounded", "reg1", 0, C * T).rearrange("p (c t) -> p c t", t=T)
        sR = rounded("s_rounded", "reg2", C * T, C * T).rearrange("p (c t) -> p c t", t=T)
        half_c, half_s, half_w, half_b = (
            rounded(f"half_{of}_{first}", of, first, 2048).rearrange("p (k n) -> p k n", n=256)
            for of, first in (("reg2", 0), ("reg2", C * T), ("ws2", 0), ("tokB", 0)))
        tR = rounded("tok_rounded", "tok4", 0, C * T).rearrange("p (c t) -> p c t", t=T)
        dense = {"a_in": (yR, hR, (half_c, half_b)), "a_out": (hR, uR, (half_c, half_b)),
                 "kv": (yR, sR, (half_w, half_c)), "q": (tR, hR, (half_w, half_s)),
                 "b_out": (uR, hR, (half_c, half_w))}

        def features(ring, slot, h):
            return ring[:, slot, :].rearrange("p (k n) -> p k n", n=512)[:, :, 256 * h:256 * (h + 1)]

        wlo = rounded("wlo", "wring", 0, SLOTS * TILE).rearrange("p (s n) -> p s n", s=SLOTS)

        def quarter(ring, q, slot):
            return ring[:, slot, (q % 2) * 2048:(q % 2 + 1) * 2048].rearrange("p (k n) -> p k n", n=512)
        cos, sin = flatB[:, 0:T], flatB[:, T:2 * T]
        snew = stack[:, :, :, :].rearrange("p j i e -> p (j i) e")[:, 0:NB, :]
        sS = flatB[:, 0:NB * (NPG + 1) * 16].rearrange("p (b g x) -> p b g x", b=NB, g=NPG + 1)
        vrow = tokA[0:V_N, 0, 0:P]
        arow = tokA[0:96, 0, P:2 * P]
        crow = crows[0:NR, :]
        psc = mrows[:, :].rearrange("p (j c s) -> p j c s", j=2, c=2)
        pex = crows[:, :].rearrange("p (j c s) -> p j c s", j=2, c=2)
        sW = wsT[:, 0:4, :].rearrange("p a (x g h) -> p (a x) g h", g=NPG, h=H)
        pwT = wsT[:, 4:8, :].rearrange("p (j t) q -> p j t q", j=2)
        lamv = lamx[0:1, :, :]
        smx = lamx[:, 2:4, :].rearrange("p a d -> p (a d)")
        wnew = lamx[:, 0, :].rearrange("p (b h) -> p b h", b=NB)
        uT = abT[:, 0:C, :]
        zT = abT[:, C:2 * C, :]
        ident = kst[:, K_ID:K_ID + P]
        qbc = yT[:, :, :].rearrange("p c t -> p (c t)")[:, 0:2 * D].rearrange("p (b n) -> p b n", b=2)
        ksm = ws[:, :, :].rearrange("p g n -> p (g n)")
        osb = ksm
        qtok = bsb[:, :, :].rearrange("p g n -> p (g n)")

        def mrow(l, n):
            if l == 1 and 6 <= n <= 8:
                return flatB[0:NR, NB * (NPG + 1) * 16:NB * (NPG + 1) * 16 + 512]
            rows = mrows if l == 0 and n < 10 else qtok
            return rows[0:NR, (n % 2) * 512:(n % 2 + 1) * 512]

        def before(l, n):
            if (l, n) in ((1, 7), (1, 8)):
                return l, n - 1
            return (l, n - 2) if n >= 2 else (l - 1, n + 10)

        pj = [ctx.enter_context(nc.psum_tensor(f"pj{i}", [P, 512], F32)) for i in range(NBANK)]
        tb = [ctx.enter_context(nc.psum_tensor(f"tb{i}", [P, 512], F32)) for i in range(2)]
        gu = [ctx.enter_context(nc.psum_tensor(f"gu{i}", [P, 512], F32)) for i in range(2)]
        st = [x[:, 0:T] for x in gu]

        consts_in, rows_in, x_in, small_in, table_in = (
            sem(n) for n in ("consts_in", "rows_in", "x_in", "small_in", "table_in"))
        slot_in = [sem(f"slot{i}_in") for i in range(SLOTS)]
        stored = {n: sem(f"{n}_stored") for n in ("cv", "kp", "ks", "vp", "vs", "yp", "ys")}
        pool_own = sem("pool_own")
        ws_masked = sem("ws_masked")
        c_silu = sem("c_silu")
        pj_done, pj_evac = sem("pj_done"), sem("pj_evac")
        tb_done, tb_evac = sem("tb_done"), sem("tb_evac")
        st_done = sem("st_done")
        dve_own = sem("dve_own")
        op_ready = sem("op_ready")
        act_in = sem("act_in")
        act_out = sem("act_out")
        sq_ready = sem("sq_ready")
        source_ready = sem("source_ready")
        source_high = sem("source_high")
        source_low = sem("source_low")
        tile_high = sem("tile_high")
        tile_low = sem("tile_low")
        hi_ready = sem("hi_ready")
        lo_ready = sem("lo_ready")
        part_used = sem("part_used")
        xhi_ready = sem("xhi_ready")
        xe_ready = sem("xe_ready")
        silu_ready = sem("silu_ready")
        a_ready = sem("a_ready")
        yg_clear = sem("yg_clear")
        rotary_in = sem("rotary_in")
        routed = sem("routed")
        more = [{n: sem(f"more{l}_{n}") for n in ("x", "piece", "done", "silu", "evac", "mask")} for l in range(DEPTH)]
        keys_used = sem("keys_used")
        values_used = sem("values_used")

        at = {}
        block = ctx.enter_context(nc.Block())

        @block.tensor
        def _(pe):
            g, b, sd = Tally(pj_done), Tally(tb_done), Tally(st_done)
            op, an, sqn = Tally(op_ready), Tally(a_ready), Tally(sq_ready)
            loads = [0] * SLOTS
            banks = [0]
            uses = at["uses"] = []

            def loaded(s, k=1, turn=0):
                loads[s] += 16 * k
                pe.wait_ge(slot_in[s], turn + loads[s])

            def operand():
                pe.wait_ge(op_ready, op.add())

            def squares():
                pe.wait_ge(sq_ready, sqn.add())

            def group(rows, n, pairs, before=lambda j: None):
                k = banks[0]
                banks[0] += 1
                if k >= NBANK:
                    pe.wait_ge(pj_evac, g.value(NBANK - 1))
                out = pj[k % NBANK][0:rows, 0:n]
                for j, (lhsT, rhs) in enumerate(pairs):
                    before(j)
                    m = pe.matmul(out, lhsT, rhs, start=(j == 0), stop=(j == len(pairs) - 1))
                m.then_inc(pj_done, 1)
                g.add()

            def turned(rows, src):
                k = banks[0] % NBANK
                banks[0] += 1
                pe.wait_ge(pj_evac, g.value(NBANK - 1))
                for c in range(4):
                    m = pe.transpose(pj[k][0:rows, c * P:(c + 1) * P], src[:, c, :], ident)
                m.then_inc(pj_done, 1)
                g.add()

            def small(parts):
                if b.n >= 2:
                    pe.wait_ge(tb_evac, b.value(1))
                bank = tb[b.n % 2]
                for (rows, c0, n), fn in parts:
                    m = fn(bank[0:rows, c0:c0 + n])
                m.then_inc(tb_done, 1)
                b.add()

            def emptied():
                pe.wait_ge(tb_evac, b.value())

            def tr(src, rows=P):
                return lambda dst: pe.transpose(dst, src, ident[0:rows, 0:rows])

            def mm(lhsT, rhs, start=True, stop=True):
                return lambda dst: pe.matmul(dst, lhsT, rhs, start=start, stop=stop)

            low, sl = Tally(tile_low), Tally(source_low)
            tiles, halves = at["tiles"], at["halves"] = [], []

            def project(s, name, first):
                xh, xl, highs = dense[name]
                loads[s] += 16
                tiles.append((s, loads[s], name))
                for h in range(2):
                    pe.wait_ge(tile_low, low.add())
                    for f in range(2):
                        cols = slice(f * P, (f + 1) * P)
                        hi, lo = highs[h][:, :, cols], features(wlo, s, h)[:, :, cols]

                        def split(j):
                            if first and h == 0 and f == 0 and j % 6 == 0:
                                pe.wait_ge(source_low, sl.add())

                        group(P, T, [(w[:, k, :], x[:, k, :]) for k in range(C) for w, x in ((hi, xh), (hi, xl), (lo, xh))], split)
                    halves.append(g.n)
                uses.append((s, g.n))

            def stat(src, which, ready):
                for k in range(C):
                    if k % 2 == 0:
                        ready()
                    m = pe.matmul(st[which][:, :], kst[:, K_ONE:K_ONE + P], src[:, k, :],
                                  start=(k == 0), stop=(k == C - 1))
                m.then_inc(st_done, 1)
                sd.add()

            def norm(src, beside=lambda: None, ready=operand):
                stat(src, 0, ready)
                beside()
                stat(sqT, 1, squares)

            def to_tokens(src):
                for q in range(2):
                    small([((NB, c * P, P), tr(src[:, 4 * q + c, TP:T])) for c in range(4)])
                for j in range(2):
                    for q in range(2):
                        small([((P, c * P, P), tr(src[:, 4 * q + c, j * P:(j + 1) * P])) for c in range(4)])

            row_group = {}

            def ada_tile(l, n, s, count=None):
                if count is None:
                    loaded(s)
                else:
                    pe.wait_ge(slot_in[s], count)
                w = wring[:, s, :].rearrange("p (k n) -> p k n", n=512)
                group(NR, 512, [(cT[:, k, :], w[:, k, :]) for k in range(C)])
                row_group[l, n] = g.n
                uses.append((s, g.n))

            def ada_turn(l, n):
                pe.wait_ge(pj_evac, row_group[l, n])
                small([((P, 16 * c, NR), tr(mrow(l, n)[:, c * P:(c + 1) * P], NR)) for c in range(4)])
                at[f"turn{l}_{n}"] = b.n

            pe.wait_ge(consts_in, 16)
            pe.wait_ge(rows_in, 16 * 8)
            small([((P, 0, V_N), tr(vrow, V_N)), ((P, P, 96), tr(arow, 96))])
            pe.wait_ge(c_silu, 1)
            small([((P, 16 * c, NR), tr(crow[:, c * P:(c + 1) * P], NR)) for c in range(C)])
            emptied()
            ada_tile(0, 0, 0)
            ada_tile(0, 1, 1)
            pe.wait_ge(x_in, 32)
            for j in range(2):
                for q in range(2):
                    small([((P, c * P, P), tr(tokB[:, j, (4 * q + c) * P:(4 * q + c + 1) * P])) for c in range(4)])
            small([((P, 16 * c, NB), tr(tokA[0:NB, 2, c * P:(c + 1) * P], NB)) for c in range(C)])
            ada_turn(0, 0)
            for n in range(2, 4):
                ada_tile(0, n, n)
                ada_turn(0, n - 1)
            ada_turn(0, 3)
            pe.wait_ge(ws_masked, 1)
            for q in range(2):
                small([((P, c * P, P), tr(ws[:, 4 * q + c, :])) for c in range(4)])
            ada_tile(0, 4, 4)

            for n, s in enumerate((5, 0, 1, 2)):
                project(s, "a_in", n == 0)
            at["uv"] = g.n
            ada_turn(0, 4)
            pe.wait_ge(pj_evac, g.n)
            norm(zT, lambda: ada_tile(0, 5, 3), lambda: None)
            ada_turn(0, 5)
            ada_tile(0, 6, 4)
            operand()
            to_tokens(zT)
            at["v_tok"] = b.n
            ada_tile(0, 7, 5)
            emptied()
            for q in range(4):
                small([((P, P * (2 * i + j), P), mm(tokA[:, j, (2 * q + i) * P:(2 * q + i + 1) * P], wsT[:, 2 * q + i, :]))
                       for i in range(2) for j in range(2)])
            ada_turn(0, 6)
            ada_tile(0, 8, 2)
            for n, s in enumerate((0, 1)):
                project(s, "a_out", n == 0)
            at["a_out"] = g.n
            ada_turn(0, 7)

            def beside():
                ada_turn(0, 8)
                ada_tile(0, 9, 3)

            norm(yT, beside)
            ada_turn(0, 9)
            ada_tile(0, 10, 4)

            def moe(l):
                def logits(k):
                    def part(dst):
                        if k % 2 == 0:
                            operand()
                        return pe.matmul(dst, rw[:, k, :], hT[:, k, :], start=(k == 0), stop=(k == C - 1))
                    return part

                small([((NE, 0, T), logits(k)) for k in range(C)])
                emptied()
                small([((n, NE * j, NE), tr(lgT[:, j * P:j * P + n], NE)) for j, n in enumerate((P, P, NB))])
                at[f"router{l}"] = b.n
                ada_tile(l, 11, (5, 2)[l])
                for n, j in ((NB, 2), (P, 0), (P, 1)):
                    for q in range(2):
                        turned(n, hT[:, 4 * q:4 * q + 4, j * P:j * P + n])
                token_groups = g.n
                operand()
                tiles = (P, P, NB)
                small([((NE, 0, 1), mm(key[0:n, j, :], kst[0:n, K_ONE:K_ONE + 1], j == 0, j == 2))
                       for j, n in enumerate(tiles)])
                emptied()
                count = ncol[:, 0:1].to_broadcast([NE, P])
                below = kst[0:NE, K_TRI:K_TRI + NE]
                parts = []
                for j, n in enumerate(tiles):
                    at_j = (n, NE * j, NE)
                    parts.append((at_j, mm(ncol[:, 0:1].to_broadcast([NE, n]), below, True, False)))
                    for i in range(j):
                        parts.append((at_j, mm(kst[:, K_ONE:K_ONE + n], key[:, i, :], False, False)))
                    parts.append((at_j, mm(kst[0:n, K_TRI:K_TRI + n], key[0:n, j, :], False, True)))
                parts.append(((P, 3 * NE, NE), mm(count, ident[0:NE, 0:NE])))
                parts.append(((P, 4 * NE, NE), mm(count, below)))
                small(parts)
                ada_turn(l, 10)
                if l == 0:
                    ada_tile(1, 0, 2)
                ada_turn(l, 11)
                pe.wait_ge(pj_evac, token_groups)
                for half in range(2):
                    operand()
                    for c in range(C):
                        group(P, T, [(tokA[0:n, j, c * P:(c + 1) * P], pick[0:n, j, half * T:(half + 1) * T])
                                     for j, n in enumerate(tiles)])
                at[f"moe{l}"] = g.n
                if l == 0:
                    ada_turn(1, 0)
                at[f"moe{l}_loads"] = list(loads)
                xn, lo, used = Tally(xe_ready), Tally(lo_ready), Tally(part_used)
                xn.n, lo.n, used.n = NE * l, 4 * NE * l, 4 * NE * l

                def part(q, slot):
                    pe.wait_ge(lo_ready, lo.add())
                    hi, low = whi[q], quarter(wlo, q, slot)
                    for k in range(4):
                        c = 4 * (q % 2) + k
                        for n, (x, w) in enumerate(((xhi, hi), (xhi, low), (xlo, hi))):
                            m = pe.matmul(gu[q // 2][:, :], x[:, c, :], w[:, k, :],
                                          start=(c == 0 and n == 0), stop=(c == C - 1 and n == 2))
                    m.then_inc(part_used, 1)
                    used.add()

                def down(s, turn):
                    loaded(s, turn=turn)
                    w = wring[:, s, :].rearrange("p (k n) -> p k n", n=D)
                    emptied()
                    for d in range(2):
                        bank = pj[banks[0] % NBANK]
                        banks[0] += 1
                        pe.wait_ge(pj_evac, g.value(NBANK - 1))
                        for i in range(4):
                            f = 4 * d + i
                            for k in range(FB):
                                m = pe.matmul(bank[:, i * P:(i + 1) * P], w[:, k, f * P:(f + 1) * P], aT[:, k, :],
                                              start=(k == 0), stop=(k == FB - 1))
                        m.then_inc(pj_done, 1)
                        g.add()

                def step(s, behind=True, turn=0):
                    pe.wait_ge(xe_ready, xn.add())
                    for q in range(4):
                        part(q, s + q // 2)
                    loads[s] += 16
                    loads[s + 1] += 16
                    if behind:
                        down(s + 2, turn)
                    pe.wait_ge(a_ready, an.add())
                    small([((P, f * P, P), tr(atok[:, f * P:(f + 1) * P])) for f in range(FB)])

                step(0, False)
                with turns(pe, 7, {g: 4, b: 2, an: 2, xn: 2, lo: 8, used: 8}) as i:
                    step(3, turn=i * 16)
                    step(0, turn=i * 16)
                for s in range(SLOTS):
                    loads[s] += 16 * 6
                step(3)
                down(2, 0)
                pe.wait_ge(pj_evac, g.n)
                at[f"moe{l}_main"] = g.n
                more_pe(l)
                small([((6, P * j, n), tr(sg[0:n, j, :], n)) for j, n in enumerate(tiles)])
                emptied()
                for i in range(4):
                    small([((P, 0, T), mm(ident[0:4, i:i + 1].to_broadcast([4, P]), lgT[0:4, :]))])
                for k in range(NK):
                    n = P if k < NK - 1 else LAST
                    for q in range(2):
                        turned(n, yg[:, 4 * q:4 * q + 4, k * P:k * P + n])
                pe.wait_ge(pj_evac, g.n)
                if l == 0:
                    ada_tile(1, 1, 0)
                operand()
                for c in range(C):
                    group(P, T, [(yr[0:(P if k < NK - 1 else LAST), k, c * P:(c + 1) * P], put[0:(P if k < NK - 1 else LAST), k, :])
                                 for k in range(NK)])
                at[f"moe{l}_end"] = g.n

            def more_pe(l):
                m = more[l]
                pe.wait_ge(routed, l + 1)
                many = pe.value_load(starts[0:1, 3 * NE:3 * NE + 1], min_val=0, max_val=1)
                with pe.If(many):
                    x, p_, ev = Tally(m["x"]), Tally(m["piece"]), Tally(m["evac"])
                    ev.add()
                    with turns(pe, NE, {x: 2, p_: 32 * 24, ev: 24}):
                        for half in range(2):
                            pe.wait_ge(m["x"], x.add())
                            for rnd in range(12):
                                pe.wait_ge(m["piece"], p_.add(32))
                                if rnd < 4:
                                    for b_ in range(2):
                                        for k in range(C):
                                            i = pe.matmul(pj[b_][:, 0:P], piece[:, b_, k, :], xe[:, k, :],
                                                          start=(k == 0), stop=(k == C - 1))
                                else:
                                    for k in range(FB):
                                        i = pe.matmul(pj[0][:, 0:P], piece[:, k // 2, k % 2, :], aT[:, k, :],
                                                      start=(k == 0), stop=(k == FB - 1))
                                i.then_inc(m["done"], 1)
                                pe.wait_ge(m["evac"], ev.add())
                with pe.Else():
                    pe.nop()

            moe(0)
            ada_turn(1, 1)
            ada_tile(1, 2, 1)

            def beside():
                ada_turn(1, 2)
                ada_tile(1, 3, 3)

            norm(yT, beside)
            ada_turn(1, 3)
            ada_tile(1, 4, 4)

            for n, s in enumerate((5, 2, 0, 1)):
                project(s, "kv", n == 0)
            at["kv"] = g.n
            ada_turn(1, 4)

            def rotary(src):
                for h in range(H):
                    small([((P, 0, T), mm(kst[:, K_ROT:K_ROT + P], src[:, h, :]))])

            pe.wait_ge(pj_evac, g.n - C)
            rotary(uT)
            for n, s in enumerate((3, 4)):
                project(s, "q", n == 0)
            at["q"] = g.n
            pe.wait_ge(pj_evac, g.n)
            rotary(cqT)
            ada_tile(1, 5, 5)
            ada_turn(1, 5)
            operand()
            for q in range(2):
                small([((NB, c * P, P), tr(cqT[:, 4 * q + c, TP:T])) for c in range(4)])
            operand()
            for c in range(2):
                small([((P, 0, 64), mm(kst[HD * c:HD * (c + 1), K_ONE:K_ONE + P], rs[HD * c:HD * (c + 1), 0:64]))])
            operand()
            small([((P, 0, 1), mm(kst[0:1, K_ONE:K_ONE + P], lams[0:1, 4:5]))])
            to_tokens(uT)
            at["k_tok"] = b.n
            to_tokens(zT)
            at["v2_tok"] = b.n

            at["spread"] = g.n
            loads[4] += 16
            loads[5] += 32
            at["cache_loads"] = list(loads)
            tile_in = [loads[4], loads[5] - 16, loads[5]]
            for s in range(SLOTS):
                loads[s] += 16 * sum(4 for j in range(len(LOADS)) if s in PAIRS[j % 3])

            def spread(s):
                for n in range(2):
                    group(P, 512, [(ident[0:NB, s:s + 1].to_broadcast([NB, P]), qtok[0:NB, n * 512:(n + 1) * 512])])
                at[f"spread{s}"] = g.n

            def values(s, k):
                slot, count = cache_slot("v", s, k)
                pe.wait_ge(slot_in[slot], at["cache_loads"][slot] + 16 * count)
                for n in range(2):
                    if k == 0:
                        pe.wait_ge(pj_evac, g.n + n + 1 - NBANK)
                    out = pj[(banks[0] + n) % NBANK][0:H, :]
                    for p in range(4):
                        m = pe.matmul(out, sW[:, s, 4 * k + p, :], wring[:, slot, p * D + n * 512:p * D + (n + 1) * 512],
                                      start=(k == 0 and p == 0), stop=(k == 1 and p == 3))
                    if k:
                        m.then_inc(pj_done, 1)
                if k:
                    g.add(2)
                    banks[0] += 2
                    at[f"values{s}"] = g.n
                else:
                    m.then_inc(values_used, 1)

            spread(0)
            for s in range(NB + 2):
                if s + 1 < NB:
                    spread(s + 1)
                if s >= 2:
                    operand()
                for c in range(2):
                    if s < NB:
                        small([((P, P * j, (j + 1) * P), mm(cqT[HD * c:HD * (c + 1), s, j * P:(j + 1) * P],
                                                            uT[HD * c:HD * (c + 1), s, 0:(j + 1) * P])) for j in range(2)])
                    if c == 0 and 1 <= s <= NB:
                        operand()
                        small([((16, 0, P), tr(smx[:, 16 * (s - 1):16 * s]))])
                if 1 <= s <= NB:
                    if s == NB:
                        emptied()
                    small([((P, 0, 16), mm(scol[0:16, 0:1].to_broadcast([16, P]), ident[0:16, 0:16]))])
                if s >= 2:
                    values(s - 2, 0)
                if s == 0:
                    ada_tile(1, 6, 4, tile_in[0])
                if s < NB:
                    for j in range(2):
                        operand()
                        small([((P, P * t, P), tr(pex[:, j, 0, t * P:(t + 1) * P])) for t in range(j + 1)])
                    weights_out = b.n
                if s < 2:
                    ada_tile(1, 7 + s, 5, tile_in[1 + s])
                if s >= 2:
                    values(s - 2, 1)
                if s == NB:
                    ada_tile(1, 9, 1)
                    squares()
                    for h in range(H):
                        small([((P, 0, TP), mm(kst[:, K_ONE:K_ONE + P], sqT[:, h, 0:TP]))])
                    at["rms"] = b.n
                if 1 <= s <= NB:
                    operand()
                    small([((P, 0, 16), mm(kst[:, K_ONE:K_ONE + P], smx[:, 16 * (s - 1):16 * s]))])
                if s < NB:
                    pe.wait_ge(tb_evac, weights_out)
                    for j in range(2):
                        small([((P, 0, P), mm(tokA[:, t, s * P:(s + 1) * P], pwT[:, j, t, :], t == 0, t == j))
                               for t in range(j + 1)])
                    at["heads"] = b.n
                if s >= 2:
                    pe.wait_ge(pj_evac, at[f"values{s - 2}"])
                    small([((P, H * c, H), tr(osb[0:H, c * P:(c + 1) * P], H)) for c in range(C)])
                    at[f"rows{s - 2}"] = b.n
                if s < 3:
                    ada_turn(1, 6 + s)
            ada_turn(1, 9)

            squares()
            small([((P, 0, H * NB), mm(kst[:, K_ONE:K_ONE + P], sqT[:, :, TP:T]))])
            at["rms_sample"] = b.n
            for n, s in enumerate((3, 4)):
                project(s, "b_out", n == 0)
            at["b_out"] = g.n
            norm(yT)
            ada_tile(1, 10, 5)
            moe(1)
            norm(yT)
            operand()
            to_tokens(xT)
            at["y_tok"] = b.n
            at["end"] = g.n

        @block.sync
        def _(sp):
            free = [None] * SLOTS
            done = [0]

            def slot(s, n=512):
                return wring[:, s, :].rearrange("p (k n) -> p k n", n=n)

            def load(s, src, groups=None, n=512):
                if free[s]:
                    sp.wait_ge(*free[s])
                sp.dma_start(slot(s, n), src).then_inc(slot_in[s], 16)
                if groups is None:
                    user, done[0] = at["uses"].pop(0)
                    assert user == s
                else:
                    done[0] += groups
                free[s] = (pj_done, done[0])

            def ada(l, n, s):
                load(s, columns("ada_w", n, l))

            def columns(name, n, l=None):
                w = a[name] if l is None else a[name][l]
                return w.rearrange("(k p) n -> p k n", p=P)[:, :, n * 512:(n + 1) * 512]

            sp.dma_start(kst[:], a["consts"]).then_inc(consts_in, 16)
            sp.dma_start(crow[0:1, :], a["c_prompt"]).then_inc(rows_in, 16)
            sp.dma_start(crow[1:NR, :], a["c_sample"]).then_inc(rows_in, 16)
            sp.dma_start(vrow[V_LNG:V_LNG + 32, :], a["ln_g"].rearrange("l j (c p) -> (l j c) p", p=P)).then_inc(rows_in, 16)
            sp.dma_start(vrow[V_LNB:V_LNB + 32, :], a["ln_b"].rearrange("l j (c p) -> (l j c) p", p=P)).then_inc(rows_in, 16)
            sp.dma_start(vrow[V_AG:V_AG + 8, :], a["a_ln_g"].rearrange("l (c p) -> (l c) p", p=P)).then_inc(rows_in, 16)
            sp.dma_start(vrow[V_AB:V_AB + 8, :], a["a_ln_b"].rearrange("l (c p) -> (l c) p", p=P)).then_inc(rows_in, 16)
            sp.dma_start(vrow[V_SUB:V_SUB + 1, :], a["b_subln_g"]).then_inc(rows_in, 16)
            sp.dma_start(arow, a["ada_b"].rearrange("l (c p) -> (l c) p", p=P)).then_inc(rows_in, 16)
            for n in range(2):
                ada(0, n, n)
            sp.dma_start(tokB[:], a["x_prompt"][0].rearrange("(j p) d -> p j d", p=P)).then_inc(x_in, 16)
            sp.dma_start(tokA[0:NB, 2, :], a["x_sample"].rearrange("b t d -> (b t) d")).then_inc(x_in, 16)
            for n in range(2, 5):
                ada(0, n, n)
            for n, s in enumerate((5, 0, 1, 2)):
                load(s, columns("a_w_in", n, 0))
            for n, s in ((5, 3), (6, 4), (7, 5), (8, 2)):
                ada(0, n, s)
            for n, s in enumerate((0, 1)):
                load(s, columns("a_w_out", n, 0))
            for n, s in ((9, 3), (10, 4), (11, 5)):
                ada(0, n, s)
            ada(1, 0, 2)

            def more_sp(l):
                m = more[l]
                sp.wait_ge(routed, l + 1)
                many = sp.value_load(starts[0:1, 3 * NE:3 * NE + 1], min_val=0, max_val=1)
                with sp.If(many):
                    sp.wait_ge(pj_evac, at[f"moe{l}_main"])
                    done = Tally(m["evac"])
                    done.add()
                    w = [a[n][l].rearrange("e (k p) n -> e p k n", p=P) for n in ("moe_w_gate", "moe_w_up", "moe_w_down")]
                    with turns(sp, NE, {done: 24}) as e:
                        for rnd in [*range(12)] * 2:
                                for b_ in range(2):
                                    if rnd < 4:
                                        src = w[b_][bass.ds(e, 1), :, :, rnd * P:(rnd + 1) * P]
                                        dst = piece[:, b_, :, :]
                                    else:
                                        src = w[2][bass.ds(e, 1), :, 2 * b_:2 * b_ + 2, (rnd - 4) * P:(rnd - 3) * P]
                                        dst = piece[:, b_, 0:2, :]
                                    sp.wait_ge(m["evac"], done.value())
                                    sp.dma_start(dst, src.rearrange("a p k n -> p (a k) n")).then_inc(m["piece"], 16)
                                done.add()
                with sp.Else():
                    sp.nop()

            def moe_loads(l):
                gate = a["moe_w_gate"][l].rearrange("e (k p) n -> e p k n", p=P)
                up = a["moe_w_up"][l].rearrange("e (k p) n -> e p k n", p=P)
                down = a["moe_w_down"][l].rearrange("e (k p) n -> e p k n", p=P)

                def parts(e, both):
                    return part_used, 4 * NE * l + 4 * e + (4 if both else 2)

                def result(e):
                    return pj_done, at[f"moe{l}"] + 2 * (e + 1)

                def step(s, e):
                    if e < NE:
                        load(s, gate[e], 0)
                        load(s + 1, up[e], 0)
                        free[s], free[s + 1] = parts(e, False), parts(e, True)
                    if e > 0:
                        load(s + 2, down[e - 1], 0, D)
                        free[s + 2] = result(e - 1)

                step(0, 0)
                step(3, 1)
                step(0, 2)
                with sp.Fori(0, 6) as i:
                    for k in range(2):
                        s = 3 - 3 * k
                        e = i * 2 + (3 + k)
                        for slot_, src, n, (sem_, v), per in (
                                (s, gate[bass.ds(e, 1)], 512, parts(1 + k, False), 8),
                                (s + 1, up[bass.ds(e, 1)], 512, parts(1 + k, True), 8),
                                (s + 2, down[bass.ds(e - 1, 1)], D, result(k), 4)):
                            sp.wait_ge(sem_, i * per + v)
                            sp.dma_start(slot(slot_, n), src.rearrange("a p k n -> p (a k) n")).then_inc(slot_in[slot_], 16)
                for e, s in ((13, 3), (14, 0)):
                    free[s], free[s + 1], free[s + 2] = parts(e, False), parts(e, True), result(e - 1)
                step(3, 15)
                step(0, 16)
                done[0] = at[f"moe{l}"] + 2 * NE
                assert done[0] == at[f"moe{l}_main"]
                more_sp(l)
                done[0] = at[f"moe{l}_end"]

            moe_loads(0)
            for n, s in ((1, 0), (2, 1), (3, 3), (4, 4)):
                ada(1, n, s)
            for name, slots in (("kv_w_k", (5, 2)), ("kv_w_v", (0, 1))):
                for n, s in enumerate(slots):
                    load(s, columns(name, n))
            for n, s in enumerate((3, 4)):
                load(s, columns("b_w_q", n, 0))
            ada(1, 5, 5)

            keys = a["cache_k"].rearrange("g p h c d -> g p (h c d)")
            vals = a["cache_v"].rearrange("g p h e -> g p (h e)")

            def pages(cache, seq, k, s, sem_, value):
                with sp.Fori(0, 4) as i:
                    page = sp.value_load(ptab[0:1, bass.ds(seq * NPG + 4 * k + i, 1)], min_val=0, max_val=POOLN - 1)
                    sp.wait_ge(sem_, value)
                    sp.dma_start(wring[:, s, bass.ds(i * D, D)],
                                 cache[bass.ds(page, 1)].rearrange("a p n -> p (a n)")).then_inc(slot_in[s], 16)

            def used(kind, seq, k):
                if kind == "k":
                    return keys_used, 2 * seq + k + 1
                return (pj_done, at[f"values{seq}"]) if k else (values_used, seq + 1)

            sp.wait_ge(table_in, 16)
            for kind, seq in LOADS:
                for k in range(2):
                    if (kind, seq) == ("k", 2):
                        for n, s in (((6, 4), (7, 5)), ((8, 5),))[k]:
                            ada(1, n, s)
                    s, _ = cache_slot(kind, seq, k)
                    pages(keys if kind == "k" else vals, seq, k, s, *free[s])
                    free[s] = used(kind, seq, k)
            ada(1, 9, 1)
            for n, s in enumerate((3, 4)):
                load(s, columns("b_w_o", n, 0))
            for n, s in ((10, 5), (11, 2)):
                ada(1, n, s)
            assert not at["uses"]
            moe_loads(1)

            sp.wait_ge(tb_evac, at["y_tok"])
            sp.dma_start(o["y_prompt"][0].rearrange("(j p) d -> p j d", p=P), tokA[:, 0:2, :]).then_inc(stored["yp"], 16)
            sp.dma_start(o["y_sample"].rearrange("b t d -> (b t) d"), tokA[0:NB, 2, :]).then_inc(stored["ys"], 16)
            for n in stored:
                sp.wait_ge(stored[n], 16)

        @block.gpsimd
        def _(pool):
            pool.dma_start(ptab[:], a["page_table"].rearrange("(o b) n -> o (b n)", o=1)).then_inc(table_in, 16)
            pool.dma_start(ws[:], a["a_w_s"][0].rearrange("g i j -> i g j")).then_inc(small_in, 16)
            pool.dma_start(bsb[:], a["a_b_s"].to_broadcast([P, 8, P])).then_inc(small_in, 16)
            pool.dma_start(ws00[:], a["a_w_s"][0:1, :, 0, 0].to_broadcast([P, 8]),
                           allow_slow_non_contiguous=True).then_inc(small_in, 16)
            pool.dma_start(rw[:], a["router_w"].rearrange("(k p) e -> p k e", p=P)).then_inc(small_in, 16)
            pool.dma_start(rbias[:], a["router_bias"].rearrange("(o e) -> o e", o=1).to_broadcast([P, NE])).then_inc(small_in, 16)
            for n, name in enumerate(("b_lam_q1", "b_lam_k1", "b_lam_q2", "b_lam_k2")):
                pool.dma_start(lamv[:, n, :], a[name]).then_inc(small_in, 16)
            pool.memset(epsc[:], EPS).then_inc(pool_own, 1)
            kint = stack[:, 0, 0, :].bitcast(I32)
            pool.iota(kint, pattern=[[-1, NE]], base=NE, channel_multiplier=0).then_inc(pool_own, 1)
            pool.wait_ge(pool_own, 2)
            pool.tensor_copy(kidx[:], kint).then_inc(pool_own, 1)
            pool.wait_ge(small_in, 16 * 9)
            pool.affine_select(out=ws[:], in_=ws[:], compare_op=ALU.is_ge, fill=0.0, base=0,
                               pattern=[[0, 8], [-1, P]], channel_multiplier=1).then_inc(ws_masked, 1)
            pool.wait_ge(tb_evac, at["v_tok"])
            pool.dma_start(o["chunk_v_sample"].rearrange("l b t d -> (l b t) d"), tokA[0:NB, 2, :]).then_inc(stored["cv"], 16)

            def clear(l):
                pool.wait_ge(tb_evac, at[f"router{l}"])
                pool.memset(reg2[:], 0.0).then_inc(yg_clear, 1)

            clear(0)
            pool.wait_ge(tb_evac, at["turn1_1"])
            pool.dma_start(flatB[:, 0:2 * T], a["rotary"].rearrange("p a t -> p (a t)")).then_inc(rotary_in, 16)
            pool.wait_ge(tb_evac, at["k_tok"])
            pool.dma_start(o["k_prompt"][0].rearrange("(j p) h c d -> p j (h c d)", p=P), tokB[:]).then_inc(stored["kp"], 16)
            pool.dma_start(o["k_sample"].rearrange("b t h c d -> (b t) (h c d)"), ksm[0:NB, :]).then_inc(stored["ks"], 16)
            pool.wait_ge(tb_evac, at["v2_tok"])
            pool.dma_start(o["v_prompt"][0].rearrange("(j p) h e -> p j (h e)", p=P), tokA[:, 0:2, :]).then_inc(stored["vp"], 16)
            pool.dma_start(o["v_sample"].rearrange("b t h e -> (b t) (h e)"), tokA[0:NB, 2, :]).then_inc(stored["vs"], 16)
            clear(1)

        @block.scalar
        def _(act):
            g, inp = Tally(pj_evac), Tally(act_in)
            banks = [0]

            def evac(dst, func=ACT.Copy, rows=P, n=T):
                bank = pj[banks[0] % NBANK]
                banks[0] += 1
                act.wait_ge(pj_done, g.add())
                act.activation(dst, bank[0:rows, 0:n] if n < 512 or rows < P else bank[:, :].rearrange("p (f n) -> p f n", n=P), func).then_inc(pj_evac, 1)

            def evac_wide(dst, rows):
                evac(dst if rows < P else dst.rearrange("p (f n) -> p f n", n=P), rows=rows, n=512)

            def answer(dst, src, func, **kw):
                act.wait_ge(act_in, inp.add())
                act.activation(dst, src, func, **kw).then_inc(act_out, 1)

            sd, ready = Tally(st_done), Tally(source_ready)
            highs = [0]

            def source_split(name, src, parts):
                for p in range(4):
                    act.wait_ge(source_ready, ready.add() if p < parts else ready.value())
                    act.activation(dense[name][0][:, 2 * p:2 * p + 2, :], src[:, 2 * p:2 * p + 2, :],
                                   ACT.Copy).then_inc(source_high, 1)

            def tile_split():
                n, h = divmod(highs[0], 2)
                highs[0] += 1
                s, count, name = at["tiles"][n]
                if h == 0:
                    act.wait_ge(slot_in[s], count)
                if n:
                    act.wait_ge(pj_done, at["halves"][2 * (n - 1) + h])
                act.activation(dense[name][2][h], features(wring, s, h), ACT.Copy).then_inc(tile_high, 1)

            def projected(dst, func=ACT.Copy, ahead=False):
                count = dst.shape[1] // 4
                for t in range(count):
                    for h in range(2):
                        for f in range(2):
                            evac(dst[:, 4 * t + 2 * h + f, :], func)
                        if t + 1 < count or (ahead and h == 0):
                            tile_split()

            def square(src):
                for c in range(0, C, 2):
                    act.wait_ge(act_in, inp.add())
                    act.activation(sqT[:, c:c + 2, :], src[:, c:c + 2, :], ACT.Square).then_inc(sq_ready, 1)

            def norm(src, beside=lambda: None):
                square(src)
                beside()
                act.wait_ge(st_done, sd.add(2))
                act.activation(rs[:], st[1][:, :], ACT.Sqrt, bias=epsc[:, 0:1], scale=1.0 / D).then_inc(act_out, 1)

            def rows(l, n):
                if l or n >= 2:
                    act.wait_ge(tb_done, at["turn%d_%d" % before(l, n)])
                evac(mrow(l, n), rows=NR, n=512)

            act.wait_ge(rows_in, 16 * 8)
            act.activation(crow, crow, ACT.Silu).then_inc(c_silu, 1)
            for n in range(4):
                rows(0, n)
            tile_split()
            source_split("a_in", hT, 4)
            tile_split()
            rows(0, 4)
            projected(abT, ACT.Gelu_apprx_tanh)
            act.wait_ge(pool_own, 1)
            norm(zT, lambda: rows(0, 5))
            rows(0, 6)
            for _ in range(2):
                tile_split()
            rows(0, 7)
            rows(0, 8)
            source_split("a_out", uT, 1)
            projected(yT)
            norm(yT[:], lambda: rows(0, 9))
            rows(0, 10)

            def moe(l):
                answer(score[:], lg[:], ACT.Exp)
                rows(l, 11)
                for n in (("cv",), ("vp", "vs"))[l]:
                    act.wait_ge(stored[n], 16)
                for n, j in ((NB, 2), (P, 0), (P, 1)):
                    for q in range(2):
                        evac_wide(tokA[0:n, j, q * 512:(q + 1) * 512], n)
                if l == 0:
                    rows(1, 0)
                used, gt = Tally(part_used), Tally(silu_ready)
                used.n, gt.n = 4 * NE * l, NE * l
                slots = list(at[f"moe{l}_loads"])

                def high(q, s, turn=0, first=False):
                    s += q // 2
                    if q % 2 == 0:
                        slots[s] += 16
                        act.wait_ge(slot_in[s], turn + slots[s])
                    if not first:
                        act.wait_ge(part_used, used.add())
                    act.activation(whi[q], quarter(wring, q, s), ACT.Copy).then_inc(hi_ready, 1)

                def tokens_high(e):
                    first = act.value_load(starts[0:1, bass.ds(e, 1)], min_val=0, max_val=SLOT_N)
                    act.activation(xhi, xg[:, :, bass.ds(first, P)], ACT.Copy).then_inc(xhi_ready, 1)

                high(0, 0, first=True)
                high(1, 0, first=True)
                for half in range(2):
                    for c in range(C):
                        evac(xg[:, c, half * T:(half + 1) * T])
                act.wait_ge(routed, l + 1)
                act.wait_ge(yg_clear, l + 1)
                act.wait_ge(pj_evac, g.value())
                if l == 0:
                    act.wait_ge(tb_done, at["turn1_0"])
                tokens_high(0)
                high(2, 0, first=True)
                high(3, 0, first=True)

                def down(e):
                    first = act.value_load(starts[0:1, bass.ds(e, 1)], min_val=0, max_val=SLOT_N)
                    act.wait_ge(pj_evac, g.value())
                    for d in range(2):
                        evac(yg[:, 4 * d:4 * d + 4, bass.ds(first, P)], n=512)

                def step(e, s, last=False, first=False, turn=0):
                    if not last:
                        high(0, s, turn)
                        high(1, s, turn)
                    act.wait_ge(part_used, used.value() if not last else used.add(2))
                    act.activation(atok, gu[0][:, :], ACT.Silu).then_inc(silu_ready, 1)
                    gt.add()
                    if not last:
                        high(2, s, turn)
                        high(3, s, turn)
                        tokens_high(e + 1)
                    if not first:
                        down(e - 1)

                step(0, 3, first=True)
                with turns(act, 7, {g: 4, used: 8, gt: 2}) as i:
                    step(i * 2 + 1, 0, turn=i * 16)
                    step(i * 2 + 2, 3, turn=i * 16)
                step(15, 0, last=True)
                down(15)
                m = more[l]
                many = act.value_load(starts[0:1, 3 * NE:3 * NE + 1], min_val=0, max_val=1)
                with act.If(many):
                    done = Tally(m["done"])
                    with turns(act, NE, {done: 24}):
                        for half in range(2):
                            for rnd in range(4):
                                act.wait_ge(m["done"], done.add())
                                act.activation(aT[:, rnd, :], pj[0][:, 0:P], ACT.Silu).then_inc(m["silu"], 1)
                            done.add(8)
                with act.Else():
                    act.nop()
                for k in range(NK):
                    n = P if k < NK - 1 else LAST
                    for q in range(2):
                        evac_wide(yr[0:n, k, q * 512:(q + 1) * 512], n)
                if l == 0:
                    rows(1, 1)
                for c in range(C):
                    evac(yT[:, c, :])

            moe(0)
            for _ in range(2):
                tile_split()
            rows(1, 2)
            norm(yT[:], lambda: rows(1, 3))
            source_split("kv", xT, 4)
            rows(1, 4)
            source_split("q", hT, 4)
            projected(abT, ahead=True)
            tile_split()
            projected(cqT)
            rows(1, 5)
            answer(lams[0:1, 2:4], lams[0:1, 0:2], ACT.Exp)

            def spread(s):
                if s >= 2:
                    act.wait_ge(keys_used, 2 * (s - 1))
                for n in range(2):
                    evac(qbc[:, s % 2, n * 512:(n + 1) * 512].rearrange("p (f n) -> p f n", n=P), n=512)

            def rms(cols, name):
                act.wait_ge(tb_evac, at[name])
                act.activation(yT[:, :, cols], yT[:, :, cols], ACT.Sqrt).then_inc(act_out, 1)

            act.wait_ge(stored["ks"], 16)
            spread(0)
            for s in range(NB + 2):
                if s + 1 < NB:
                    spread(s + 1)
                if s < NB:
                    for j in range(2):
                        n = (j + 1) * P
                        act.wait_ge(act_in, inp.add())
                        for c in range(2):
                            act.activation(pex[:, j, c, 0:n], psc[:, j, c, 0:n], ACT.Exp, bias=pst[:, j, c:c + 1],
                                           accum_out=pst[:, j, 2 + c:3 + c]).then_inc(act_out, 1)
                if 1 <= s <= NB:
                    answer(sS[:, s - 1], sS[:, s - 1], ACT.Exp)
                if s == NB:
                    act.wait_ge(tb_evac, at["heads"])
                    act.activation(sqT[:, :, 0:TP], hT[:, :, 0:TP], ACT.Square).then_inc(sq_ready, 1)
                if s >= 2:
                    if s >= 3:
                        act.wait_ge(tb_done, at[f"rows{s - 3}"])
                    for n in range(2):
                        evac(osb[0:H, n * 512:(n + 1) * 512], rows=H, n=512)
                if s == NB + 1:
                    tile_split()
                if s == 0:
                    act.wait_ge(stored["kp"], 16)
                    rows(1, 6)
                if s < 2:
                    rows(1, 7 + s)
                if s == NB:
                    rows(1, 9)
                if s == NB:
                    rms(slice(0, TP), "rms")
            act.wait_ge(act_in, inp.add())
            act.activation(sqT[:, :, TP:T], hT[:, :, TP:T], ACT.Square).then_inc(sq_ready, 1)
            rms(slice(TP, T), "rms_sample")
            source_split("b_out", hT, 1)
            act.wait_ge(tb_done, at[f"rows{NB - 1}"])
            tile_split()
            projected(yT)
            norm(yT[:])
            rows(1, 10)
            moe(1)
            norm(yT[:])
            assert g.n == at["end"]

        @block.vector
        def _(dve):
            own, tbe, op, inp, out = Tally(dve_own), Tally(tb_evac), Tally(op_ready), Tally(act_in), Tally(act_out)
            an, gp = Tally(a_ready), Tally(pj_evac)
            sd = Tally(st_done)

            def link(ins):
                ins.then_inc(dve_own, 1)
                dve.wait_ge(dve_own, own.add())

            def last_empty():
                dve.wait_ge(tb_evac, tbe.value())

            def batch():
                dve.wait_ge(tb_done, tbe.value() + 1)
                return tb[tbe.n % 2]

            def empty(ins):
                ins.then_inc(tb_evac, 1)
                tbe.add()

            def ready(ins):
                ins.then_inc(op_ready, 1)
                dve.wait_ge(op_ready, op.add())

            def ask(ins):
                ins.then_inc(act_in, 1)
                inp.add()

            def answered(n=1):
                dve.wait_ge(act_out, out.add(n))

            def mod_rows(l, n):
                bank = batch()[:, 0:64].rearrange("p (c r) -> p c r", r=16)[:, :, 0:NR]
                plus = 1.0 if (n // 2) % 3 else 0.0
                bias = adabT[:, 48 * l + 4 * n:48 * l + 4 * n + 4].unsqueeze(2).to_broadcast([P, 4, NR])
                empty(dve.scalar_tensor_tensor(mT[:, 4 * n:4 * n + 4, :], bank, plus, bias, ALU.add, ALU.add))

            def modulate(sh, sc, dense_next):
                for c in range(0, C, 2):
                    h = hT[:, c:c + 2, TP:T]
                    dve.tensor_tensor(h, xT[:, c:c + 2, TP:T], mT[:, sc + c:sc + c + 2, 1:NR], ALU.mult).then_inc(dve_own, 1)
                    for k in range(c, c + 2):
                        dve.tensor_scalar(hT[:, k, 0:TP], xT[:, k, 0:TP], mT[:, sc + k, 0:1], mT[:, sh + k, 0:1],
                                          ALU.mult, ALU.add)
                    dve.wait_ge(dve_own, own.add())
                    i = dve.tensor_tensor(h, h, mT[:, sh + c:sh + c + 2, 1:NR], ALU.add)
                    if dense_next:
                        i.then_inc(source_ready, 1)
                    else:
                        ready(i)

            lows, high, sh = [0], Tally(tile_high), Tally(source_high)

            def tile_split():
                n, h = divmod(lows[0], 2)
                lows[0] += 1
                s, _, name = at["tiles"][n]
                dve.wait_ge(tile_high, high.add())
                dve.tensor_tensor(features(wlo, s, h), features(wring, s, h), dense[name][2][h].bitcast(F32),
                                  ALU.subtract).then_inc(tile_low, 1)

            def source_split(name, src):
                xh, xl, _ = dense[name]
                for p in range(4):
                    two = slice(2 * p, 2 * p + 2)
                    dve.wait_ge(source_high, sh.add())
                    dve.tensor_tensor(xl[:, two, :], src[:, two, :], xh[:, two, :].bitcast(F32),
                                      ALU.subtract).then_inc(source_low, 1)

            def residual(gate, groups):
                link(dve.tensor_scalar(xT[:], xT[:], ALPHA, None, ALU.mult))
                for c in range(0, C, 2):
                    dve.wait_ge(pj_evac, groups - C + 2 + c)
                    for k in range(c, c + 2):
                        dve.scalar_tensor_tensor(yT[:, k, 0:TP], yT[:, k, 0:TP], mT[:, gate + k, 0:1], xT[:, k, 0:TP],
                                                 ALU.mult, ALU.add)
                    y = yT[:, c:c + 2, TP:T]
                    link(dve.tensor_tensor(y, y, mT[:, gate + c:gate + c + 2, 1:NR], ALU.mult))
                    ready(dve.tensor_tensor(y, y, xT[:, c:c + 2, TP:T], ALU.add))

            def across(x):
                return x.unsqueeze(1).to_broadcast([P, C, T])

            def norm(src, dst, g0, b0, beside=lambda: None, dense_next=False):
                dve.wait_ge(st_done, sd.add())
                for c in range(0, C, 2):
                    two = src[:, c:c + 2, :]
                    ask(dve.scalar_tensor_tensor(two, st[0].unsqueeze(1).to_broadcast([P, 2, T]), -1.0 / D, two,
                                                 ALU.mult, ALU.add))
                sd.add()
                beside()
                answered()
                link(dve.reciprocal(rs[:], rs[:]))
                link(dve.tensor_tensor(src, src, across(rs[:]), ALU.mult))
                for c in range(C):
                    i = dve.tensor_scalar(dst[:, c, :], src[:, c, :], vT[:, g0 + c:g0 + c + 1], vT[:, b0 + c:b0 + c + 1],
                                          ALU.mult, ALU.add)
                    if dense_next and c % 2:
                        i.then_inc(source_ready, 1)
                return i

            def tokens(sample, prompt):
                for q in range(2):
                    empty(dve.tensor_copy(sample[0:NB, q * 512:(q + 1) * 512], batch()[0:NB, :]))
                for j in range(2):
                    for q in range(2):
                        empty(dve.tensor_copy(prompt[:, j, q * 512:(q + 1) * 512], batch()[:, :]))

            dve.memset(pos[:], 0.0)
            link(dve.memset(lg[:], 0.0))
            bank = batch()
            link(dve.tensor_copy(vT[:], bank[:, 0:V_N]))
            empty(dve.tensor_copy(adabT[:], bank[:, P:P + 96]))
            empty(dve.tensor_copy(cT[:], batch()[:, 0:128].rearrange("p (c r) -> p c r", r=16)[:, :, 0:NR]))
            for j in range(2):
                for q in range(2):
                    empty(dve.tensor_copy(xT[:, 4 * q:4 * q + 4, j * P:(j + 1) * P],
                                          batch()[:, :].rearrange("p (c t) -> p c t", c=4)))
            empty(dve.tensor_copy(xT[:, :, TP:T], batch()[:, 0:128].rearrange("p (c r) -> p c r", r=16)[:, :, 0:NB]))
            for n in range(4):
                mod_rows(0, n)
            for q in range(2):
                empty(dve.tensor_copy(wsT[:, 4 * q:4 * q + 4, :], batch()[:, :].rearrange("p (c t) -> p c t", c=4)))
            last_empty()
            modulate(0, 8, True)

            tile_split()
            source_split("a_in", hT)
            tile_split()
            for _ in range(6):
                tile_split()
            mod_rows(0, 4)
            ready(norm(zT, zT, V_AG, V_AB))
            mod_rows(0, 5)
            tokens(tokA[:, 2, :], tokA)
            for _ in range(2):
                tile_split()
            dve.wait_ge(small_in, 16 * 9)
            for q in range(4):
                both = sqT[:, 2 * (q % 2):2 * (q % 2) + 2, 0:TP]
                mix = both.rearrange("p g (j i) -> p g j i", j=2)
                empty(dve.tensor_tensor(mix, batch()[:, :].rearrange("p (g j i) -> p g j i", g=2, j=2),
                                        bsb[:, 2 * q:2 * q + 2, :].unsqueeze(2).to_broadcast([P, 2, 2, P]), ALU.add))
                last_empty()
                dve.tensor_tensor(uT[:, 2 * q:2 * q + 2, 0:TP], uT[:, 2 * q:2 * q + 2, 0:TP], both, ALU.mult)
            mix = rs[:, 0:64].rearrange("p (c b) -> p c b", b=NB)
            link(dve.tensor_tensor(mix, zT[:, :, TP:T], ws00[:].unsqueeze(2).to_broadcast([P, C, NB]), ALU.mult))
            link(dve.tensor_tensor(mix, mix, bsb[:, :, 0:1].to_broadcast([P, C, NB]), ALU.add))
            dve.tensor_tensor(uT[:, :, TP:T], uT[:, :, TP:T], mix, ALU.mult).then_inc(source_ready, 1)
            source_split("a_out", uT)
            mod_rows(0, 6)
            for _ in range(2):
                tile_split()
            mod_rows(0, 7)
            residual(16, at["a_out"])
            link(norm(yT[:], xT, V_LNG, V_LNB, lambda: mod_rows(0, 8)))
            mod_rows(0, 9)
            last_empty()

            def reduce(dst, src, op):
                link(dve.tensor_reduce(dst, src, AX.X, op))

            def first_max(dst, src, keys, shape):
                reduce(one[:], src, ALU.max)
                link(dve.tensor_tensor(dst, src, one[:].to_broadcast(shape), ALU.is_equal))
                link(dve.tensor_tensor(dst, dst, keys, ALU.mult))
                reduce(one[:], dst, ALU.max)
                link(dve.tensor_tensor(dst, dst, one[:].to_broadcast(shape), ALU.is_equal))

            dve.wait_ge(pool_own, 3)

            def more_dve(l):
                m = more[l]
                many = dve.value_load(starts[0:1, 3 * NE:3 * NE + 1], min_val=0, max_val=1)
                with dve.If(many):
                    done, silu, ev, x, ms = (Tally(m[n]) for n in ("done", "silu", "evac", "x", "mask"))
                    dve.memset(upT, 0.0).then_inc(m["evac"], 1)
                    dve.wait_ge(m["evac"], ev.add())
                    with turns(dve, NE, {done: 24, silu: 8, ev: 24, x: 2, ms: 18}) as e:
                        for half in range(2):
                            first = dve.value_load(starts[0:1, bass.ds(e + NE * (half + 1), 1)], min_val=0, max_val=SLOT_N)
                            dve.tensor_scalar(upT[:, 0, :], kst[:, K_IOTA:K_IOTA + P], lim[:, half, bass.ds(e, 1)], None,
                                              ALU.is_lt).then_inc(m["mask"], 1)
                            dve.wait_ge(m["mask"], ms.add())
                            dve.tensor_copy(xe, xg[:, :, bass.ds(first, P)]).then_inc(m["x"], 1)
                            x.add()
                            for rnd in range(12):
                                dve.wait_ge(m["done"], done.add())
                                if rnd < 4:
                                    dve.wait_ge(m["silu"], silu.add())
                                    i = dve.tensor_tensor(aT[:, rnd, :], aT[:, rnd, :], pj[1][:, 0:P], ALU.mult)
                                else:
                                    dve.tensor_tensor(upT[:, 1, :], pj[0][:, 0:P], upT[:, 0, :], ALU.mult).then_inc(m["mask"], 1)
                                    dve.wait_ge(m["mask"], ms.add())
                                    row = yg[:, rnd - 4:rnd - 3, bass.ds(first, P)]
                                    i = dve.tensor_tensor(row, row, upT[:, 1:2, :], ALU.add)
                                i.then_inc(m["evac"], 1)
                                dve.wait_ge(m["evac"], ev.add())
                with dve.Else():
                    dve.nop()

            def moe(l):
                modulate(24, 32, False)
                empty(dve.tensor_copy(lgT[:], batch()[0:NE, 0:T]))
                bank = batch()[:, 0:3 * NE].rearrange("p (j e) -> p j e", e=NE)
                dve.tensor_copy(lg[:, 0:2, :], bank[:, 0:2, :])
                empty(dve.tensor_copy(lg[0:NB, 2, :], bank[0:NB, 2, :]))
                last_empty()
                full = [P, 3, NE]
                reduce(one[:], lg[:], ALU.max)
                ask(dve.tensor_tensor(lg[:], lg[:], one[:].to_broadcast(full), ALU.subtract))
                answered()
                reduce(one[:], score[:], ALU.add)
                link(dve.reciprocal(one[:], one[:]))
                link(dve.tensor_tensor(score[:], score[:], one[:].to_broadcast(full), ALU.mult))
                link(dve.tensor_tensor(sel[:], score[:], rbias[:].unsqueeze(1).to_broadcast(full), ALU.add))
                s4 = sel[:].rearrange("p j (g e) -> p j g e", e=EG)
                dve.tensor_tensor(pair[0][:], s4[:, :, :, 0], s4[:, :, :, 1], ALU.max)
                dve.tensor_tensor(pair[1][:], s4[:, :, :, 0], s4[:, :, :, 1], ALU.min)
                dve.tensor_tensor(pair[2][:], s4[:, :, :, 2], s4[:, :, :, 3], ALU.max)
                link(dve.tensor_tensor(pair[3][:], s4[:, :, :, 2], s4[:, :, :, 3], ALU.min))
                link(dve.tensor_tensor(pair[1][:], pair[1][:], pair[3][:], ALU.max))
                dve.tensor_tensor(pair[3][:], pair[0][:], pair[2][:], ALU.min)
                link(dve.tensor_tensor(pair[0][:], pair[0][:], pair[2][:], ALU.max))
                link(dve.tensor_tensor(pair[1][:], pair[1][:], pair[3][:], ALU.max))
                link(dve.tensor_tensor(pair[0][:], pair[0][:], pair[1][:], ALU.add))
                first_max(pair[2][:], pair[0][:], kidx[:, 12:16].unsqueeze(1).to_broadcast([P, 3, EG]), [P, 3, EG])
                link(dve.tensor_scalar(pair[2][:], pair[2][:], -NEG, NEG, ALU.mult, ALU.add))
                link(dve.tensor_tensor(s4, s4, pair[2][:].unsqueeze(3).to_broadcast([P, 3, EG, EG]), ALU.add))
                keys = kidx[:].unsqueeze(1).to_broadcast(full)
                first_max(top[0][:], sel[:], keys, full)
                link(dve.scalar_tensor_tensor(sel[:], top[0][:], 2 * NEG, sel[:], ALU.mult, ALU.add))
                first_max(top[1][:], sel[:], keys, full)
                ready(dve.tensor_tensor(key[:], top[0][:], top[1][:], ALU.add))
                empty(dve.tensor_copy(ncol[:], batch()[0:NE, 0:1]))
                link(dve.tensor_tensor(score[:], score[:], key[:], ALU.mult))
                reduce(one[:], score[:], ALU.add)
                link(dve.reciprocal(one[:], one[:]))
                link(dve.tensor_tensor(score[:], score[:], one[:].to_broadcast(full), ALU.mult))
                bank = batch()
                dve.tensor_copy(pos[:, 0:2, :], bank[:, 0:2 * NE].rearrange("p (j e) -> p j e", e=NE))
                dve.tensor_copy(pos[0:NB, 2, :], bank[0:NB, 2 * NE:3 * NE])
                empty(dve.tensor_copy(nrow[:], bank[:, 3 * NE:5 * NE]))
                last_empty()
                for i in range(2):
                    dve.tensor_tensor(stack[:, :, i, :], top[i][:], pos[:], ALU.mult)
                    link(dve.tensor_tensor(stack[:, :, 2 + i, :], top[i][:], score[:], ALU.mult))
                reduce(sg[:, :, 0:4].unsqueeze(3), stack[:], ALU.add)
                link(dve.tensor_scalar(sg[:, :, 4:6], sg[:, :, 0:2], -float(T), None, ALU.add))
                iota = kst[:, K_IOTA:K_IOTA + T]
                for half in range(2):
                    s0 = 4 * half
                    for j in range(3):
                        i = dve.tensor_scalar(pick[:, j, half * T:(half + 1) * T], iota, sg[:, j, s0:s0 + 1], None, ALU.is_equal)
                    link(i)
                    for j in range(3):
                        at_h = pick[:, j, half * T:(half + 1) * T]
                        i = dve.scalar_tensor_tensor(at_h, iota, sg[:, j, s0 + 1:s0 + 2], at_h, ALU.is_equal, ALU.add)
                    ready(i)
                hn, un, gt, xh = Tally(hi_ready), Tally(part_used), Tally(silu_ready), Tally(xhi_ready)
                hn.n, un.n, gt.n, xh.n = 4 * NE * l, 4 * NE * l, NE * l, NE * l

                def low(q, s):
                    s += q // 2
                    dve.wait_ge(hi_ready, hn.add())
                    dve.tensor_tensor(quarter(wlo, q, s), quarter(wring, q, s), whi[q].bitcast(F32),
                                      ALU.subtract).then_inc(lo_ready, 1)

                mod_rows(l, 10)
                mod_rows(l, 11)
                link(dve.memset(xg[:, :, SLOT_N:PACK], 0.0))
                dve.tensor_copy(startf[:, 0:NE], nrow[0:1, NE:2 * NE])
                for k in range(2):
                    dve.tensor_scalar(startf[:, NE * (k + 1):NE * (k + 2)], nrow[0:1, NE:2 * NE], float(SPAN * (k + 1)),
                                      float(SLOT_N), ALU.add, ALU.min)
                    dve.tensor_scalar(lim[:, k, :], nrow[:, 0:NE], -float(SPAN * (k + 1)), None, ALU.add)
                reduce(startf[:, 3 * NE:3 * NE + 1], nrow[0:1, 0:NE], ALU.max)
                link(dve.tensor_scalar(startf[:, 3 * NE:3 * NE + 1], startf[:, 3 * NE:3 * NE + 1], float(SPAN), None, ALU.is_gt))
                dve.tensor_copy(starts[:], startf[:]).then_inc(routed, 1)
                dve.wait_ge(routed, l + 1)
                low(0, 0)
                low(1, 0)
                if l == 0:
                    mod_rows(1, 0)
                dve.wait_ge(pj_evac, at[f"moe{l}"])

                def tokens_low(e):
                    first = dve.value_load(starts[0:1, bass.ds(e, 1)], min_val=0, max_val=SLOT_N)
                    dve.wait_ge(xhi_ready, xh.add())
                    dve.tensor_tensor(xlo, xg[:, :, bass.ds(first, P)], xhi.bitcast(F32), ALU.subtract).then_inc(xe_ready, 1)

                def step(e, s, last=False):
                    if not last:
                        low(0, s)
                        low(1, s)
                    dve.wait_ge(silu_ready, gt.add())
                    dve.wait_ge(part_used, un.add(4))
                    dve.tensor_tensor(atok, atok, gu[1][:, :], ALU.mult).then_inc(a_ready, 1)
                    an.add()
                    if not last:
                        tokens_low(e + 1)
                        low(2, s)
                        low(3, s)
                    empty(dve.tensor_copy(aT, batch()[:, :].rearrange("p (f n) -> p f n", n=P)))

                tokens_low(0)
                low(2, 0)
                low(3, 0)
                step(0, 3)
                with turns(dve, 7, {hn: 8, un: 8, gt: 2, xh: 2, tbe: 2, an: 2}) as i:
                    step(i * 2 + 1, 0)
                    step(i * 2 + 2, 3)
                step(15, 0, last=True)
                gp.n = at[f"moe{l}"]
                dve.wait_ge(pj_evac, gp.add(2 * NE))
                assert gp.n == at[f"moe{l}_main"]
                more_dve(l)
                empty(dve.tensor_copy(lgT[0:6, :], batch()[0:6, 0:T]))
                for i in range(4):
                    empty(dve.tensor_copy(sgB[:, i, :], batch()[:, 0:T]))
                last_empty()
                for k in range(NK):
                    mine = kst[:, K_PART + k:K_PART + k + 1]
                    dve.scalar_tensor_tensor(put[:, k, :], sgB[:, 0, :], mine, sgB[:, 2, :], ALU.is_equal, ALU.mult)
                    link(dve.scalar_tensor_tensor(rs[:], sgB[:, 1, :], mine, sgB[:, 3, :], ALU.is_equal, ALU.mult))
                    i = dve.tensor_tensor(put[:, k, :], put[:, k, :], rs[:], ALU.add)
                    if k < NK - 1:
                        link(i)
                ready(i)
                if l == 0:
                    mod_rows(1, 1)
                residual(40, at[f"moe{l}_end"])

            moe(0)
            def beside():
                mod_rows(1, 2)
                for _ in range(2):
                    tile_split()

            norm(yT[:], xT, V_LNG + 8, V_LNB + 8, beside, True)
            source_split("kv", xT)
            mod_rows(1, 3)
            last_empty()
            modulate(0, 8, True)
            tile_split()
            source_split("q", hT)
            for _ in range(6):
                tile_split()
            mod_rows(1, 4)
            dve.wait_ge(rotary_in, 16)

            def partners(into):
                for h in range(H):
                    empty(dve.tensor_tensor(into[:, h, :], batch()[:, 0:T], sin, ALU.mult))

            partners(yT)
            tile_split()
            last_empty()
            link(dve.tensor_tensor(uT, uT, across(cos), ALU.mult))
            tile_split()
            link(dve.tensor_tensor(uT, uT, yT[:], ALU.add))
            tile_split()
            partners(sqT)
            last_empty()
            link(dve.tensor_tensor(cqT, cqT, across(cos), ALU.mult))
            i = dve.tensor_tensor(cqT, cqT, sqT[:], ALU.add)
            ready(i)
            mod_rows(1, 5)
            for q in range(2):
                empty(dve.tensor_scalar(qtok[0:NB, q * 512:(q + 1) * 512], batch()[0:NB, :], HD ** -0.5, None, ALU.mult))
            ready(dve.tensor_tensor(rs[:, 0:64].rearrange("p (h b) -> p h b", b=NB), cqT[:, :, TP:T], uT[:, :, TP:T], ALU.mult))
            for c in range(2):
                empty(dve.tensor_scalar(snew.rearrange("p b (h c) -> p c h b", c=2)[:, c],
                                        batch()[:, 0:64].rearrange("p (h b) -> p h b", b=NB), HD ** -0.5, None, ALU.mult))
            lv = lamv.rearrange("o (a b) d -> o a b d", b=2)
            link(dve.tensor_tensor(lv[:, :, 0, :], lv[:, :, 0, :], lv[:, :, 1, :], ALU.mult))
            ask(dve.tensor_reduce(lams[0:1, 0:2].unsqueeze(2), lv[:, :, 0, :], AX.X, ALU.add))
            answered()
            link(dve.tensor_tensor(lams[0:1, 4:5], lams[0:1, 3:4], lams[0:1, 2:3], ALU.subtract))
            ready(dve.tensor_scalar(lams[0:1, 4:5], lams[0:1, 4:5], -LAM_INIT, None, ALU.add))
            empty(dve.tensor_copy(nlam[:], batch()[:, 0:1]))
            link(dve.tensor_scalar(subg[:], vT[:, V_SUB:V_SUB + 1], 1.0 - LAM_INIT, None, ALU.mult))
            tokens(ksm, tokB)
            dve.wait_ge(stored["cv"], 16)
            tokens(tokA[:, 2, :], tokA)
            dve.wait_ge(stored["kp"], 16)

            dve.tensor_copy(sS[:, :, NPG, :], snew)

            def scores(s, k, q):
                slot, count = cache_slot("k", s, k)
                if q == 0:
                    if k == 0:
                        dve.wait_ge(pj_evac, at[f"spread{s}"])
                    dve.wait_ge(slot_in[slot], at["cache_loads"][slot] + 16 * count)
                keys = wring[:, slot, q * 2 * D:(q + 1) * 2 * D]
                link(dve.tensor_tensor(keys.rearrange("p (g n) -> p g n", g=2), keys.rearrange("p (g n) -> p g n", g=2),
                                       qbc[:, s % 2:s % 2 + 1, :].to_broadcast([P, 2, D]), ALU.mult))
                g0 = 4 * k + 2 * q
                i = dve.tensor_reduce(sS[:, s, g0:g0 + 2, :].rearrange("p g x -> p (g x)").unsqueeze(2),
                                      keys.rearrange("p (x d) -> p x d", d=HD), AX.X, ALU.add)
                if q == 1:
                    i.then_inc(keys_used, 1)

            def rms(cols):
                answered()
                link(dve.reciprocal(yT[:, :, cols], yT[:, :, cols]))
                return dve.scalar_tensor_tensor(hT[:, :, cols], hT[:, :, cols], subg[:, 0:1], yT[:, :, cols],
                                                ALU.mult, ALU.mult)

            for s in range(NB + 2):
                m = s - 1
                soft = 0 <= m < NB
                if soft:
                    mine = smx[:, 16 * m:16 * m + 16]
                    wide = mine.unsqueeze(1).to_broadcast([P, NPG + 1, 16])
                if s < NB:
                    scores(s, 0, 0)
                for c in range(2):
                    if s < NB:
                        bank = batch()
                        for j in range(2):
                            n = (j + 1) * P
                            i = dve.scalar_tensor_tensor(psc[:, j, c, 0:n], bank[:, P * j:P * j + n], HD ** -0.5,
                                                         kst[:, K_MASK + (1 - j) * P:K_MASK + 2 * P], ALU.mult, ALU.add)
                        empty(i)
                    if c == 0 and soft:
                        empty(dve.tensor_reduce(scol[0:16, :], batch()[0:16, 0:P], AX.X, ALU.max))
                    if s < NB:
                        last_empty()
                        for j in range(2):
                            n = (j + 1) * P
                            i = dve.tensor_reduce(pst[:, j, c:c + 1], psc[:, j, c, 0:n], AX.X, ALU.max, negate=True)
                            if c:
                                ask(i)
                if s < NB:
                    scores(s, 0, 1)
                if soft:
                    empty(dve.tensor_copy(mine, batch()[:, 0:16]))
                    last_empty()
                    ask(dve.tensor_tensor(sS[:, m], sS[:, m], wide, ALU.subtract))
                if s < NB:
                    for j in range(2):
                        n = (j + 1) * P
                        answered(2)
                        link(dve.reciprocal(pst[:, j, 4:6], pst[:, j, 2:4]))
                        dve.tensor_scalar(psc[:, j, 0, 0:n], pex[:, j, 0, 0:n], pst[:, j, 4:5], None, ALU.mult)
                        link(dve.tensor_scalar(pst[:, j, 5:6], pst[:, j, 5:6], nlam[:, 0:1], None, ALU.mult))
                        ready(dve.scalar_tensor_tensor(pex[:, j, 0, 0:n], pex[:, j, 1, 0:n], pst[:, j, 5:6],
                                                       psc[:, j, 0, 0:n], ALU.mult, ALU.add))
                    scores(s, 1, 0)
                if soft:
                    answered()
                if s < NB:
                    for j in range(2):
                        empty(dve.tensor_copy(pwT[:, j, 0:j + 1, :],
                                              batch()[:, 0:(j + 1) * P].rearrange("p (t q) -> p t q", q=P)))
                if s == NB:
                    for h in range(H):
                        empty(dve.tensor_scalar(yT[:, h, 0:TP], batch()[:, 0:TP], 1.0 / P, EPS, ALU.mult, ALU.add))
                if soft:
                    ready(dve.tensor_reduce(mine.unsqueeze(2), sS[:, m, 0:NPG, :].rearrange("p g x -> p x g"), AX.X, ALU.add))
                if s < NB:
                    scores(s, 1, 1)
                if soft:
                    empty(dve.tensor_tensor(mine, batch()[:, 0:16], sS[:, m, NPG, :], ALU.add))
                    last_empty()
                    link(dve.reciprocal(mine, mine))
                    odd = mine.rearrange("p (x c) -> p x c", c=2)[:, :, 1:2]
                    link(dve.tensor_scalar(odd, odd, nlam[:, 0:1], None, ALU.mult))
                    link(dve.tensor_tensor(sS[:, m], sS[:, m], wide, ALU.mult))
                    e4 = sS[:, m].rearrange("p g (h c) -> p g h c", c=2)
                    dve.tensor_tensor(sW[:, m], e4[:, 0:NPG, :, 0], e4[:, 0:NPG, :, 1], ALU.add)
                    ready(dve.tensor_tensor(wnew[:, m, :], e4[:, NPG, :, 0], e4[:, NPG, :, 1], ALU.add))
                if s == NB + 1:
                    tile_split()
                if s < NB:
                    for j in range(2):
                        i = dve.tensor_copy(hT[:, s, j * P:(j + 1) * P], batch()[:, 0:P])
                        empty(i)
                if s >= 2:
                    empty(dve.tensor_copy(hT[:, :, TP + s - 2:TP + s - 1],
                                          batch()[:, 0:(H + 1) * (H - 1) + 1:H + 1].unsqueeze(2)))
                if s < 3:
                    mod_rows(1, 6 + s)
                if s < NB:
                    ready(dve.tensor_reduce(smx[:, 16 * s:16 * s + 16].unsqueeze(2),
                                            sS[:, s].rearrange("p g x -> p x g"), AX.X, ALU.max))
                if s == NB:
                    rms(slice(0, TP))
            mod_rows(1, 9)
            mix = rs[:, 0:64].rearrange("p (h b) -> p h b", b=NB)
            link(dve.tensor_tensor(mix, zT[:, :, TP:T], wnew.rearrange("p b h -> p h b"), ALU.mult))
            ask(dve.tensor_tensor(hT[:, :, TP:T], hT[:, :, TP:T], mix, ALU.add))
            empty(dve.tensor_scalar(yT[:, :, TP:T], batch()[:, 0:H * NB].rearrange("p (h b) -> p h b", b=NB),
                                    1.0 / P, EPS, ALU.mult, ALU.add))
            rms(slice(TP, T)).then_inc(source_ready, 1)
            source_split("b_out", hT)
            for _ in range(3):
                tile_split()
            residual(16, at["b_out"])
            link(norm(yT[:], xT, V_LNG + 16, V_LNB + 16))
            last_empty()
            moe(1)
            ready(norm(yT[:], xT, V_LNG + 24, V_LNB + 24))
            dve.wait_ge(stored["vp"], 16)
            dve.wait_ge(stored["vs"], 16)
            tokens(tokA[:, 2, :], tokA)


_OUTS = [("y_prompt", (1, TP, D)), ("y_sample", (NB, 1, D)), ("k_prompt", (1, TP, H, 2, HD)),
         ("v_prompt", (1, TP, H, P)), ("k_sample", (NB, 1, H, 2, HD)), ("v_sample", (NB, 1, H, P)),
         ("chunk_v_sample", (1, NB, 1, D))]


def kernel(**inputs):
    import concourse.bacc as bacc
    from concourse.bass_utils import run_bass_kernel_spmd

    nc = bacc.Bacc("TRN2", target_bir_lowering=False, num_devices=1)
    arrays = {f"in_{n}": np.ascontiguousarray(v) for n, v in inputs.items()}
    arrays["in_consts"] = constants()
    arrays["in_rotary"] = rotary()
    ins = {n[3:]: nc.dram_tensor(n, v.shape, mybir.dt.from_np(v.dtype), kind="ExternalInput").ap()
           for n, v in arrays.items()}
    outs = {n: nc.dram_tensor(f"out_{n}", s, F32, kind="ExternalOutput").ap() for n, s in _OUTS}
    build(nc, ins, outs)
    r = run_bass_kernel_spmd(nc, [arrays], core_ids=[0])
    return tuple(r.results[0][f"out_{n}"] for n, _ in _OUTS)
```
